# Optimizing a Trainium2 kernel written in Bass

```python
import math
import jax, jax.numpy as jnp
from jax import lax
import numpy as np

D_MODEL = 1024
BATCH = 1
SEQ = 256
DEPTH = 2

HEAD_DIM = 64
GDN_HEADS = 6
RET_HEADS = 4
MLSTM_HEADS = 6
GDN_WIDTH = GDN_HEADS * HEAD_DIM
RET_WIDTH = RET_HEADS * HEAD_DIM
MLSTM_WIDTH = MLSTM_HEADS * HEAD_DIM
D_MIX = GDN_WIDTH + RET_WIDTH + MLSTM_WIDTH
CONV_WIDTH = 4
CHUNK = 64
ROPE_BASE = 10000.0
N_GROUPS = 4
EXPERTS_PER_GROUP = 8
N_EXPERTS = N_GROUPS * EXPERTS_PER_GROUP
TOP_K = 2
D_EXPERT = D_MODEL // 4
EPS = 1e-6
IN_SPLITS = (3 * GDN_WIDTH, GDN_WIDTH, GDN_HEADS, GDN_HEADS,
             RET_WIDTH, RET_WIDTH, RET_WIDTH, RET_WIDTH,
             2 * MLSTM_WIDTH, MLSTM_WIDTH, MLSTM_WIDTH, MLSTM_HEADS, MLSTM_HEADS)
D_IN_PROJ = sum(IN_SPLITS)

kernel_name = 'hymba_style_gdn_retention_mlstm_hmoe'

def rms_norm(x, gain):
    xf = x.astype(jnp.float32)
    y = xf * lax.rsqrt(jnp.mean(xf * xf, axis=-1, keepdims=True) + EPS)
    return (y * gain.astype(jnp.float32)).astype(x.dtype)

def head_rms(x):
    return x * lax.rsqrt(jnp.mean(x * x, axis=-1, keepdims=True) + EPS)

def l2norm(x):
    return x * lax.rsqrt(jnp.sum(x * x, axis=-1, keepdims=True) + EPS)

def to_heads(x, n_heads):
    b, t, _ = x.shape
    return x.reshape(b, t, n_heads, -1).transpose(0, 2, 1, 3)

def from_heads(x):
    b, h, t, d = x.shape
    return x.transpose(0, 2, 1, 3).reshape(b, t, h * d)

def to_chunks(x):
    b, h, t = x.shape[:3]
    return x.reshape(b, h, t // CHUNK, CHUNK, *x.shape[3:])

def causal_conv(x, w):
    k, c = w.shape
    return lax.conv_general_dilated(x, w.astype(x.dtype)[:, None, :], window_strides=(1,),
                                    padding=[(k - 1, 0)], dimension_numbers=('NWC', 'WIO', 'NWC'),
                                    feature_group_count=c)

def rotary(x):
    t, d = x.shape[2], x.shape[3]
    inv_freq = ROPE_BASE ** (-jnp.arange(0, d, 2, dtype=jnp.float32) / d)
    ang = jnp.arange(t, dtype=jnp.float32)[:, None] * inv_freq[None, :]
    cos, sin = jnp.cos(ang), jnp.sin(ang)
    x1, x2 = x[..., : d // 2], x[..., d // 2:]
    return jnp.concatenate([x1 * cos - x2 * sin, x1 * sin + x2 * cos], axis=-1)

def chunk_gated_delta(q, k, v, g, beta):
    b, h, t, dk = q.shape
    dv = v.shape[-1]
    qc = to_chunks(q * dk ** -0.5)
    kc = to_chunks(k)
    kb = to_chunks(k * beta[..., None])
    vb = to_chunks(v * beta[..., None])
    gc = jnp.cumsum(to_chunks(g), axis=-1)
    tril = jnp.tril(jnp.ones((CHUNK, CHUNK), bool))
    strict = jnp.tril(jnp.ones((CHUNK, CHUNK), bool), -1)
    decay = jnp.exp(jnp.where(tril, gc[..., :, None] - gc[..., None, :], -jnp.inf))
    a_mat = jnp.where(strict, jnp.einsum('bhncd,bhnsd->bhncs', kb, kc) * decay, 0.0)
    rhs = jnp.concatenate([vb, kb * jnp.exp(gc)[..., None]], axis=-1)
    sol = lax.linalg.triangular_solve(a_mat, rhs, left_side=True, lower=True, unit_diagonal=True)
    u, w = sol[..., :dv], sol[..., dv:]
    qk = jnp.einsum('bhncd,bhnsd->bhncs', qc, kc) * decay

    def step(state, xs):
        q_c, k_c, u_c, w_c, g_c, qk_c = xs
        v_new = u_c - jnp.einsum('bhcd,bhde->bhce', w_c, state)
        o = (jnp.einsum('bhcd,bhde->bhce', q_c * jnp.exp(g_c)[..., None], state)
             + jnp.einsum('bhcs,bhse->bhce', qk_c, v_new))
        g_last = g_c[..., -1]
        state = (state * jnp.exp(g_last)[..., None, None]
                 + jnp.einsum('bhcd,bhce->bhde', k_c * jnp.exp(g_last[..., None] - g_c)[..., None], v_new))
        return state, o

    xs = tuple(jnp.moveaxis(a_, 2, 0) for a_ in (qc, kc, u, w, gc, qk))
    _, o = lax.scan(step, jnp.zeros((b, h, dk, dv), q.dtype), xs)
    return jnp.moveaxis(o, 0, 2).reshape(b, h, t, dv)

def chunk_retention(q, k, v):
    b, h, t, dk = q.shape
    dv = v.shape[-1]
    log_gamma = jnp.log(1.0 - 2.0 ** (-5.0 - jnp.arange(h, dtype=jnp.float32)))
    qc, kc, vc = to_chunks(q), to_chunks(k), to_chunks(v)
    pos = jnp.arange(CHUNK, dtype=jnp.float32)
    tril = jnp.tril(jnp.ones((CHUNK, CHUNK), jnp.float32))
    decay = jnp.exp((pos[:, None] - pos[None, :]) * log_gamma[:, None, None]) * tril
    scores = jnp.einsum('bhncd,bhnsd->bhncs', qc, kc) * decay[None, :, None]
    o_intra = jnp.einsum('bhncs,bhnse->bhnce', scores, vc)
    k_scale = jnp.exp(log_gamma[:, None] * (CHUNK - 1 - pos))
    q_scale = jnp.exp(log_gamma[:, None] * (pos + 1))
    chunk_decay = jnp.exp(log_gamma * CHUNK)
    kv = jnp.einsum('bhncd,bhnce->bhnde', kc * k_scale[None, :, None, :, None], vc)

    def step(state, kv_c):
        return chunk_decay[None, :, None, None] * state + kv_c, state

    _, prev = lax.scan(step, jnp.zeros((b, h, dk, dv), q.dtype), jnp.moveaxis(kv, 2, 0))
    prev = jnp.moveaxis(prev, 0, 2)
    o_inter = jnp.einsum('bhncd,bhnde->bhnce', qc * q_scale[None, :, None, :, None], prev)
    return (o_intra + o_inter).reshape(b, h, t, dv)

def chunk_mlstm(q, k, v, log_i, log_f):
    b, h, t, dk = q.shape
    dv = v.shape[-1]
    qc, kc, vc = to_chunks(q), to_chunks(k), to_chunks(v)
    bc = jnp.cumsum(to_chunks(log_f), axis=-1)
    ic = to_chunks(log_i)
    qk = jnp.einsum('bhncd,bhnsd->bhncs', qc, kc)
    tril = jnp.tril(jnp.ones((CHUNK, CHUNK), bool))

    def step(carry, xs):
        c_st, n_st, m_st = carry
        q_c, k_c, v_c, b_c, i_c, qk_c = xs
        log_d = jnp.where(tril, b_c[..., :, None] - b_c[..., None, :] + i_c[..., None, :], -jnp.inf)
        m_t = jnp.maximum(b_c + m_st[..., None], jnp.max(log_d, axis=-1))
        inter = jnp.exp(b_c + m_st[..., None] - m_t)
        wmat = jnp.exp(log_d - m_t[..., None]) * qk_c
        num = (inter[..., None] * jnp.einsum('bhcd,bhde->bhce', q_c, c_st)
               + jnp.einsum('bhcs,bhse->bhce', wmat, v_c))
        den = inter * jnp.einsum('bhcd,bhd->bhc', q_c, n_st) + jnp.sum(wmat, axis=-1)
        h_c = num / jnp.maximum(jnp.abs(den), jnp.exp(-m_t))[..., None]
        b_last = b_c[..., -1]
        a_c = b_last[..., None] - b_c + i_c
        m_new = jnp.maximum(b_last + m_st, jnp.max(a_c, axis=-1))
        dec = jnp.exp(b_last + m_st - m_new)
        wk = jnp.exp(a_c - m_new[..., None])
        c_st = dec[..., None, None] * c_st + jnp.einsum('bhcd,bhce->bhde', k_c * wk[..., None], v_c)
        n_st = dec[..., None] * n_st + jnp.einsum('bhc,bhcd->bhd', wk, k_c)
        return (c_st, n_st, m_new), h_c

    init = (jnp.zeros((b, h, dk, dv), q.dtype), jnp.zeros((b, h, dk), q.dtype), jnp.zeros((b, h), q.dtype))
    xs = tuple(jnp.moveaxis(a_, 2, 0) for a_ in (qc, kc, vc, bc, ic, qk))
    _, o = lax.scan(step, init, xs)
    return jnp.moveaxis(o, 0, 2).reshape(b, h, t, dv)

def gdn_mixer(qkv, z, b_logit, a_logit, conv_w, a_log, dt_bias, norm_gain):
    qkv = jax.nn.silu(causal_conv(qkv, conv_w))
    q, k, v = jnp.split(qkv, 3, axis=-1)
    q = l2norm(to_heads(q, GDN_HEADS))
    k = l2norm(to_heads(k, GDN_HEADS))
    v = to_heads(v, GDN_HEADS)
    beta = jax.nn.sigmoid(b_logit).transpose(0, 2, 1)
    g = (-jnp.exp(a_log) * jax.nn.softplus(a_logit + dt_bias)).transpose(0, 2, 1)
    o = chunk_gated_delta(q, k, v, g, beta)
    return from_heads(head_rms(o)) * norm_gain * jax.nn.silu(z)

def retention_mixer(q, k, v, gate, norm_gain):
    q = rotary(to_heads(q, RET_HEADS))
    k = rotary(to_heads(k, RET_HEADS)) * HEAD_DIM ** -0.5
    v = to_heads(v, RET_HEADS)
    o = chunk_retention(q, k, v)
    return from_heads(head_rms(o)) * norm_gain * jax.nn.silu(gate)

def mlstm_mixer(qk, v, o_logit, i_logit, f_logit, conv_w, i_bias, f_bias, norm_gain):
    qk = jax.nn.silu(causal_conv(qk, conv_w))
    q, k = jnp.split(qk, 2, axis=-1)
    q = to_heads(q, MLSTM_HEADS) * HEAD_DIM ** -0.5
    k = to_heads(k, MLSTM_HEADS)
    v = to_heads(v, MLSTM_HEADS)
    log_i = (i_logit + i_bias).transpose(0, 2, 1)
    log_f = jax.nn.log_sigmoid(f_logit + f_bias).transpose(0, 2, 1)
    h = chunk_mlstm(q, k, v, log_i, log_f)
    return jax.nn.sigmoid(o_logit) * (from_heads(head_rms(h)) * norm_gain)

def hierarchical_moe(h, router_group, router_expert, router_bias, expert_gate, expert_up, expert_down):
    b, t, d = h.shape
    tok = h.reshape(b * t, d)
    group_prob = jax.nn.softmax((tok @ router_group).astype(jnp.float32), axis=-1)
    group_p, group_idx = lax.top_k(group_prob, 1)
    expert_logits = (tok @ router_expert).astype(jnp.float32) + router_bias.astype(jnp.float32)
    expert_logits = expert_logits.reshape(-1, N_GROUPS, EXPERTS_PER_GROUP)
    in_group = jnp.take_along_axis(expert_logits, group_idx[:, :, None], axis=1)[:, 0]
    top_logit, top_idx = lax.top_k(in_group, TOP_K)
    weights = jax.nn.softmax(top_logit, axis=-1) * group_p
    expert_id = group_idx * EXPERTS_PER_GROUP + top_idx
    combine = jnp.einsum('nk,nke->ne', weights, jax.nn.one_hot(expert_id, N_EXPERTS, dtype=jnp.float32))
    out = jnp.zeros((b * t, d), jnp.float32)
    for e in range(N_EXPERTS):
        y = (jax.nn.silu(tok @ expert_gate[e]) * (tok @ expert_up[e])) @ expert_down[e]
        out = out + combine[:, e:e + 1] * y.astype(jnp.float32)
    return out.astype(h.dtype).reshape(b, t, d)

def hybrid_layer(x, norm_mix, w_in, gdn_conv, gdn_a_log, gdn_dt_bias, gdn_norm, ret_norm,
                 mlstm_conv, mlstm_i_bias, mlstm_f_bias, mlstm_norm, w_out, norm_ffn,
                 router_group, router_expert, router_bias, expert_gate, expert_up, expert_down):
    h = rms_norm(x, norm_mix)
    proj = jnp.einsum('btd,dp->btp', h, w_in).astype(jnp.float32)
    (g_qkv, g_z, g_b, g_a, r_q, r_k, r_v, r_g,
     m_qk, m_v, m_o, m_i, m_f) = jnp.split(proj, np.cumsum(IN_SPLITS)[:-1].tolist(), axis=-1)
    y_gdn = gdn_mixer(g_qkv, g_z, g_b, g_a, gdn_conv, gdn_a_log, gdn_dt_bias, gdn_norm)
    y_ret = retention_mixer(r_q, r_k, r_v, r_g, ret_norm)
    y_mlstm = mlstm_mixer(m_qk, m_v, m_o, m_i, m_f, mlstm_conv, mlstm_i_bias, mlstm_f_bias, mlstm_norm)
    mix = jnp.concatenate([y_gdn, y_ret, y_mlstm], axis=-1).astype(x.dtype)
    x = x + jnp.einsum('btm,md->btd', mix, w_out)
    x = x + hierarchical_moe(rms_norm(x, norm_ffn), router_group, router_expert, router_bias,
                             expert_gate, expert_up, expert_down)
    return x

def setup_inputs(seed: int = 0) -> dict:
    key = jax.random.key(seed)
    ks = jax.random.split(key, 24)
    f32 = jnp.float32
    L = DEPTH

    def normal(k, shape, scale):
        return scale * jax.random.normal(k, shape, f32)

    def gain(k, shape):
        return 1.0 + 0.02 * jax.random.normal(k, shape, f32)

    a_init = jax.random.uniform(ks[4], (L, GDN_HEADS), f32, 1.0, 16.0)
    dt = jnp.exp(jax.random.uniform(ks[5], (L, GDN_HEADS), f32, math.log(1e-3), math.log(1e-1)))
    dt_bias = dt + jnp.log(-jnp.expm1(-dt))
    f_bias = jnp.linspace(3.0, 6.0, MLSTM_HEADS, dtype=f32)[None, :] + normal(ks[10], (L, MLSTM_HEADS), 0.1)
    return {
        'x': normal(ks[0], (BATCH, SEQ, D_MODEL), 1.0),
        'norm_mix': gain(ks[1], (L, D_MODEL)),
        'w_in': normal(ks[2], (L, D_MODEL, D_IN_PROJ), D_MODEL ** -0.5),
        'gdn_conv': normal(ks[3], (L, CONV_WIDTH, 3 * GDN_WIDTH), CONV_WIDTH ** -0.5),
        'gdn_a_log': jnp.log(a_init),
        'gdn_dt_bias': dt_bias,
        'gdn_norm': gain(ks[6], (L, GDN_WIDTH)),
        'ret_norm': gain(ks[7], (L, RET_WIDTH)),
        'mlstm_conv': normal(ks[8], (L, CONV_WIDTH, 2 * MLSTM_WIDTH), CONV_WIDTH ** -0.5),
        'mlstm_i_bias': normal(ks[9], (L, MLSTM_HEADS), 0.1),
        'mlstm_f_bias': f_bias,
        'mlstm_norm': gain(ks[11], (L, MLSTM_WIDTH)),
        'w_out': normal(ks[12], (L, D_MIX, D_MODEL), D_MIX ** -0.5),
        'norm_ffn': gain(ks[13], (L, D_MODEL)),
        'router_group': normal(ks[14], (L, D_MODEL, N_GROUPS), D_MODEL ** -0.5),
        'router_expert': normal(ks[15], (L, D_MODEL, N_EXPERTS), D_MODEL ** -0.5),
        'router_bias': normal(ks[16], (L, N_EXPERTS), 0.01),
        'expert_gate': normal(ks[17], (L, N_EXPERTS, D_MODEL, D_EXPERT), D_MODEL ** -0.5),
        'expert_up': normal(ks[18], (L, N_EXPERTS, D_MODEL, D_EXPERT), D_MODEL ** -0.5),
        'expert_down': normal(ks[19], (L, N_EXPERTS, D_EXPERT, D_MODEL), D_EXPERT ** -0.5),
        'norm_final': gain(ks[20], (D_MODEL,)),
    }

def reference(x, norm_mix, w_in, gdn_conv, gdn_a_log, gdn_dt_bias, gdn_norm, ret_norm,
              mlstm_conv, mlstm_i_bias, mlstm_f_bias, mlstm_norm, w_out, norm_ffn,
              router_group, router_expert, router_bias, expert_gate, expert_up, expert_down, norm_final):
    for l in range(DEPTH):
        x = hybrid_layer(x, norm_mix[l], w_in[l], gdn_conv[l], gdn_a_log[l], gdn_dt_bias[l], gdn_norm[l],
                         ret_norm[l], mlstm_conv[l], mlstm_i_bias[l], mlstm_f_bias[l], mlstm_norm[l],
                         w_out[l], norm_ffn[l], router_group[l], router_expert[l], router_bias[l],
                         expert_gate[l], expert_up[l], expert_down[l])
    return rms_norm(x, norm_final)


_drawn_inputs = setup_inputs


def setup_inputs(seed=0):
    import zlib

    import numpy as np

    out = dict(_drawn_inputs(seed))
    spreads = {}
    factors = {'ret_norm': 4.353,
     'mlstm_i_bias': 64.0,
     'norm_final': 25.769,
     'gdn_norm': 8.326,
     'mlstm_norm': 3.984,
     'router_bias': 3.616,
     'norm_ffn': 2.793}
    for name, (base, spread) in spreads.items():
        noise = np.random.default_rng([zlib.crc32(name.encode()), seed]).standard_normal(out[name].shape)
        drawn = base * np.exp(spread * noise) if base else spread * noise
        out[name] = __import__('jax').numpy.asarray(drawn.astype(out[name].dtype))
    for name, factor in factors.items():
        out[name] = (out[name] * factor).astype(out[name].dtype)
    return out
```

```python
from contextlib import ExitStack
import math

import concourse.bass as bass
from concourse import mybir

F32 = mybir.dt.float32
BF16 = mybir.dt.bfloat16
U32 = mybir.dt.uint32
I32 = mybir.dt.int32
ALU = mybir.AluOpType
ACT = mybir.ActivationFunctionType
AX_X = mybir.AxisListType.X

P = 128
LAYERS = 2
D = 1024
T = 256
TT = T // P
KD = D // P
HD = 64
GH, RH, MH = 6, 4, 6
GP, RP, MP = GH // 2, RH // 2, MH // 2
MIX = GP + RP + MP
CONV = 4
GROUPS, PER_GROUP = 4, 8
EXPERTS = GROUPS * PER_GROUP
DE = D // 4
EPS = 1e-6
RING = 12
SLOT = 2048
COLS = SLOT // KD
QUADS = EXPERTS // 4
CAP = P // 4
MAXROUND = T // CAP
COUNT = T + CAP
NEG = -1e30
QK_SCALE = HD ** -0.5

GW, RW, MW = GH * HD, RH * HD, MH * HD
C_Z = 3 * GW
C_B = C_Z + GW
C_RQ = C_B + 2 * GH
C_RV = C_RQ + 2 * RW
C_RG = C_RV + RW
C_MQ = C_RG + RW
C_MV = C_MQ + 2 * MW
C_MO = C_MV + MW
C_I = C_MO + MW
D_IN = C_I + 2 * MH
NG = 2 * GH + 2 * MH
PROJ = [("gates", [(C_B, 2 * GH), (C_I, 2 * MH)])]
PROJ += [(("gdn", s), [(COLS * s, min(COLS, 3 * GW - COLS * s))]) for s in range(5)]
PROJ += [(("rqk", 0), [(C_RQ, COLS)]), (("rqk", 1), [(C_RQ + RW, COLS)])]
PROJ += [(("rv", 0), [(C_RV, RW)])]
PROJ += [(("mqk", s), [(C_MQ + COLS * s, COLS)]) for s in range(3)]
PROJ += [(("mv", s), [(C_MV + P * s, P)]) for s in range(3)]
PROJ += [(("gate", 0), [(C_Z, COLS)]), (("gate", 1), [(C_Z + COLS, P)]), (("gate", 2), [(C_RG, RW)]),
         (("gate", 3), [(C_MO, COLS)]), (("gate", 4), [(C_MO + COLS, P)])]
GATE_TILES = [(0, 1), (2,), (3, 4), (5, 6), (7,)]
SLOT_OF = {name: i for i, (name, _) in enumerate(PROJ)}
WIDTH = {name: sum(n for _, n in cols) for name, cols in PROJ}
NPROJ = len(PROJ)
NMIX = NPROJ + D // COLS
assert NMIX % RING == 0 and D_IN == 4120

CONST = ["ident", "cum", "ncum", "nsuffix", "before", "ones", "nones", "headsum", "swap"]
LEVELS = [2 ** i for i in range(7)]

PAR = {}
_at = 0
for _name, _n in [("gain_mix", KD), ("gain_ffn", KD), ("conv_g", 9 * CONV), ("conv_m", 6 * CONV),
                  ("head_gain", MIX), ("a_log", GH), ("bias3", 2 * GH + 2 * MH), ("router_bias", 36)]:
    PAR[_name] = (_at, _at + _n)
    _at += _n
NPAR = _at


def psum_plan():
    order = [("hT", i) for i in range(4)] + ["gates"] + [("gdn", s) for s in range(5)]
    order += ["rows", "cols", ("beta", 0), ("beta", 1)] + [("nrm", s) for s in range(3)]
    order += [("vt", p) for p in range(GP)] + [("dec", 0)]
    for h in range(GH):
        if h % 2 == 0 and h // 2 + 1 < GP:
            order += [("dec", h // 2 + 1)]
        order += [("kq0", h), ("kq1", h)]
    order += [("A", g) for g in range(3)] + [("X", 0, g) for g in range(3)]
    for lev in range(1, 7):
        order += [("W", lev, g) for g in range(3)] + [("Z", lev, g) for g in range(3)]
        if lev < 6:
            order += [("X", lev, g) for g in range(3)]
    order += ["u1", "t1", "u2"] + [("o", p) for p in range(GP)] + [("on", p) for p in range(GP)]
    order += [("rqk", 0), ("rqk", 1), ("rsw", 0), ("rsw", 1), ("rv", 0)]
    order += [("mqk", s) for s in range(3)] + [("mv", s) for s in range(3)] + [("gate", s) for s in range(5)]
    order += [("rs", h) for h in range(RH)] + [("o", 3), ("o", 4), ("on", 3), ("on", 4)]
    for p in range(MP):
        order += [("mdec", p), ("ms", 2 * p), ("ms", 2 * p + 1), ("em", p), ("o", 5 + p), ("on", 5 + p)]
    order += [("wo", n) for n in range(D // COLS)]
    order += [("h2T", i) for i in range(4)] + ["logits", "rank"]
    return order


def trunk(nc, x_in, consts, level_masks, params, w_mix, router_w, e_gate, e_up, e_down, gain_final, out):
    order = psum_plan()
    bank_of = {name: (i % 8, i // 8) for i, name in enumerate(order)}
    uses = [sum(1 for i in range(len(order)) if i % 8 == b) for b in range(8)]

    with ExitStack() as ctx:
        def sb(name, shape, dt=F32):
            return ctx.enter_context(nc.sbuf_tensor(name, shape, dt))

        def sem(name):
            return ctx.enter_context(nc.semaphore(name))

        ring = sb("ring", [P, RING, SLOT])
        x = sb("x", [P, TT, D])
        xn = sb("xn", [P, TT * D])
        hT = sb("hT", [P, KD * T])
        kqz = sb("kqz", [P, GH, 2, T])
        kf = sb("kf", [P, GP, T])
        raw = sb("raw", [P, 9 * T])
        vb = sb("vb", [P, TT, GW])
        kq = sb("kq", [P, GH * 2 * 384])
        xxt = sb("xxt", [P, 12 * T])
        cst = sb("cst", [P, len(CONST), P])
        lvl = sb("lvl", [P, len(LEVELS), P], BF16)
        maskc = sb("maskc", [P, T])
        dist = sb("dist", [P, 384])
        rot = sb("rot", [P, 2, T])
        selin = sb("selin", [P, 3, TT, P])
        rows = sb("rows", [P, T])
        rowsraw = sb("rowsraw", [P, T])
        ebuf = sb("ebuf", [P, 2, 384])
        par = sb("par", [P, NPAR])
        rw = sb("rw", [P, KD, 36])
        epsc = sb("epsc", [P, 1])
        ss = sb("ss", [P, 8])
        gz = sb("gz", [P, TT, 24])
        sp = sb("sp", [P, 4, TT, 18])
        ea = sb("ea", [P, GH])
        dpos = sb("dpos", [P, TT, 12])
        beta = sb("beta", [P, TT, GH])
        colv = sb("colv", [P, 32])
        colA = sb("colA", [P, TT, MH])
        iota = sb("iota", [P, COUNT + 8])
        lg = sb("lg", [P, TT, 36])
        rt = sb("rt", [P, TT, 64])
        rtx = sb("rtx", [P, 2, TT, 8], U32)
        pick = sb("pick", [P, 4, TT, EXPERTS])
        sel = sb("sel", [P, 2, TT, EXPERTS + 4])
        nround_f = sb("nround_f", [P, 32 + 2 * QUADS])
        nround = sb("nround", [P, QUADS], I32)

        def c(name):
            return cst[:, CONST.index(name), :]

        def pv(name, i=0, n=1):
            a, _ = PAR[name]
            return par[:, a + i:a + i + n]

        xn3 = xn[:, :].rearrange("p (t d) -> p t d", t=TT)
        hT3 = hT[:, :].rearrange("p (k t) -> p k t", k=KD)
        mixT = xn[:, :].rearrange("p (c t) -> p c t", c=MIX)
        raw3 = raw[:, :].rearrange("p (c t) -> p c t", c=9)
        Amat = raw[:, 0:12 * P].rearrange("p (m t) -> p m t", m=12)
        XT = xxt[:, 0:12 * P].rearrange("p (m t) -> p m t", m=12)
        X = xxt[:, 12 * P:24 * P].rearrange("p (m t) -> p m t", m=12)
        sqn = xxt[:, 0:6 * T].rearrange("p (c t) -> p c t", c=6)
        rn = xxt[:, 6 * T:12 * T].rearrange("p (c t) -> p c t", c=6)
        gateT = xxt[:, 0:MIX * T].rearrange("p (c t) -> p c t", c=MIX)
        KQ = kq[:, :].rearrange("p (h a t) -> p h a t", h=GH, a=2)
        betab = kq[:, 5 * 768:6 * 768].rearrange("p (c t) -> p c t", c=3)
        HAL = T + 4
        cin_g = xn[:, 0:3 * HAL].rearrange("p (b t) -> p b t", b=3)
        acc_g = xn[:, 3 * HAL:3 * HAL + 4 * T].rearrange("p (b t) -> p b t", b=4)
        cin_m = raw[:, 0:3 * HAL].rearrange("p (b t) -> p b t", b=3)
        acc_m = raw[:, 3 * HAL:3 * HAL + 4 * T].rearrange("p (b t) -> p b t", b=4)
        vm = kq[:, 0:768].rearrange("p (t c) -> p t c", t=TT)
        vr = kq[:, 768:1280].rearrange("p (t c) -> p t c", t=TT)
        rkf = kq[:, 1280:1792].rearrange("p (c t) -> p c t", c=RP)
        prob = kq[:, 1792:2560].rearrange("p (b t) -> p b t", b=2)
        rraw = kq[:, 2560:3584].rearrange("p (a c t) -> p a c t", a=2, c=2)
        rtmp = kq[:, 3584:4096].rearrange("p (c t) -> p c t", c=2)
        mtmp = kq[:, 2560:3584].rearrange("p (b t) -> p b t", b=4)
        sqo = hT3[:, 0:5, :]
        rro = hT3[:, 5:8, :]
        hq = hT[:, 0:1024].rearrange("p (k s) -> p k s", k=KD)
        ysb = hT[:, 1024:2048].rearrange("p (n s) -> p n s", n=2)
        Psel = kq[:, 0:128].bitcast(BF16).rearrange("p (t s) -> p t s", t=TT)
        Pwt = kq[:, 128:384].rearrange("p (t s) -> p t s", t=TT)
        PwT = kq[:, 384:640]
        sg = kq[:, 640:896]
        hmid = kq[:, 896:1152]
        hmT = kq[:, 1152:1408].rearrange("p (f s) -> p f s", f=2)
        part = [kq[:, 1408 + 1024 * i:1408 + 1024 * (i + 1)].bitcast(BF16).rearrange("p (t d) -> p t d", t=TT) for i in range(3)]
        rest = xxt[:, 0:TT * D].rearrange("p (t d) -> p t d", t=TT)
        gfin = kq[:, 0:D]
        fin = kqz[:, :, :, :].rearrange("p h a t -> p (h a t)")[:, 0:TT * D].rearrange("p (t d) -> p t d", t=TT)
        junk = hT[:, 0:1024]

        ps = ctx.enter_context(nc.psum_tensor("ps", [P, 8, 512], F32))

        first = sem("layer_first")
        full = [sem(f"bank_full{b}") for b in range(8)]
        free = [sem(f"bank_free{b}") for b in range(8)]
        dve_chain = sem("dve_chain")
        act_chain = sem("act_chain")
        rstd_ready = sem("rstd_ready")
        sumsq_go = sem("sumsq_go")
        xn_ready = sem("xn_ready")
        hT_ready = sem("hT_ready")
        gates_z = sem("gates_z")
        gates_e = sem("gates_e")
        gates_col = sem("gates_col")
        selin_ready = sem("selin_ready")
        rows_ready = sem("rows_ready")
        cin_ready = sem("cin_ready")
        cin_used = sem("cin_used")
        conv_ready = sem("conv_ready")
        conv_m_go = sem("conv_m_go")
        raw_ready = sem("raw_ready")
        sq_ready = sem("sq_ready")
        rn_ready = sem("rn_ready")
        beta_ready = sem("beta_ready")
        kq_in_ready = sem("kq_in_ready")
        earg_ready = sem("earg_ready")
        e_ready = sem("e_ready")
        kq_ready = sem("kq_ready")
        vb_ready = sem("vb_ready")
        a_ready = sem("a_ready")
        xt_ready = sem("xt_ready")
        x_ready = sem("x_ready")
        w_ready = sem("w_ready")
        u_ready = sem("u_ready")
        t1_ready = sem("t1_ready")
        o_sq_ready = sem("o_sq_ready")
        o_sq_in = sem("o_sq_in")
        o_rr_ready = sem("o_rr_ready")
        rraw_ready = sem("rraw_ready")
        rq_ready = sem("rq_ready")
        val_ready = sem("val_ready")
        mq_ready = sem("mq_ready")
        gate_ready = sem("gate_ready")
        rdec_ready = sem("rdec_ready")
        p_ready = sem("p_ready")
        em_ready = sem("em_ready")
        mix_ready = sem("mix_ready")
        x_mixed = sem("x_mixed")
        route_in = sem("route_in")
        route_exp = sem("route_exp")
        mask_ready = sem("mask_ready")
        part_ready = sem("part_ready")
        rest_ready = sem("rest_ready")
        acc_init = sem("acc_init")
        acc_last = sem("acc_last")
        x_out = sem("x_out")
        last = sem("layer_last")
        const_in = sem("const_in")
        x_loaded = sem("x_loaded")
        init_done = sem("init_done")
        par_in = sem("par_in")
        routed = sem("routed")
        layer_end = sem("layer_end")
        layer_go = sem("layer_go")
        arrived = [sem(f"slot_arrived{s}") for s in range(RING)]
        slots_free = sem("slots_free")
        psel_ready = sem("psel_ready")
        gath_full = sem("gath_full")
        hq_ready = sem("hq_ready")
        pwt_full = sem("pwt_full")
        pwt_ready = sem("pwt_ready")
        gate_full = sem("gate_full")
        sg_ready = sem("sg_ready")
        up_full = sem("up_full")
        hmid_ready = sem("hmid_ready")
        hmt_full = sem("hmt_full")
        hmt_ready = sem("hmt_ready")
        y_full = sem("y_full")
        y0_ready = sem("y0_ready")
        y1_ready = sem("y1_ready")
        gfin_in = sem("gfin_in")
        out_ready = sem("out_ready")
        out_done = sem("out_done")
        per_layer = range(first.num, last.num + 1)

        def rounds_done(eng, rounds):
            return eng.snap(rounds, min_val=0, max_val=MAXROUND * QUADS * LAYERS)

        def end_of_layer(eng, l):
            eng.sem_inc(layer_end, 1)
            eng.wait_ge(layer_go, l + 1)

        block = ctx.enter_context(nc.Block())

        @block.sync
        def _(sync):
            def load_quad(l, q, base):
                for m, src in enumerate((e_gate, e_up, e_down)):
                    for e in range(4):
                        i = 4 * m + e
                        sync.wait_ge(slots_free, base + i + 1)
                        sync.dma_start(ring[:, i, :], src[l, q * 4 + e]).then_inc(arrived[i], 16)

            sync.dma_start(x[:, :, :], x_in).then_inc(x_loaded, 16)
            with sync.Fori(0, LAYERS) as l:
                start = l * (NMIX + QUADS * RING)
                for i in range(NMIX):
                    s = i % RING
                    n = WIDTH[PROJ[i][0]] if i < NPROJ else COLS
                    sync.wait_ge(slots_free, start + i + 1)
                    dst = ring[:, s, :].rearrange("p (k c) -> p k c", k=KD)
                    src = w_mix[l, i].rearrange("p (k c) -> p k c", k=KD)
                    if n == COLS:
                        dst, src = ring[:, s, :], w_mix[l, i]
                    else:
                        dst, src = dst[:, :, 0:n], src[:, :, 0:n]
                    sync.dma_start(dst, src).then_inc(arrived[s], 16)
                with sync.Fori(0, QUADS) as q:
                    load_quad(l, q, start + NMIX + q * RING)
                sync.sem_inc(layer_end, 1)
            sync.wait_ge(out_ready, 1)
            sync.dma_start(out, fin).then_inc(out_done, 16)
            sync.wait_ge(out_done, 16)

        @block.gpsimd
        def _(pool):
            pool.dma_start(cst[:, :, :], consts[:, 0:len(CONST) * P].rearrange("p (a b) -> p a b", b=P)).then_inc(const_in, 16)
            o = len(CONST) * P
            pool.dma_start(maskc[:, :], consts[:, o:o + T]).then_inc(const_in, 16)
            pool.dma_start(dist[:, :], consts[:, o + T:o + T + 384]).then_inc(const_in, 16)
            o += T + 384
            pool.dma_start(rot[:, :, :], consts[:, o:o + 2 * T].rearrange("p (a b) -> p a b", b=T)).then_inc(const_in, 16)
            pool.dma_start(iota[:, :], consts[:, o + 2 * T:o + 2 * T + COUNT + 8]).then_inc(const_in, 16)
            pool.dma_start(lvl[:, :, :], level_masks).then_inc(const_in, 16)
            pool.memset(selin[:, :, :, :], 0.0).then_inc(init_done, 1)
            pool.memset(rows[:, :], 0.0).then_inc(init_done, 1)
            pool.memset(epsc[:, :], EPS).then_inc(init_done, 1)
            pool.memset(rt[:, :, :], -3e38).then_inc(init_done, 1)
            pool.memset(kqz[:, :, :, :], 0.0).then_inc(init_done, 1)
            pool.memset(sel[:, :, :, :], -1.0).then_inc(init_done, 1)
            with pool.Fori(0, LAYERS) as l:
                pool.dma_start(par[:, :], params[l]).then_inc(par_in, 16)
                pool.dma_start(rw[:, :, :], router_w[l]).then_inc(par_in, 16)
                pool.wait_ge(layer_end, l * 4 + 4)
                pool.sem_inc(first, 1)
                pool.sem_clear(per_layer)
                pool.sem_inc(layer_go, 1)
            pool.dma_start(gfin, gain_final).then_inc(gfin_in, 16)
            pool.wait_ge(gfin_in, 16)

        @block.tensor
        def _(pe):
            rounds = pe.alloc_register("pe_rounds")
            pe.reg_mov(rounds, 0)
            nreg = pe.alloc_register("pe_nround")

            def begin(name):
                b, n = bank_of[name]
                if n:
                    pe.wait_ge(free[b], n)
                return ps[:, b, :]

            def done(ins, name):
                ins.then_inc(full[bank_of[name][0]], 1)

            def have_slot(start_lap, i):
                pe.wait_ge(arrived[i % RING], (start_lap + i // RING) * 16 + 16)

            def slot_w(i):
                return ring[:, i % RING, :].rearrange("p (k c) -> p k c", k=KD)

            held = []

            def release():
                if held:
                    b, n = bank_of[held.pop()]
                    pe.wait_ge(full[b], n + 1)
                    pe.sem_inc(slots_free, 1)

            def project_cm(name, start_lap):
                i = SLOT_OF[name]
                bank = begin(name)
                have_slot(start_lap, i)
                w = slot_w(i)
                for ct in range(WIDTH[name] // P):
                    for k in range(KD):
                        mm = pe.matmul(bank[:, ct * T:(ct + 1) * T], w[:, k, ct * P:(ct + 1) * P], hT3[:, k, :],
                                       start=(k == 0), stop=(k == KD - 1))
                done(mm, name)
                release()
                held.append(name)

            def project_tm(name, start_lap):
                i = SLOT_OF[name]
                n = WIDTH[name]
                bank = begin(name)
                have_slot(start_lap, i)
                w = slot_w(i)
                for j in range(TT):
                    for k in range(KD):
                        mm = pe.matmul(bank[:, j * n:(j + 1) * n], hT3[:, k, j * P:(j + 1) * P], w[:, k, 0:n],
                                       start=(k == 0), stop=(k == KD - 1))
                done(mm, name)
                release()
                held.append(name)

            def transpose_x(kind, xn_count):
                for i in range(4):
                    j, half = i // 2, i % 2
                    bank = begin((kind, i))
                    if half == 0:
                        pe.wait_ge(xn_ready, xn_count + j + 1)
                    for kk in range(4):
                        k = half * 4 + kk
                        mm = pe.transpose(bank[:, kk * P:(kk + 1) * P], xn3[:, j, k:D:KD], c("ident"))
                    done(mm, (kind, i))

            pe.sem_inc(slots_free, RING)
            pe.wait_ge(const_in, 16 * 6)
            pe.wait_ge(x_loaded, 16)
            pe.wait_ge(init_done, 6)
            with pe.Fori(0, LAYERS) as l:
                lap = l * (NMIX // RING + QUADS)
                transpose_x("hT", 0)
                pe.wait_ge(hT_ready, 4)
                project_tm("gates", lap)
                for s in range(5):
                    project_cm(("gdn", s), lap)

                pe.wait_ge(selin_ready, 1)
                bank = begin("rows")
                for j in range(TT):
                    o_ = bank[:, j * P:(j + 1) * P]
                    pe.matmul(o_, selin[:, 0, j, :], c("ncum"), start=True, stop=False)
                    pe.matmul(o_, selin[:, 1, j, :], c("ident"), start=False, stop=False)
                    pe.matmul(o_, selin[:, 2, j, :], c("cum"), start=False, stop=(j == 0))
                    if j:
                        pe.matmul(o_, selin[:, 2, 0, :], c("ones"), start=False, stop=True)
                for j in range(TT):
                    o_ = bank[64:64 + MH, T + j * P:T + (j + 1) * P]
                    mm = pe.matmul(o_, dpos[:, j, GH:GH + MH], c("ncum"), start=True, stop=(j == 0))
                    if j:
                        mm = pe.matmul(o_, dpos[:, 0, GH:GH + MH], c("nones"), start=False, stop=True)
                done(mm, "rows")
                release()
                bank = begin("cols")
                pe.matmul(bank[:, 0:12], c("cum"), dpos[:, 0, :], start=True, stop=True)
                pe.matmul(bank[:, 12:24], c("cum"), dpos[:, 1, :], start=True, stop=False)
                pe.matmul(bank[:, 18:24], c("ones"), dpos[:, 0, GH:GH + MH], start=False, stop=True)
                mm = pe.matmul(bank[:, 24:24 + GH], c("nsuffix"), dpos[:, 0, 0:GH], start=True, stop=True)
                done(mm, "cols")
                pe.wait_ge(rows_ready, 1)
                for p in range(GP):
                    if p % 2 == 0:
                        bank = begin(("beta", p // 2))
                    for a in range(2):
                        r = GH + 2 * p + a
                        mm = pe.matmul(bank[64 * a:64 * a + 64, (p % 2) * T:(p % 2) * T + T],
                                       cst[:, 0, r:r + 1].to_broadcast([P, 64]), rows[:, :], start=True, stop=True)
                    if p % 2 or p == GP - 1:
                        done(mm, ("beta", p // 2))
                for s in range(3):
                    bank = begin(("nrm", s))
                    pe.wait_ge(sq_ready, s + 1)
                    mm = pe.matmul(bank[:, :], c("headsum"), sqn[:, 2 * s:2 * s + 2, :], start=True, stop=True)
                    done(mm, ("nrm", s))
                def decay_rows(i):
                    bank = begin(("dec", i))
                    for a in range(2):
                        r = 2 * i + a
                        mm = pe.matmul(bank[:, a * T:(a + 1) * T], cst[:, 0, r:r + 1].to_broadcast([P, P]), rows[:, :],
                                       start=True, stop=True)
                    done(mm, ("dec", i))

                pe.wait_ge(raw_ready, 9)
                for p in range(GP):
                    bank = begin(("vt", p))
                    for j in range(TT):
                        mm = pe.transpose(bank[:, j * P:(j + 1) * P], raw3[:, 6 + p, j * P:(j + 1) * P], c("ident"))
                    done(mm, ("vt", p))
                decay_rows(0)
                for h in range(GH):
                    if h % 2 == 0 and h // 2 + 1 < GP:
                        decay_rows(h // 2 + 1)
                    pe.wait_ge(kq_in_ready, h // 2 + 1)
                    bank = begin(("kq0", h))
                    done(pe.matmul(bank[:, :], kf[:, h // 2, 0:P], kqz[:, h, :, :], start=True, stop=True), ("kq0", h))
                    bank = begin(("kq1", h))
                    done(pe.matmul(bank[:, 0:T], kf[:, h // 2, P:T], kqz[:, h, :, P:T], start=True, stop=True), ("kq1", h))
                for g in range(3):
                    bank = begin(("A", g))
                    pe.wait_ge(kq_ready, 2 * g + 2)
                    for m in range(4):
                        h, j = 2 * g + m // 2, m % 2
                        mm = pe.transpose(bank[:, m * P:(m + 1) * P], KQ[:, h, 0, 256 * j:256 * j + P], c("ident"))
                    done(mm, ("A", g))
                for g in range(3):
                    bank = begin(("X", 0, g))
                    pe.wait_ge(xt_ready, g + 1)
                    for m in range(4):
                        mm = pe.transpose(bank[:, m * P:(m + 1) * P], XT[:, 4 * g + m, :], c("ident"))
                    done(mm, ("X", 0, g))
                for lev in range(1, 7):
                    for g in range(3):
                        bank = begin(("W", lev, g))
                        pe.wait_ge(a_ready, g + 1)
                        pe.wait_ge(xt_ready, 3 * lev + g - 2)
                        for m in range(4):
                            mm = pe.matmul(bank[:, m * P:(m + 1) * P], Amat[:, 4 * g + m, :], XT[:, 4 * g + m, :],
                                           start=True, stop=True)
                        done(mm, ("W", lev, g))
                    for g in range(3):
                        bank = begin(("Z", lev, g))
                        pe.wait_ge(w_ready, 3 * (lev - 1) + g + 1)
                        pe.wait_ge(x_ready, 3 * (lev - 1) + g + 1)
                        for m in range(4):
                            h, j = 2 * g + m // 2, m % 2
                            mm = pe.matmul(bank[:, m * P:(m + 1) * P], X[:, 4 * g + m, :], KQ[:, h, 0, 256 * j:256 * j + P],
                                           start=True, stop=True)
                        done(mm, ("Z", lev, g))
                    if lev < 6:
                        for g in range(3):
                            bank = begin(("X", lev, g))
                            pe.wait_ge(xt_ready, 3 * lev + g + 1)
                            for m in range(4):
                                mm = pe.transpose(bank[:, m * P:(m + 1) * P], XT[:, 4 * g + m, :], c("ident"))
                            done(mm, ("X", lev, g))
                bank = begin("u1")
                pe.wait_ge(xt_ready, 21)
                pe.wait_ge(vb_ready, 3)
                for h in range(GH):
                    mm = pe.matmul(bank[:, h * HD:(h + 1) * HD], XT[:, 2 * h, :], vb[:, 0, h * HD:(h + 1) * HD],
                                   start=True, stop=True)
                done(mm, "u1")
                bank = begin("t1")
                pe.wait_ge(u_ready, 1)
                for h in range(GH):
                    mm = pe.matmul(bank[:, h * HD:(h + 1) * HD], KQ[:, h, 0, P:2 * P], vb[:, 0, h * HD:(h + 1) * HD],
                                   start=True, stop=True)
                done(mm, "t1")
                bank = begin("u2")
                pe.wait_ge(t1_ready, 1)
                for h in range(GH):
                    mm = pe.matmul(bank[:, h * HD:(h + 1) * HD], XT[:, 2 * h + 1, :], vb[:, 1, h * HD:(h + 1) * HD],
                                   start=True, stop=True)
                done(mm, "u2")

                def head_out(dst, value, weights):
                    pe.matmul(dst, value[0], weights[:, 0:T], start=True, stop=False)
                    return pe.matmul(dst[:, P:T], value[1], weights[:, T:384], start=False, stop=True)

                pe.wait_ge(u_ready, 2)
                for p in range(GP):
                    bank = begin(("o", p))
                    for a in range(2):
                        h = 2 * p + a
                        v = [vb[:, j, h * HD:(h + 1) * HD] for j in range(TT)]
                        mm = head_out(bank[64 * a:64 * a + 64, 0:T], v, KQ[:, h, 1, :])
                    done(mm, ("o", p))

                def head_norm(cidx, src):
                    bank = begin(("on", cidx))
                    pe.wait_ge(o_sq_ready, cidx + 1)
                    done(pe.matmul(bank[:, 0:T], c("headsum"), src, start=True, stop=True), ("on", cidx))

                for p in range(GP):
                    head_norm(p, raw3[:, p, :])

                project_cm(("rqk", 0), lap)
                project_cm(("rqk", 1), lap)
                for a in range(2):
                    bank = begin(("rsw", a))
                    pe.wait_ge(rraw_ready, a + 1)
                    done(pe.matmul(bank[:, :], c("swap"), rraw[:, a, :, :], start=True, stop=True), ("rsw", a))
                project_tm(("rv", 0), lap)
                for s in range(3):
                    project_cm(("mqk", s), lap)
                for s in range(3):
                    project_tm(("mv", s), lap)
                for s in range(5):
                    project_cm(("gate", s), lap)
                release()
                pe.wait_ge(rq_ready, 2)
                for h in range(RH):
                    bank = begin(("rs", h))
                    pe.matmul(bank[:, 0:T], rkf[:, h // 2, 0:P], kqz[:, h, 0, :], start=True, stop=True)
                    done(pe.matmul(bank[:, T:384], rkf[:, h // 2, P:T], kqz[:, h, 0, P:T], start=True, stop=True), ("rs", h))
                for p in range(RP):
                    bank = begin(("o", 3 + p))
                    if p == 0:
                        pe.wait_ge(val_ready, 1)
                    for a in range(2):
                        h = 2 * p + a
                        pe.wait_ge(p_ready, h + 1)
                        v = [vr[:, j, h * HD:(h + 1) * HD] for j in range(TT)]
                        mm = head_out(bank[64 * a:64 * a + 64, 0:T], v, prob[:, a, :])
                    done(mm, ("o", 3 + p))
                for p in range(RP):
                    head_norm(3 + p, sqo[:, p, :])
                pe.wait_ge(mq_ready, 12)
                pe.wait_ge(val_ready, 4)
                for p in range(MP):
                    bank = begin(("mdec", p))
                    for a in range(2):
                        r = 32 + 2 * p + a
                        mm = pe.matmul(bank[:, a * T:(a + 1) * T], cst[:, 0, r:r + 1].to_broadcast([P, P]), rows[:, :],
                                       start=True, stop=True)
                    done(mm, ("mdec", p))
                    for h in (2 * p, 2 * p + 1):
                        bank = begin(("ms", h))
                        pe.matmul(bank[:, 0:T], kf[:, p, 0:P], kqz[:, h, 1, :], start=True, stop=True)
                        done(pe.matmul(bank[:, T:384], kf[:, p, P:T], kqz[:, h, 1, P:T], start=True, stop=True), ("ms", h))
                    bank = begin(("em", p))
                    for a in range(2):
                        r = 64 + 2 * p + a
                        mm = pe.matmul(bank[64 * a:64 * a + 64, 0:T], cst[:, 0, r:r + 1].to_broadcast([P, 64]), rows[:, :],
                                       start=True, stop=True)
                    done(mm, ("em", p))
                    bank = begin(("o", 5 + p))
                    one = [cst[:, CONST.index("ones"), 0:64]] * 2
                    for a in range(2):
                        h = 2 * p + a
                        pe.wait_ge(p_ready, RH + h + 1)
                        v = [vm[:, j, h * HD:(h + 1) * HD] for j in range(TT)]
                        head_out(bank[64 * a:64 * a + 64, 0:T], v, prob[:, a, :])
                        mm = head_out(bank[64 * a:64 * a + 64, T:2 * T], one, prob[:, a, :])
                    done(mm, ("o", 5 + p))
                    head_norm(5 + p, sqo[:, 2 + p, :])
                pe.wait_ge(mix_ready, MIX)
                for n in range(D // COLS):
                    i = NPROJ + n
                    bank = begin(("wo", n))
                    have_slot(lap, i)
                    w = slot_w(i)
                    for j in range(TT):
                        for k in range(KD):
                            mm = pe.matmul(bank[:, j * COLS:(j + 1) * COLS], mixT[:, k, j * P:(j + 1) * P], w[:, k, :],
                                           start=(k == 0), stop=(k == KD - 1))
                    done(mm, ("wo", n))
                    release()
                    held.append(("wo", n))
                release()
                transpose_x("h2T", 2)
                pe.wait_ge(hT_ready, 8)
                bank = begin("logits")
                for j in range(TT):
                    for k in range(KD):
                        mm = pe.matmul(bank[:, j * 36:(j + 1) * 36], hT3[:, k, j * P:(j + 1) * P], rw[:, k, :],
                                       start=(k == 0), stop=(k == KD - 1))
                done(mm, "logits")
                bank = begin("rank")
                pe.wait_ge(mask_ready, 1)
                pe.matmul(bank[:, 0:32], c("before"), pick[:, 0, 0, :], start=True, stop=True)
                pe.matmul(bank[:, 32:64], c("before"), pick[:, 0, 1, :], start=True, stop=False)
                pe.matmul(bank[:, 32:64], c("ones"), pick[:, 0, 0, :], start=False, stop=True)
                pe.matmul(bank[:, 64:96], c("ones"), pick[:, 0, 0, :], start=True, stop=False)
                mm = pe.matmul(bank[:, 64:96], c("ones"), pick[:, 0, 1, :], start=False, stop=True)
                done(mm, "rank")
                for b in range(8):
                    pe.wait_ge(free[b], uses[b])
                for j in range(TT):
                    for n in range(2):
                        mm = pe.matmul(ps[:, 2 * j + n, :], c("ident"), x[:, j, n * 512:(n + 1) * 512],
                                       start=True, stop=False, skip_group_check=True)
                mm.then_inc(acc_init, 1)
                pe.wait_ge(routed, l + 1)
                pe.sem_inc(first, 1)

                def gather(n):
                    pe.wait_ge(psel_ready, n * 2 + 1)
                    for half in range(2):
                        for kk in range(4):
                            k = half * 4 + kk
                            for j in range(TT):
                                for i in range(3):
                                    mm = pe.matmul(ps[:, 4 + 3 * half, kk * P:(kk + 1) * P], part[i][:, j, k:D:KD], Psel[:, j, :],
                                                   start=(j == 0 and i == 0), stop=(j == TT - 1 and i == 2))
                        mm.then_inc(gath_full, 1)

                pe.wait_ge(part_ready, 3)
                pe.wait_ge(rest_ready, 2)
                gather(rounds_done(pe, rounds) + l)
                with pe.Fori(0, QUADS) as q:
                    pe.reg_load(nreg, nround[0:1, bass.ds(q, 1)])
                    nv = pe.snap(nreg, min_val=1, max_val=MAXROUND)
                    qlap = lap + NMIX // RING + q
                    with pe.Fori(0, nv) as r:
                        n = rounds_done(pe, rounds)
                        pe.wait_ge(hq_ready, (n + l) * 2 + 2)
                        for m in range(2):
                            for e in range(4):
                                pe.wait_ge(arrived[4 * m + e], qlap * 16 + 16)
                            for k in range(KD):
                                for e in range(4):
                                    mm = pe.matmul(ps[32 * e:32 * e + 32, 5 + m, 0:DE], hq[:, k, 32 * e:32 * e + 32],
                                                   ring[:, 4 * m + e, k * DE:(k + 1) * DE],
                                                   start=(k == 0), stop=(k == KD - 1), skip_group_check=True)
                            mm.then_inc((gate_full, up_full)[m], 1)
                            if m == 0:
                                pe.wait_ge(psel_ready, (n + l) * 2 + 2)
                                for j in range(TT):
                                    mm = pe.transpose(ps[:, 4, j * P:(j + 1) * P], Pwt[:, j, :], c("ident"))
                                mm.then_inc(pwt_full, 1)
                        pe.wait_ge(pwt_ready, n + 1)
                        gather(n + l + 1)
                        pe.wait_ge(up_full, n + 1)
                        with pe.If(r == nv - 1):
                            pe.sem_inc(slots_free, 8)
                        pe.wait_ge(hmid_ready, n + 1)
                        for f in range(2):
                            mm = pe.transpose(ps[:, 6, T + f * P:T + (f + 1) * P], hmid[:, f:DE:2], c("ident"))
                        mm.then_inc(hmt_full, 1)
                        pe.wait_ge(hmt_ready, n + 1)
                        for e in range(4):
                            pe.wait_ge(arrived[8 + e], qlap * 16 + 16)
                        for h in range(2):
                            for f in range(2):
                                for e in range(4):
                                    mm = pe.matmul(ps[32 * e:32 * e + 32, 5 + h, :], hmT[:, f, 32 * e:32 * e + 32],
                                                   ring[:, 8 + e, f * D + h * 512:f * D + (h + 1) * 512],
                                                   start=(f == 0), stop=(f == 1), skip_group_check=True)
                            mm.then_inc(y_full, 1)
                        pe.wait_ge(y_full, n * 2 + 2)
                        with pe.If(r == nv - 1):
                            pe.sem_inc(slots_free, 4)
                        for h in range(2):
                            pe.wait_ge((y0_ready, y1_ready)[h], n + 1)
                            for j in range(TT):
                                mm = pe.matmul(ps[:, 2 * j + h, :], PwT[:, j * P:(j + 1) * P], ysb[:, h, :],
                                               start=False, stop=False, skip_group_check=True)
                        pe.reg_add(rounds, rounds, 1)
                pe.drain().then_inc(acc_last, 1)
                end_of_layer(pe, l)

        @block.scalar
        def _(act):
            rounds = act.alloc_register("act_rounds")
            act.reg_mov(rounds, 0)
            nreg = act.alloc_register("act_nround")
            chain = [0]

            def link(ins):
                chain[0] += 1
                ins.then_inc(act_chain, 1)
                act.wait_ge(act_chain, chain[0])

            def get(name):
                b, n = bank_of[name]
                act.wait_ge(full[b], n + 1)
                return ps[:, b, :]

            def rstd(done_sem, count):
                for j in range(TT):
                    link(act.activation(junk, x[:, j, :], ACT.Square, accum_out=ss[:, j:j + 1]))
                link(act.activation(ss[:, 2:4], ss[:, 0:2], ACT.Ln, scale=1.0 / D, bias=epsc[:, :]))
                act.activation(ss[:, 4:6], ss[:, 2:4], ACT.Exp, scale=-0.5).then_inc(done_sem, 1)

            def conv_in(name, tiles, cin, i0):
                bank = get(name)
                for n_, _ in enumerate(tiles):
                    i = i0 + n_
                    if i >= 3:
                        act.wait_ge(cin_used, i - 2)
                    ins = act.activation(cin[:, i % 3, 3:3 + T], bank[:, n_ * T:(n_ + 1) * T], ACT.Copy)
                    link(ins)
                    act.sem_inc(cin_ready, 1)
                act.sem_inc(free[bank_of[name][0]], 1)

            act.wait_ge(const_in, 16 * 6)
            act.wait_ge(x_loaded, 16)
            act.wait_ge(init_done, 6)
            with act.Fori(0, LAYERS) as l:
                act.wait_ge(par_in, l * 32 + 32)
                act.sem_inc(first, 1)
                rstd(rstd_ready, 0)
                act.activation(ea[:, :], pv("a_log", 0, GH), ACT.Exp).then_inc(gates_e, 1)
                act.wait_ge(gates_z, 1)
                link(act.activation(sp[:, 2, :, :], sp[:, 1, :, :], ACT.Exp, scale=-1.0))
                act.activation(sp[:, 3, :, :], sp[:, 2, :, :], ACT.Ln, bias=1.0).then_inc(gates_e, 1)
                act.wait_ge(gates_col, 1)
                act.activation(beta[:, :, :], sp[:, 0, :, 0:GH], ACT.Exp).then_inc(gates_e, 1)
                slots = [(0, 1), (2, 3), (4, 5), (6, 7), (8,)]
                for s, tiles in enumerate(slots):
                    conv_in(("gdn", s), tiles, cin_g, 2 * s)
                    if s:
                        for t in slots[s - 1]:
                            act.wait_ge(conv_ready, t + 1)
                            act.activation(raw3[:, t, :], acc_g[:, t % 4, :], ACT.Silu).then_inc(raw_ready, 1)
                act.wait_ge(conv_ready, 9)
                act.activation(raw3[:, 8, :], acc_g[:, 0, :], ACT.Silu).then_inc(raw_ready, 1)
                act.wait_ge(raw_ready, 9)
                for s in range(3):
                    act.activation(sqn[:, 2 * s:2 * s + 2, :], raw3[:, 2 * s:2 * s + 2, :], ACT.Square).then_inc(sq_ready, 1)
                for p in range(GP):
                    bank = get(("beta", p // 2))
                    ins = act.activation(betab[:, p, :], bank[:, (p % 2) * T:(p % 2) * T + T], ACT.Exp)
                    link(ins)
                    act.sem_inc(beta_ready, 1)
                    if p % 2 or p == GP - 1:
                        act.sem_inc(free[bank_of[("beta", p // 2)][0]], 1)
                for s in range(3):
                    bank = get(("nrm", s))
                    ins = act.activation(rn[:, 2 * s:2 * s + 2, :], bank[:, :], ACT.Ln, bias=epsc[:, :])
                    link(ins)
                    act.sem_inc(free[bank_of[("nrm", s)][0]], 1)
                    act.activation(rn[:, 2 * s:2 * s + 2, :], rn[:, 2 * s:2 * s + 2, :], ACT.Exp, scale=-0.5).then_inc(rn_ready, 1)
                for h in range(GH):
                    act.wait_ge(earg_ready, h + 1)
                    act.activation(ebuf[:, h % 2, :], ebuf[:, h % 2, :], ACT.Exp).then_inc(e_ready, 1)
                act.wait_ge(kq_ready, GH)
                for g in range(3):
                    bank = get(("A", g))
                    link(act.activation(Amat[:, 4 * g:4 * g + 4, :], bank[:, :], ACT.Copy))
                    act.sem_inc(a_ready, 1)
                    act.sem_inc(free[bank_of[("A", g)][0]], 1)
                for lev in range(6):
                    for g in range(3):
                        bank = get(("X", lev, g))
                        link(act.activation(X[:, 4 * g:4 * g + 4, :], bank[:, :], ACT.Copy))
                        act.sem_inc(x_ready, 1)
                        act.sem_inc(free[bank_of[("X", lev, g)][0]], 1)
                for i, name in enumerate(("u1", "u2")):
                    bank = get(name)
                    link(act.activation(vb[:, i, :], bank[:, 0:GW], ACT.Copy))
                    act.sem_inc(u_ready, 1)
                    act.sem_inc(free[bank_of[name][0]], 1)

                def out_rr(cidx, dst):
                    bank = get(("on", cidx))
                    link(act.activation(dst, bank[:, 0:T], ACT.Ln, scale=1.0 / HD, bias=epsc[:, :]))
                    act.sem_inc(free[bank_of[("on", cidx)][0]], 1)
                    act.activation(dst, dst, ACT.Exp, scale=-0.5).then_inc(o_rr_ready, 1)

                for p in range(GP):
                    bank = get(("o", p))
                    act.activation(raw3[:, p, :], bank[:, 0:T], ACT.Square).then_inc(o_sq_ready, 1)
                for p in range(GP):
                    out_rr(p, raw3[:, 3 + p, :])
                for a in range(2):
                    bank = get(("rqk", a))
                    link(act.activation(rraw[:, a, :, :], bank[:, :], ACT.Copy))
                    act.sem_inc(rraw_ready, 1)
                    act.sem_inc(free[bank_of[("rqk", a)][0]], 1)
                bank = get(("rv", 0))
                link(act.activation(vr[:, :, :], bank.rearrange("p (j c) -> p j c", j=TT), ACT.Copy))
                act.sem_inc(val_ready, 1)
                act.sem_inc(free[bank_of[("rv", 0)][0]], 1)

                def mlstm_silu(t):
                    act.wait_ge(conv_ready, 9 + t + 1)
                    src = acc_m[:, t % 4, :]
                    if t < MP:
                        for a in range(2):
                            act.activation(kqz[64 * a:64 * a + 64, 2 * t + a, 1, :], src[64 * a:64 * a + 64, :],
                                           ACT.Silu).then_inc(mq_ready, 1)
                    else:
                        act.activation(kf[:, t - MP, :], src, ACT.Silu).then_inc(mq_ready, 2)

                act.wait_ge(conv_m_go, 1)
                for s in range(3):
                    conv_in(("mqk", s), (0, 1), cin_m, 9 + 2 * s)
                    if s:
                        mlstm_silu(2 * s - 2)
                        mlstm_silu(2 * s - 1)
                mlstm_silu(4)
                mlstm_silu(5)
                for s in range(3):
                    bank = get(("mv", s))
                    link(act.activation(vm[:, :, P * s:P * (s + 1)], bank[:, 0:T].rearrange("p (j c) -> p j c", j=TT), ACT.Copy))
                    act.sem_inc(val_ready, 1)
                    act.sem_inc(free[bank_of[("mv", s)][0]], 1)
                for s, tiles in enumerate(GATE_TILES):
                    bank = get(("gate", s))
                    for n_, ct in enumerate(tiles):
                        f, sc = (ACT.Silu, 1.0) if ct < GP + RP else (ACT.Tanh, 0.5)
                        link(act.activation(gateT[:, ct, :], bank[:, n_ * T:(n_ + 1) * T], f, scale=sc))
                    act.sem_inc(gate_ready, 1)
                    act.sem_inc(free[bank_of[("gate", s)][0]], 1)
                for h in range(RH):
                    if h >= 2:
                        act.wait_ge(p_ready, h - 1)
                    lgam = math.log(1.0 - 2.0 ** (-5.0 - h))
                    act.activation(ebuf[:, h % 2, :], dist[:, :], ACT.Exp, scale=lgam).then_inc(rdec_ready, 1)
                for p in range(RP):
                    bank = get(("o", 3 + p))
                    act.activation(sqo[:, p, :], bank[:, 0:T], ACT.Square).then_inc(o_sq_ready, 1)
                for p in range(RP):
                    out_rr(3 + p, rro[:, p, :])
                for p in range(MP):
                    for h in (2 * p, 2 * p + 1):
                        act.wait_ge(earg_ready, GH + h + 1)
                        act.activation(ebuf[:, h % 2, :], ebuf[:, h % 2, :], ACT.Exp).then_inc(e_ready, 1)
                    bank = get(("em", p))
                    if p:
                        act.wait_ge(o_sq_in, p)
                    link(act.activation(mtmp[:, 0, :], bank[:, 0:T], ACT.Exp, scale=-1.0))
                    act.sem_inc(free[bank_of[("em", p)][0]], 1)
                    bank = get(("o", 5 + p))
                    act.activation(mtmp[:, 1, :], bank[:, T:2 * T], ACT.Abs).then_inc(em_ready, 1)
                    act.wait_ge(o_sq_in, p + 1)
                    act.activation(sqo[:, 2 + p, :], mixT[:, 5 + p, :], ACT.Square).then_inc(o_sq_ready, 1)
                    out_rr(5 + p, rro[:, p, :])
                act.wait_ge(x_mixed, 4)
                rstd(rstd_ready, 1)
                for j in range(TT):
                    act.wait_ge(xn_ready, 3 + j)
                    act.activation(part[0][:, j, :], xn3[:, j, :], ACT.Copy).then_inc(part_ready, 1)
                act.wait_ge(rest_ready, 1)
                act.activation(part[1], rest, ACT.Copy).then_inc(part_ready, 1)
                act.wait_ge(route_in, 1)
                act.activation(rt[:, :, 24:28], rt[:, :, 20:24], ACT.Exp).then_inc(route_exp, 1)
                act.wait_ge(route_in, 2)
                act.activation(rt[:, :, 60:61], rt[:, :, 59:60], ACT.Exp).then_inc(route_exp, 1)
                act.wait_ge(routed, l + 1)
                act.sem_inc(first, 1)
                with act.Fori(0, QUADS) as q:
                    act.reg_load(nreg, nround[0:1, bass.ds(q, 1)])
                    nv = act.snap(nreg, min_val=1, max_val=MAXROUND)
                    with act.Fori(0, nv) as r:
                        n = rounds_done(act, rounds)
                        act.wait_ge(gate_full, n + 1)
                        act.activation(sg, ps[:, 5, 0:DE], ACT.Silu).then_inc(sg_ready, 1)
                        act.wait_ge(pwt_full, n + 1)
                        act.activation(PwT, ps[:, 4, 0:T], ACT.Copy).then_inc(pwt_ready, 1)
                        act.wait_ge(hmt_full, n + 1)
                        act.activation(hmT[:, :, :], ps[:, 6, T:2 * T], ACT.Copy).then_inc(hmt_ready, 1)
                        act.wait_ge(y_full, n * 2 + 1)
                        act.activation(ysb[:, 0, :], ps[:, 5, :], ACT.Copy).then_inc(y0_ready, 1)
                        act.reg_add(rounds, rounds, 1)
                act.wait_ge(acc_last, 1)
                for b in range(4):
                    act.activation(x[:, b // 2, (b % 2) * 512:(b % 2 + 1) * 512], ps[:, b, :], ACT.Copy).then_inc(x_out, 1)
                act.wait_ge(x_out, 4)
                end_of_layer(act, l)
            chain[0] = 0
            rstd(rstd_ready, 0)

        @block.vector
        def _(dve):
            rounds = dve.alloc_register("dve_rounds")
            dve.reg_mov(rounds, 0)
            nreg = dve.alloc_register("dve_nround")
            chain = [0]
            TTn = dve.tensor_tensor

            def link(ins):
                chain[0] += 1
                ins.then_inc(dve_chain, 1)
                dve.wait_ge(dve_chain, chain[0])

            def get(name):
                b, n = bank_of[name]
                dve.wait_ge(full[b], n + 1)
                return ps[:, b, :]

            def free_(name):
                dve.sem_inc(free[bank_of[name][0]], 1)

            def scale_x(count):
                dve.wait_ge(rstd_ready, count)
                for j in range(TT):
                    dve.tensor_scalar(xn3[:, j, :], x[:, j, :], ss[:, 4 + j:5 + j], None, ALU.mult).then_inc(xn_ready, 1)

            def evac_hT(kind, gain):
                for i in range(4):
                    j, half = i // 2, i % 2
                    bank = get((kind, i))
                    g = pv(gain, half * 4, 4).unsqueeze(2).to_broadcast([P, 4, P])
                    link(TTn(hT3[:, half * 4:half * 4 + 4, j * P:(j + 1) * P],
                             bank.rearrange("p (k t) -> p k t", k=4), g, ALU.mult))
                    dve.sem_inc(hT_ready, 1)
                    free_((kind, i))

            def conv(i, cin, acc, w):
                dve.wait_ge(cin_ready, i + 1)
                s, a = cin[:, i % 3, :], acc[:, (i if i < 9 else i - 9) % 4, :]
                j_ = i if i < 9 else i - 9
                if j_ >= 4:
                    if i < 9:
                        dve.wait_ge(raw_ready, j_ - 3)
                    else:
                        dve.wait_ge(mq_ready, 2 * (j_ - 3))
                link(dve.tensor_scalar(a, s[:, 0:T], w(0), None, ALU.mult))
                for t in range(1, CONV):
                    link(dve.scalar_tensor_tensor(out=a, in0=s[:, t:t + T], scalar=w(t), in1=a, op0=ALU.mult, op1=ALU.add))
                dve.sem_inc(conv_ready, 1)
                dve.sem_inc(cin_used, 1)

            dve.wait_ge(const_in, 16 * 6)
            dve.wait_ge(x_loaded, 16)
            dve.wait_ge(init_done, 6)
            with dve.Fori(0, LAYERS) as l:
                dve.wait_ge(par_in, l * 32 + 32)
                dve.sem_inc(first, 1)
                scale_x(1)
                evac_hT("hT", "gain_mix")
                link(dve.memset(cin_g[:, :, 0:3], 0.0))
                bank = get("gates")
                b3 = bank[:, 0:TT * NG].rearrange("p (j c) -> p j c", j=TT)
                bias = pv("bias3", 0, 24).unsqueeze(1).to_broadcast([P, TT, 24])
                link(TTn(gz[:, :, :], b3, bias, ALU.add))
                free_("gates")
                link(dve.tensor_scalar(sp[:, 0, :, 0:6], gz[:, :, 0:6], -1.0, None, ALU.mult))
                link(dve.tensor_copy(sp[:, 0, :, 6:12], gz[:, :, 6:12]))
                link(dve.tensor_scalar(sp[:, 0, :, 12:18], gz[:, :, 18:24], -1.0, None, ALU.mult))
                z2 = sp[:, 0, :, :].rearrange("p j c -> p (j c)")
                dve.scalar_tensor_tensor(out=sp[:, 1, :, :].rearrange("p j c -> p (j c)"), in0=z2, scalar=-1.0, in1=z2,
                                         op0=ALU.mult, op1=ALU.max).then_inc(gates_z, 1)
                dve.wait_ge(gates_e, 2)
                link(dve.scalar_tensor_tensor(out=sp[:, 1, :, :].rearrange("p j c -> p (j c)"), in0=z2, scalar=0.0,
                                              in1=sp[:, 3, :, :].rearrange("p j c -> p (j c)"), op0=ALU.max, op1=ALU.add))
                link(dve.tensor_scalar(sp[:, 0, :, 0:6], sp[:, 1, :, 0:6], -1.0, None, ALU.mult))
                dve.sem_inc(gates_col, 1)
                link(dve.tensor_copy(selin[:, 1, :, 6:12], sp[:, 0, :, 0:6]))
                eab = ea[:, :].unsqueeze(1).to_broadcast([P, TT, GH])
                link(TTn(dpos[:, :, 0:6], sp[:, 1, :, 6:12], eab, ALU.mult))
                link(dve.tensor_copy(dpos[:, :, 6:12], sp[:, 1, :, 12:18]))
                link(dve.tensor_copy(selin[:, 0, :, 0:6], dpos[:, :, 0:6]))
                for o_ in (32, 64):
                    link(dve.tensor_copy(selin[:, 1, :, o_:o_ + 6], gz[:, :, 12:18]))
                    link(dve.tensor_copy(selin[:, 2, :, o_:o_ + 6], dpos[:, :, 6:12]))
                dve.sem_inc(selin_ready, 1)

                def wg(t):
                    return lambda k: pv("conv_g", t * CONV + k)

                for t in range(9):
                    conv(t, cin_g, acc_g, wg(t))
                bank = get("rows")
                link(dve.tensor_copy(rowsraw[:, :], bank[:, 0:T]))
                link(dve.tensor_copy(rows[0:12, :], rowsraw[0:12, :]))
                for q0 in (32, 64):
                    s = rowsraw[q0:q0 + 6, :]
                    link(dve.tensor_tensor_scan(rows[q0:q0 + 6, :], s, s, 0.0, ALU.max, ALU.max))
                link(dve.tensor_scalar(rows[32:38, :], rows[32:38, :], -1.0, None, ALU.mult))
                link(TTn(rows[64:70, :], rows[64:70, :], bank[64:70, T:2 * T], ALU.add))
                dve.sem_inc(rows_ready, 1)
                free_("rows")
                bank = get("cols")
                link(dve.tensor_copy(colv[:, 0:30], bank[:, 0:30]))
                free_("cols")
                cv = colv[:, 0:24].rearrange("p (j c) -> p j c", j=TT)
                link(TTn(colA[:, :, :], cv[:, :, 6:12], gz[:, :, 12:18], ALU.add))
                dve.wait_ge(beta_ready, GP)
                for t in range(6):
                    dve.wait_ge(rn_ready, t // 2 + 1)
                    if t < 3:
                        for a in range(2):
                            r_ = slice(64 * a, 64 * a + 64)
                            link(dve.scalar_tensor_tensor(out=kqz[r_, 2 * t + a, 1, :], in0=raw3[r_, t, :], scalar=QK_SCALE,
                                                          in1=rn[r_, t, :], op0=ALU.mult, op1=ALU.mult))
                    else:
                        p = t - 3
                        link(TTn(kf[:, p, :], raw3[:, t, :], rn[:, t, :], ALU.mult))
                        for a in range(2):
                            r_ = slice(64 * a, 64 * a + 64)
                            link(TTn(kqz[r_, 2 * p + a, 0, :], kf[r_, p, :], betab[r_, p, :], ALU.mult))
                        dve.sem_inc(kq_in_ready, 1)
                dve.wait_ge(gates_e, 3)
                vb4 = vb[:, :, :].rearrange("p t (h d) -> p t h d", h=GH)

                def earg(i, p):
                    bank = get(("dec", p))
                    h = i
                    bc = bank[:, (h % 2) * T:(h % 2 + 1) * T]
                    e = ebuf[:, h % 2, :]
                    for dst, src, col, lim in ((slice(0, P), slice(0, P), colv[:, h:h + 1], maskc[:, 0:P]),
                                               (slice(P, T), slice(P, T), colv[:, 24 + h:25 + h], maskc[:, P:T]),
                                               (slice(T, 384), slice(P, T), colv[:, 12 + h:13 + h], maskc[:, 0:P])):
                        link(dve.scalar_tensor_tensor(out=e[:, dst], in0=bc[:, src], scalar=col, in1=lim,
                                                      op0=ALU.add, op1=ALU.min))
                    dve.sem_inc(earg_ready, 1)

                def kq_mul(h):
                    dve.wait_ge(e_ready, h + 1)
                    e = ebuf[:, h % 2, :]
                    bank = get(("kq0", h))
                    link(TTn(KQ[:, h, :, 0:T], bank.rearrange("p (a t) -> p a t", a=2),
                             e[:, 0:T].unsqueeze(1).to_broadcast([P, 2, T]), ALU.mult))
                    free_(("kq0", h))
                    bank = get(("kq1", h))
                    link(TTn(KQ[:, h, :, T:384], bank[:, 0:T].rearrange("p (a t) -> p a t", a=2),
                             e[:, T:384].unsqueeze(1).to_broadcast([P, 2, P]), ALU.mult))
                    free_(("kq1", h))
                    dve.sem_inc(kq_ready, 1)

                for p in range(GP):
                    bank = get(("vt", p))
                    b_ = beta[:, :, 2 * p:2 * p + 2].unsqueeze(3).to_broadcast([P, TT, 2, HD])
                    link(TTn(vb4[:, :, 2 * p:2 * p + 2, :],
                             bank[:, 0:T].rearrange("p (t h d) -> p t h d", t=TT, h=2), b_, ALU.mult))
                    free_(("vt", p))
                    dve.sem_inc(vb_ready, 1)
                for h in range(GH):
                    if h == 0:
                        earg(0, 0)
                    if h + 1 < GH:
                        earg(h + 1, (h + 1) // 2)
                    if h % 2 == 0:
                        free_(("dec", h // 2))
                    kq_mul(h)

                def diag(h):
                    return KQ[:, h, 0, :].rearrange("p (b t) -> p b t", b=3)[:, 0:3:2, :]

                idb = cst[:, 0, :].unsqueeze(1)
                for g in range(3):
                    for h in (2 * g, 2 * g + 1):
                        link(TTn(XT[:, 2 * h:2 * h + 2, :], diag(h), lvl[:, 0, :].unsqueeze(1).to_broadcast([P, 2, P]), ALU.mult))
                    link(TTn(XT[:, 4 * g:4 * g + 4, :], idb.to_broadcast([P, 4, P]), XT[:, 4 * g:4 * g + 4, :], ALU.subtract))
                    dve.sem_inc(xt_ready, 1)
                for lev in range(1, 7):
                    for g in range(3):
                        bank = get(("W", lev, g))
                        for a in range(2):
                            h = 2 * g + a
                            link(TTn(diag(h), bank[:, a * T:(a + 1) * T].rearrange("p (b t) -> p b t", b=2),
                                     lvl[:, lev, :].unsqueeze(1).to_broadcast([P, 2, P]), ALU.mult))
                        dve.sem_inc(w_ready, 1)
                        free_(("W", lev, g))
                    for g in range(3):
                        bank = get(("Z", lev, g))
                        link(TTn(XT[:, 4 * g:4 * g + 4, :], XT[:, 4 * g:4 * g + 4, :],
                                 bank.rearrange("p (m t) -> p m t", m=4), ALU.subtract))
                        dve.sem_inc(xt_ready, 1)
                        free_(("Z", lev, g))
                bank = get("t1")
                link(TTn(vb[:, 1, :], vb[:, 1, :], bank[:, 0:GW], ALU.subtract))
                dve.sem_inc(t1_ready, 1)
                free_("t1")

                def gain_out(cidx):
                    bank = get(("o", cidx))
                    dve.wait_ge(o_sq_ready, cidx + 1)
                    link(dve.tensor_scalar(mixT[:, cidx, :], bank[:, 0:T], pv("head_gain", cidx), None, ALU.mult))
                    free_(("o", cidx))

                def norm_out(cidx, rr):
                    dve.wait_ge(o_rr_ready, cidx + 1)
                    link(TTn(mixT[:, cidx, :], mixT[:, cidx, :], rr, ALU.mult))

                for p in range(GP):
                    gain_out(p)
                for p in range(GP):
                    norm_out(p, raw3[:, 3 + p, :])
                link(dve.memset(cin_m[:, :, 0:3], 0.0))
                dve.sem_inc(conv_m_go, 1)
                for a in range(2):
                    bank = get(("rsw", a))
                    sin_b = rot[:, 1, :].unsqueeze(1).to_broadcast([P, 2, T])
                    cos_b = rot[:, 0, :].unsqueeze(1).to_broadcast([P, 2, T])
                    link(TTn(rtmp[:, :, :], bank.rearrange("p (c t) -> p c t", c=2), sin_b, ALU.mult))
                    free_(("rsw", a))
                    link(TTn(rraw[:, a, :, :], rraw[:, a, :, :], cos_b, ALU.mult))
                    if a == 0:
                        for b in range(2):
                            r_ = slice(64 * b, 64 * b + 64)
                            link(TTn(kqz[r_, b:4:2, 0, :], rraw[r_, a, :, :], rtmp[r_, :, :], ALU.add))
                    else:
                        link(TTn(rkf[:, :, :], rraw[:, a, :, :], rtmp[:, :, :], ALU.add))
                    dve.sem_inc(rq_ready, 1)

                def wm(t):
                    return lambda k: pv("conv_m", t * CONV + k)

                for t in range(6):
                    conv(9 + t, cin_m, acc_m, wm(t))
                for h in range(RH):
                    bank = get(("rs", h))
                    dve.wait_ge(rdec_ready, h + 1)
                    if h == 2:
                        dve.wait_ge(full[bank_of[("o", 3)][0]], bank_of[("o", 3)][1] + 1)
                    link(dve.scalar_tensor_tensor(out=prob[:, h % 2, :], in0=bank[:, 0:384], scalar=QK_SCALE,
                                                  in1=ebuf[:, h % 2, :], op0=ALU.mult, op1=ALU.mult))
                    dve.sem_inc(p_ready, 1)
                    free_(("rs", h))
                for p in range(RP):
                    gain_out(3 + p)
                for p in range(RP):
                    norm_out(3 + p, rro[:, p, :])
                for p in range(MP):
                    bank = get(("mdec", p))
                    for a in range(2):
                        h = 2 * p + a
                        bc = bank[:, a * T:(a + 1) * T]
                        link(dve.scalar_tensor_tensor(out=ebuf[:, a, 0:T], in0=bc, scalar=colA[:, 0, h:h + 1], in1=maskc[:, :],
                                                      op0=ALU.add, op1=ALU.min))
                        link(dve.scalar_tensor_tensor(out=ebuf[:, a, T:384], in0=bc[:, P:T], scalar=colA[:, 1, h:h + 1],
                                                      in1=maskc[:, 0:P], op0=ALU.add, op1=ALU.min))
                        dve.sem_inc(earg_ready, 1)
                    free_(("mdec", p))
                    for a in range(2):
                        h = 2 * p + a
                        bank = get(("ms", h))
                        dve.wait_ge(e_ready, GH + h + 1)
                        if a == 0:
                            prev = ("o", 4 + p)
                            dve.wait_ge(full[bank_of[prev][0]], bank_of[prev][1] + 1)
                        link(dve.scalar_tensor_tensor(out=prob[:, a, :], in0=bank[:, 0:384], scalar=QK_SCALE,
                                                      in1=ebuf[:, a, :], op0=ALU.mult, op1=ALU.mult))
                        dve.sem_inc(p_ready, 1)
                        free_(("ms", h))
                    bank = get(("o", 5 + p))
                    dve.wait_ge(em_ready, p + 1)
                    link(TTn(mtmp[:, 2, :], mtmp[:, 0, :], mtmp[:, 1, :], ALU.max))
                    link(dve.reciprocal(mtmp[:, 2, :], mtmp[:, 2, :]))
                    link(TTn(mixT[:, 5 + p, :], bank[:, 0:T], mtmp[:, 2, :], ALU.mult))
                    dve.sem_inc(o_sq_in, 1)
                    free_(("o", 5 + p))
                    dve.wait_ge(o_rr_ready, 5 + p + 1)
                    link(dve.scalar_tensor_tensor(out=mixT[:, 5 + p, :], in0=mixT[:, 5 + p, :], scalar=pv("head_gain", 5 + p),
                                                  in1=rro[:, p, :], op0=ALU.mult, op1=ALU.mult))
                dve.wait_ge(gate_ready, 5)
                for ct in range(MIX):
                    if ct >= GP + RP:
                        link(dve.tensor_scalar(gateT[:, ct, :], gateT[:, ct, :], 0.5, 0.5, ALU.mult, ALU.add))
                    link(TTn(mixT[:, ct, :], mixT[:, ct, :], gateT[:, ct, :], ALU.mult))
                    dve.sem_inc(mix_ready, 1)
                for n in range(D // COLS):
                    bank = get(("wo", n))
                    link(TTn(x[:, :, n * COLS:(n + 1) * COLS], x[:, :, n * COLS:(n + 1) * COLS],
                             bank.rearrange("p (j c) -> p j c", j=TT), ALU.add))
                    dve.sem_inc(x_mixed, 1)
                    free_(("wo", n))
                scale_x(2)
                evac_hT("h2T", "gain_ffn")
                dve.wait_ge(part_ready, 2)
                TTn(rest, xn3[:, :, :], part[0], ALU.subtract).then_inc(rest_ready, 1)
                bank = get("logits")
                link(TTn(lg[:, :, :], bank[:, 0:72].rearrange("p (j c) -> p j c", j=TT),
                         pv("router_bias", 0, 36).unsqueeze(1).to_broadcast([P, TT, 36]), ALU.add))
                free_("logits")
                link(dve.tensor_copy(rt[:, :, 0:4], lg[:, :, 0:4]))
                for j in range(TT):
                    link(dve.max(rt[:, j, 8:16], rt[:, j, 0:8]))
                    link(dve.max_index(rtx[:, 0, j, :], rt[:, j, 8:16], rt[:, j, 0:8]))
                link(dve.tensor_copy(rt[:, :, 30:31], rtx[:, 0, :, 0:1]))
                link(TTn(rt[:, :, 20:24], rt[:, :, 0:4], rt[:, :, 8:9].to_broadcast([P, TT, 4]), ALU.subtract))
                dve.sem_inc(route_in, 1)
                link(TTn(rt[:, :, 16:20], iota[:, 0:4].unsqueeze(1).to_broadcast([P, TT, 4]),
                         rt[:, :, 30:31].to_broadcast([P, TT, 4]), ALU.is_equal))
                el = lg[:, :, 4:36].rearrange("p j (g e) -> p j e g", g=GROUPS)
                prod = pick[:, 3, :, :].rearrange("p j (e g) -> p j e g", g=GROUPS)
                link(TTn(prod, el, rt[:, :, 16:20].unsqueeze(2).to_broadcast([P, TT, PER_GROUP, GROUPS]), ALU.mult))
                link(dve.tensor_reduce(rt[:, :, 32:40], prod, AX_X, ALU.add))
                for j in range(TT):
                    link(dve.max(rt[:, j, 40:48], rt[:, j, 32:40]))
                    link(dve.max_index(rtx[:, 1, j, :], rt[:, j, 40:48], rt[:, j, 32:40]))
                link(dve.tensor_copy(rt[:, :, 48:50], rtx[:, 1, :, 0:2]))
                link(TTn(rt[:, :, 59:60], rt[:, :, 41:42], rt[:, :, 40:41], ALU.subtract))
                dve.sem_inc(route_in, 1)
                link(dve.tensor_scalar(rt[:, :, 31:32], rt[:, :, 30:31], float(PER_GROUP), None, ALU.mult))
                link(TTn(rt[:, :, 48:50], rt[:, :, 48:50], rt[:, :, 31:32].to_broadcast([P, TT, 2]), ALU.add))
                dve.wait_ge(route_exp, 1)
                link(dve.tensor_reduce(rt[:, :, 28:29], rt[:, :, 24:28], AX_X, ALU.add))
                link(dve.reciprocal(rt[:, :, 29:30], rt[:, :, 28:29]))
                dve.wait_ge(route_exp, 2)
                link(dve.tensor_scalar(rt[:, :, 61:62], rt[:, :, 60:61], 1.0, None, ALU.add))
                link(dve.reciprocal(rt[:, :, 62:63], rt[:, :, 61:62]))
                link(TTn(rt[:, :, 52:53], rt[:, :, 62:63], rt[:, :, 29:30], ALU.mult))
                link(TTn(rt[:, :, 53:54], rt[:, :, 52:53], rt[:, :, 60:61], ALU.mult))
                io32 = iota[:, 0:32].unsqueeze(1).to_broadcast([P, TT, EXPERTS])

                def over(col):
                    return rt[:, :, col:col + 1].to_broadcast([P, TT, EXPERTS])

                link(TTn(pick[:, 2, :, :], io32, over(48), ALU.is_equal))
                link(TTn(pick[:, 3, :, :], io32, over(49), ALU.is_equal))
                link(TTn(pick[:, 0, :, :], pick[:, 2, :, :], pick[:, 3, :, :], ALU.add))
                dve.sem_inc(mask_ready, 1)
                link(TTn(pick[:, 1, :, :], pick[:, 2, :, :], over(52), ALU.mult))
                link(TTn(pick[:, 3, :, :], pick[:, 3, :, :], over(53), ALU.mult))
                link(TTn(sel[:, 1, :, 0:EXPERTS], pick[:, 1, :, :], pick[:, 3, :, :], ALU.add))
                dve.wait_ge(part_ready, 3)
                TTn(part[2], rest, part[1], ALU.subtract).then_inc(rest_ready, 1)
                bank = get("rank")
                rk = pick[:, 2, :, :].rearrange("p j e -> p (j e)")
                link(dve.scalar_tensor_tensor(out=rk, in0=bank[:, 0:64], scalar=1.0,
                                              in1=pick[:, 0, :, :].rearrange("p j e -> p (j e)"), op0=ALU.add, op1=ALU.mult))
                link(dve.tensor_scalar(sel[:, 0, :, 0:EXPERTS], pick[:, 2, :, :], -1.0, None, ALU.add))
                link(dve.tensor_reduce(nround_f[:, 0:QUADS], bank[:, 64:96].rearrange("p (q e) -> p q e", e=4), AX_X, ALU.max))
                free_("rank")
                over_q = pick[:, 3, :, :].rearrange("p j e -> p (j e)").rearrange("p (q k) -> p q k", q=QUADS)
                link(TTn(over_q, iota[:, COUNT:COUNT + 8].unsqueeze(1).to_broadcast([P, QUADS, 8]),
                         nround_f[:, 0:QUADS].unsqueeze(2).to_broadcast([P, QUADS, 8]), ALU.is_lt))
                link(dve.tensor_reduce(nround_f[:, QUADS:2 * QUADS], over_q, AX_X, ALU.add))
                link(dve.tensor_scalar(nround[:, :], nround_f[:, QUADS:2 * QUADS], 1.0, None, ALU.max))
                dve.sem_inc(routed, 1)
                gq = pv("gain_ffn", 0, KD)

                def select(q4, ids, n):
                    for j in range(TT):
                        rkq = sel[:, 0, j, q4].unsqueeze(2).to_broadcast([P, 4, CAP])
                        ins = TTn(Psel[:, j, :].rearrange("p (e s) -> p e s", e=4), ids.unsqueeze(1).to_broadcast([P, 4, CAP]),
                                  rkq, ALU.is_equal)
                    ins.then_inc(psel_ready, 1)
                    dve.wait_ge(psel_ready, n * 2 + 1)
                    for j in range(TT):
                        wq = sel[:, 1, j, q4].unsqueeze(2).to_broadcast([P, 4, CAP])
                        ins = TTn(Pwt[:, j, :].rearrange("p (e s) -> p e s", e=4),
                                  Psel[:, j, :].rearrange("p (e s) -> p e s", e=4), wq, ALU.mult)
                    ins.then_inc(psel_ready, 1)

                def selected(n):
                    for half in range(2):
                        dve.wait_ge(gath_full, n * 2 + half + 1)
                        TTn(hq[:, half * 4:half * 4 + 4, :], ps[:, 4 + 3 * half, :].rearrange("p (k s) -> p k s", k=4),
                            gq[:, half * 4:half * 4 + 4].unsqueeze(2).to_broadcast([P, 4, P]), ALU.mult).then_inc(hq_ready, 1)

                n0 = rounds_done(dve, rounds) + l
                select(slice(0, 4), iota[:, 0:CAP], n0)
                selected(n0)
                with dve.Fori(0, QUADS) as q:
                    dve.reg_load(nreg, nround[0:1, bass.ds(q, 1)])
                    nv = dve.snap(nreg, min_val=1, max_val=MAXROUND)
                    with dve.Fori(0, nv) as r:
                        n = rounds_done(dve, rounds)
                        dve.wait_ge(pwt_full, n + 1)
                        with dve.If(r < nv - 1):
                            select(bass.ds(q * 4, 4), iota[:, bass.ds(r * CAP + CAP, CAP)], n + l + 1)
                        with dve.Else():
                            select(bass.ds(q * 4 + 4, 4), iota[:, 0:CAP], n + l + 1)
                        dve.wait_ge(sg_ready, n + 1)
                        dve.wait_ge(up_full, n + 1)
                        TTn(hmid, sg, ps[:, 6, 0:DE], ALU.mult).then_inc(hmid_ready, 1)
                        selected(n + l + 1)
                        dve.wait_ge(y_full, n * 2 + 2)
                        dve.tensor_copy(ysb[:, 1, :], ps[:, 6, :]).then_inc(y1_ready, 1)
                        dve.reg_add(rounds, rounds, 1)
                end_of_layer(dve, l)
            chain[0] = 0
            dve.wait_ge(rstd_ready, 1)
            dve.wait_ge(gfin_in, 16)
            for j in range(TT):
                link(dve.scalar_tensor_tensor(out=fin[:, j, :], in0=x[:, j, :], scalar=ss[:, 4 + j:5 + j], in1=gfin,
                                              op0=ALU.mult, op1=ALU.mult))
            dve.sem_inc(out_ready, 1)



def kernel(**inputs):
    import numpy as np
    import concourse.bacc as bacc
    from concourse.bass_utils import run_bass_kernel_spmd

    g = {k: np.ascontiguousarray(v) for k, v in inputs.items()}

    i = np.arange(P)
    row, col = i[:, None], i[None, :]
    tiles = {
        "ident": row == col, "cum": row <= col, "ncum": -1.0 * (row <= col), "nsuffix": -1.0 * (row > col),
        "before": row < col, "ones": np.ones((P, P)), "nones": -np.ones((P, P)), "headsum": row // HD == col // HD,
        "swap": 1.0 * ((row == col - HD // 2) & (col % HD >= HD // 2)) - 1.0 * ((row == col + HD // 2) & (col % HD < HD // 2)),
    }
    maskc = np.concatenate([np.where(row <= col, 0.0, NEG), np.zeros((P, P))], 1)
    d0 = np.where(row <= col, col - row, -NEG)
    dist = np.concatenate([d0, col + P - row, d0], 1)
    inv_freq = (np.float32(10000.0) ** (-np.arange(0, HD, 2, dtype=np.float32) / np.float32(HD))).astype(np.float32)
    ang = np.arange(T, dtype=np.float32)[None, :] * inv_freq[i % (HD // 2)][:, None]
    count = np.concatenate([np.arange(COUNT), CAP * np.arange(8)])
    consts = np.concatenate([tiles[n].astype(np.float32) for n in CONST] + [maskc, dist, np.cos(ang), np.sin(ang),
                            np.broadcast_to(count, (P, COUNT + 8))], 1).astype(np.float32)
    level_masks = np.stack([((row // (2 * b) == col // (2 * b)) & (row // b % 2 == 0) & (col // b % 2 == 1))
                            for b in LEVELS], 1).astype(np.float32)

    w_in = g["w_in"].reshape(LAYERS, P, KD, D_IN)
    w_mix = np.zeros((LAYERS, NMIX, P, KD, COLS), np.float32)
    for s, (_, cols) in enumerate(PROJ):
        at = 0
        for a, n in cols:
            w_mix[:, s, :, :, at:at + n] = w_in[:, :, :, a:a + n]
            at += n
    w_out = g["w_out"].reshape(LAYERS, KD, P, D // COLS, COLS)
    w_mix[:, NPROJ:] = w_out.transpose(0, 3, 2, 1, 4)
    w_mix = w_mix.reshape(LAYERS, NMIX, P, SLOT)

    def rows_all(a):
        return np.broadcast_to(a[:, None, :], (LAYERS, P, a.shape[1]))

    def conv_cols(a):
        return a.reshape(LAYERS, CONV, -1, P).transpose(0, 3, 2, 1).reshape(LAYERS, P, -1)

    head_gain = np.concatenate([g["gdn_norm"], g["ret_norm"], g["mlstm_norm"]], 1).reshape(LAYERS, MIX, P).transpose(0, 2, 1)
    zeros = np.zeros((LAYERS, P, GH), np.float32)
    params = np.concatenate([
        g["norm_mix"].reshape(LAYERS, P, KD), g["norm_ffn"].reshape(LAYERS, P, KD), conv_cols(g["gdn_conv"]),
        conv_cols(g["mlstm_conv"]), head_gain, rows_all(g["gdn_a_log"]), zeros, rows_all(g["gdn_dt_bias"]),
        rows_all(g["mlstm_i_bias"]), rows_all(g["mlstm_f_bias"]), np.zeros((LAYERS, P, GROUPS), np.float32),
        rows_all(g["router_bias"])], 2)
    router_w = np.concatenate([g["router_group"], g["router_expert"]], 2).reshape(LAYERS, P, KD, GROUPS + EXPERTS)
    experts = [g[n].reshape(LAYERS, EXPERTS, P, SLOT) for n in ("expert_gate", "expert_up", "expert_down")]
    x_in = g["x"].reshape(TT, P, D).transpose(1, 0, 2)
    gain_final = np.broadcast_to(g["norm_final"][None, :], (P, D))

    nc = bacc.Bacc("TRN2", target_bir_lowering=False, num_devices=1)
    arrays, args = {}, []
    for name, a in [("x_in", x_in), ("consts", consts), ("level_masks", level_masks), ("params", params), ("w_mix", w_mix),
                    ("router_w", router_w), ("e_gate", experts[0]), ("e_up", experts[1]), ("e_down", experts[2]),
                    ("gain_final", gain_final)]:
        a = np.ascontiguousarray(a)
        arrays[name] = a
        args.append(nc.dram_tensor(name, a.shape, F32, kind="ExternalInput").ap())
    out = nc.dram_tensor("out", (T, D), F32, kind="ExternalOutput").ap()
    trunk(nc, *args, out.rearrange("(j p) d -> p j d", p=P))
    r = run_bass_kernel_spmd(nc, [arrays], core_ids=[0])
    return r.results[0]["out"].reshape(1, T, D)
```

```python
from contextlib import ExitStack
import math

import concourse.bass as bass
from concourse import mybir

F32 = mybir.dt.float32
BF16 = mybir.dt.bfloat16
U32 = mybir.dt.uint32
I32 = mybir.dt.int32
ALU = mybir.AluOpType
ACT = mybir.ActivationFunctionType
AX_X = mybir.AxisListType.X

P = 128
LAYERS = 2
D = 1024
T = 256
TT = T // P
KD = D // P
HD = 64
GH, RH, MH = 6, 4, 6
GP, RP, MP = GH // 2, RH // 2, MH // 2
MIX = GP + RP + MP
CONV = 4
GROUPS, PER_GROUP = 4, 8
EXPERTS = GROUPS * PER_GROUP
DE = D // 4
EPS = 1e-6
RING = 12
SLOT = 2048
COLS = SLOT // KD
QUADS = EXPERTS // 4
CAP = P // 4
MAXROUND = T // CAP
COUNT = T + CAP
NEG = -1e30
QK_SCALE = HD ** -0.5

GW, RW, MW = GH * HD, RH * HD, MH * HD
C_Z = 3 * GW
C_B = C_Z + GW
C_RQ = C_B + 2 * GH
C_RV = C_RQ + 2 * RW
C_RG = C_RV + RW
C_MQ = C_RG + RW
C_MV = C_MQ + 2 * MW
C_MO = C_MV + MW
C_I = C_MO + MW
D_IN = C_I + 2 * MH
NG = 2 * GH + 2 * MH
PROJ = [("gates", [(C_B, 2 * GH), (C_I, 2 * MH)])]
PROJ += [(("gdn", s), [(COLS * s, min(COLS, 3 * GW - COLS * s))]) for s in range(5)]
PROJ += [(("gate", 0), [(C_Z, COLS)]), (("gate", 1), [(C_Z + COLS, P)]), (("gate", 2), [(C_RG, RW)]),
         (("gate", 3), [(C_MO, COLS)]), (("gate", 4), [(C_MO + COLS, P)])]
PROJ += [(("rqk", 0), [(C_RQ, COLS)]), (("rqk", 1), [(C_RQ + RW, COLS)])]
PROJ += [(("mqk", s), [(C_MQ + COLS * s, COLS)]) for s in range(3)]
PROJ += [(("rv", 0), [(C_RV, RW)])]
PROJ += [(("mv", s), [(C_MV + P * s, P)]) for s in range(3)]
GATE_TILES = [(0, 1), (2,), (3, 4), (5, 6), (7,)]
SLOT_OF = {name: i for i, (name, _) in enumerate(PROJ)}
WIDTH = {name: sum(n for _, n in cols) for name, cols in PROJ}
NPROJ = len(PROJ)
NMIX = NPROJ + D // COLS
assert NMIX % RING == 0 and D_IN == 4120

CONST = ["ident", "cum", "ncum", "nsuffix", "before", "ones", "nones", "headsum", "swap"]
LEVELS = [2 ** i for i in range(7)]

PAR = {}
_at = 0
for _name, _n in [("gain_mix", KD), ("gain_ffn", KD), ("conv_g", 9 * CONV), ("conv_m", 6 * CONV),
                  ("head_gain", MIX), ("a_log", GH), ("bias3", 2 * GH + 2 * MH), ("router_bias", 36)]:
    PAR[_name] = (_at, _at + _n)
    _at += _n
NPAR = _at
NCONST = len(CONST) * P + T + 384 + 2 * T + COUNT + 8
LN_EXP = "natural_log_exp_and_others"


def psum_plan():
    order = [("hT", i) for i in range(4)] + ["gates"] + [("gdn", s) for s in range(5)]
    order += ["rows", "cols", ("gate", 0), ("gate", 1), ("beta", 0), ("beta", 1)] + [("nrm", s) for s in range(3)]
    order += [("vt", p) for p in range(GP)] + [("dec", 0)]
    for h in range(GH):
        if h == 2:
            order += [("gate", 2)]
        if h % 2 == 0 and h // 2 + 1 < GP:
            order += [("dec", h // 2 + 1)]
        order += [("kq0", h), ("kq1", h)]
    order += [("gate", 3)] + [("A", g) for g in range(3)] + [("gate", 4)] + [("X", 0, g) for g in range(3)]
    for lev in range(1, 7):
        order += [("W", lev, g) for g in range(3)] + [("Z", lev, g) for g in range(3)]
        if lev < 6:
            order += [("X", lev, g) for g in range(3)]
    order += ["u1", ("rqk", 0), "t1", "u2", ("rqk", 1)] + [("o", p) for p in range(GP)] + [("on", p) for p in range(GP)]
    order += [("rsw", 0), ("rsw", 1)] + [("mqk", s) for s in range(3)] + [("rv", 0), ("mv", 0)]
    order += [("rs", h) for h in range(RH)] + [("mdec", 0), ("mv", 1), ("o", 3), ("o", 4), ("mv", 2), ("on", 3), ("on", 4)]
    order += [("ms", 0), ("ms", 1), ("em", 0), ("mdec", 1), ("ms", 2), ("ms", 3), ("em", 1), ("o", 5)]
    order += [("mdec", 2), ("ms", 4), ("ms", 5), ("em", 2), ("o", 6), ("on", 5), ("o", 7), ("on", 6), ("on", 7)]
    order += [("wo", n) for n in range(D // COLS)]
    order += [("h2T", i) for i in range(4)] + ["logits", "rank"]
    return order


def trunk(nc, x_in, consts, level_masks, params, w_mix, router_w, e_gate, e_up, e_down, gain_final, out):
    order = psum_plan()
    bank_of, uses = {}, [0] * 8
    for i, name in enumerate(order):
        b = i % 8 if name != "rank" else 4 + i % 4
        bank_of[name] = (b, uses[b])
        uses[b] += 1

    with ExitStack() as ctx:
        def sb(name, shape, dt=F32):
            return ctx.enter_context(nc.sbuf_tensor(name, shape, dt))

        def sem(name):
            return ctx.enter_context(nc.semaphore(name))

        ring = sb("ring", [P, RING, SLOT])
        x = sb("x", [P, TT, D])
        xn = sb("xn", [P, TT * D])
        hT = sb("hT", [P, KD * T])
        kqz = sb("kqz", [P, GH, 2, T])
        kf = sb("kf", [P, GP, T])
        raw = sb("raw", [P, 9 * T])
        vb = sb("vb", [P, TT, GW])
        kq = sb("kq", [P, GH * 2 * 384])
        xxt = sb("xxt", [P, 12 * T])
        shapes = sb("shapes", [P, NCONST])
        lvl = sb("lvl", [P, len(LEVELS), P], BF16)
        selin = sb("selin", [P, 3, TT, P])
        rows = sb("rows", [P, T])
        rowsraw = sb("rowsraw", [P, T])
        ebuf = sb("ebuf", [P, 2, 384])
        par = sb("par", [P, NPAR])
        par_next = sb("par_next", [P, NPAR])
        rw = sb("rw", [P, KD, 36])
        epsc = sb("epsc", [P, 1])
        ss = sb("ss", [P, 8])
        gz = sb("gz", [P, TT, 24])
        sp = sb("sp", [P, 4, TT, 18])
        ea = sb("ea", [P, GH])
        dpos = sb("dpos", [P, TT, 12])
        beta = sb("beta", [P, TT, GH])
        colv = sb("colv", [P, 32])
        colA = sb("colA", [P, TT, MH])
        lg = sb("lg", [P, TT, 36])
        rt = sb("rt", [P, TT, 64])
        rtx = sb("rtx", [P, 2, TT, 8], U32)
        pick = sb("pick", [P, 4, TT, EXPERTS])
        sel = sb("sel", [P, 2, TT, EXPERTS + 4])
        nround_f = sb("nround_f", [P, 32 + 2 * QUADS])
        nround = sb("nround", [P, QUADS], I32)

        o = len(CONST) * P
        cst = shapes[:, 0:o].rearrange("p (a b) -> p a b", b=P)
        maskc = shapes[:, o:o + T]
        dist = shapes[:, o + T:o + T + 384]
        o += T + 384
        rot = shapes[:, o:o + 2 * T].rearrange("p (a b) -> p a b", b=T)
        iota = shapes[:, o + 2 * T:NCONST]

        def c(name):
            return cst[:, CONST.index(name), :]

        def pv(name, i=0, n=1):
            a, _ = PAR[name]
            return par[:, a + i:a + i + n]

        xn3 = xn[:, :].rearrange("p (t d) -> p t d", t=TT)
        hT3 = hT[:, :].rearrange("p (k t) -> p k t", k=KD)
        mixT = xn[:, :].rearrange("p (c t) -> p c t", c=MIX)
        raw3 = raw[:, :].rearrange("p (c t) -> p c t", c=9)
        Amat = raw[:, 0:12 * P].rearrange("p (m t) -> p m t", m=12)
        XT = xxt[:, 0:12 * P].rearrange("p (m t) -> p m t", m=12)
        X = xxt[:, 12 * P:24 * P].rearrange("p (m t) -> p m t", m=12)
        sqn = xxt[:, 0:6 * T].rearrange("p (c t) -> p c t", c=6)
        rn = xxt[:, 6 * T:12 * T].rearrange("p (c t) -> p c t", c=6)
        KQ = kq[:, :].rearrange("p (h a t) -> p h a t", h=GH, a=2)
        betab = kq[:, 5 * 768:6 * 768].rearrange("p (c t) -> p c t", c=3)
        HAL = T + 4
        cin_g = xn[:, 0:3 * HAL].rearrange("p (b t) -> p b t", b=3)
        acc_g = xn[:, 3 * HAL:3 * HAL + 4 * T].rearrange("p (b t) -> p b t", b=4)
        cin_m = raw[:, 0:3 * HAL].rearrange("p (b t) -> p b t", b=3)
        acc_m = raw[:, 3 * HAL:3 * HAL + 4 * T].rearrange("p (b t) -> p b t", b=4)
        vm = kq[:, 0:768].rearrange("p (t c) -> p t c", t=TT)
        vr = kq[:, 768:1280].rearrange("p (t c) -> p t c", t=TT)
        rkf = kq[:, 1280:1792].rearrange("p (c t) -> p c t", c=RP)
        rprob = [kq[:, 1792 + 384 * h:2176 + 384 * h] for h in range(2)]
        rprob += [xxt[:, 2304 + 384 * h:2688 + 384 * h] for h in range(2)]
        mprob = xxt[:, 0:MH * 384].rearrange("p (h t) -> p h t", h=MH)
        rraw = kq[:, 2560:3584].rearrange("p (a c t) -> p a c t", a=2, c=2)
        rtmp = kq[:, 3584:4096].rearrange("p (c t) -> p c t", c=2)
        rsq = kq[:, 4096:4608].rearrange("p (c t) -> p c t", c=2)
        rrr = rraw[:, 0, :, :]
        mh, mden, mem = raw3[:, 0:3, :], raw3[:, 3:6, :], raw3[:, 6:9, :]
        msq, mrr = hT3[:, 0:3, :], hT3[:, 3:6, :]
        hq = hT[:, 0:1024].rearrange("p (k s) -> p k s", k=KD)
        ysb = hT[:, 1024:2048].rearrange("p (n s) -> p n s", n=2)
        Psel = kq[:, 0:128].bitcast(BF16).rearrange("p (t s) -> p t s", t=TT)
        Pwt = kq[:, 128:384].rearrange("p (t s) -> p t s", t=TT)
        PwT = kq[:, 384:640]
        sg = kq[:, 640:896]
        hmid = kq[:, 896:1152]
        hmT = kq[:, 1152:1408].rearrange("p (f s) -> p f s", f=2)
        part = [kq[:, 1408 + 1024 * i:1408 + 1024 * (i + 1)].bitcast(BF16).rearrange("p (t d) -> p t d", t=TT) for i in range(3)]
        rest = xxt[:, 0:TT * D].rearrange("p (t d) -> p t d", t=TT)
        gfin = kq[:, 0:D]
        fin = kqz[:, :, :, :].rearrange("p h a t -> p (h a t)")[:, 0:TT * D].rearrange("p (t d) -> p t d", t=TT)
        junk = hT[:, 0:1024]

        ps = ctx.enter_context(nc.psum_tensor("ps", [P, 8, 512], F32))

        first = sem("layer_first")
        full = [sem(f"bank_full{b}") for b in range(8)]
        free = [sem(f"bank_free{b}") for b in range(8)]
        dve_chain = sem("dve_chain")
        act_chain = sem("act_chain")
        rstd_ready = sem("rstd_ready")
        sumsq_go = sem("sumsq_go")
        xn_ready = sem("xn_ready")
        hT_ready = sem("hT_ready")
        gates_z = sem("gates_z")
        gates_e = sem("gates_e")
        gates_col = sem("gates_col")
        selin_ready = sem("selin_ready")
        rows_ready = sem("rows_ready")
        cin_ready = sem("cin_ready")
        cin_used = sem("cin_used")
        conv_ready = sem("conv_ready")
        conv_m_go = sem("conv_m_go")
        raw_ready = sem("raw_ready")
        sq_ready = sem("sq_ready")
        rn_ready = sem("rn_ready")
        beta_ready = sem("beta_ready")
        kq_in_ready = sem("kq_in_ready")
        earg_ready = sem("earg_ready")
        e_ready = sem("e_ready")
        kq_ready = sem("kq_ready")
        vb_ready = sem("vb_ready")
        a_ready = sem("a_ready")
        xt_ready = sem("xt_ready")
        x_ready = sem("x_ready")
        w_ready = sem("w_ready")
        u_ready = sem("u_ready")
        t1_ready = sem("t1_ready")
        o_sq_ready = sem("o_sq_ready")
        o_sq_in = sem("o_sq_in")
        o_rr_ready = sem("o_rr_ready")
        rraw_ready = sem("rraw_ready")
        rq_ready = sem("rq_ready")
        val_ready = sem("val_ready")
        mq_ready = sem("mq_ready")
        gate_ready = sem("gate_ready")
        rdec_ready = sem("rdec_ready")
        p_ready = sem("p_ready")
        em_ready = sem("em_ready")
        mix_ready = sem("mix_ready")
        x_mixed = sem("x_mixed")
        route_in = sem("route_in")
        route_exp = sem("route_exp")
        mask_ready = sem("mask_ready")
        part_ready = sem("part_ready")
        rest_ready = sem("rest_ready")
        acc_init = sem("acc_init")
        acc_last = sem("acc_last")
        x_out = sem("x_out")
        last = sem("layer_last")
        const_in = sem("const_in")
        x_loaded = sem("x_loaded")
        init_done = sem("init_done")
        par_in = sem("par_in")
        rw_in = sem("rw_in")
        lvl_in = sem("lvl_in")
        par_ready = sem("par_ready")
        routed = sem("routed")
        logits_read = sem("logits_read")
        layer_end = sem("layer_end")
        layer_go = sem("layer_go")
        arrived = [sem(f"slot_arrived{s}") for s in range(RING)]
        slots_free = sem("slots_free")
        psel_ready = sem("psel_ready")
        gath_full = sem("gath_full")
        hq_ready = sem("hq_ready")
        pwt_full = sem("pwt_full")
        pwt_ready = sem("pwt_ready")
        gate_full = sem("gate_full")
        sg_ready = sem("sg_ready")
        up_full = sem("up_full")
        hmid_ready = sem("hmid_ready")
        hmt_full = sem("hmt_full")
        hmt_ready = sem("hmt_ready")
        y_full = sem("y_full")
        y0_ready = sem("y0_ready")
        y1_ready = sem("y1_ready")
        gfin_in = sem("gfin_in")
        out_ready = sem("out_ready")
        out_done = sem("out_done")
        per_layer = range(first.num, last.num + 1)

        def rounds_done(eng, rounds):
            return eng.snap(rounds, min_val=0, max_val=MAXROUND * QUADS * LAYERS)

        def end_of_layer(eng, l):
            eng.sem_inc(layer_end, 1)
            eng.wait_ge(layer_go, l + 1)

        block = ctx.enter_context(nc.Block())

        @block.sync
        def _(sync):
            def load_quad(l, q, base):
                for m, src in enumerate((e_gate, e_up, e_down)):
                    for e in range(4):
                        i = 4 * m + e
                        sync.wait_ge(slots_free, base + i + 1)
                        sync.dma_start(ring[:, i, :], src[l, q * 4 + e]).then_inc(arrived[i], 16)

            sync.dma_start(x[:, :, :], x_in).then_inc(x_loaded, 16)
            sync.dma_start(shapes[:, :], consts).then_inc(const_in, 16)
            with sync.Fori(0, LAYERS) as l:
                start = l * (NMIX + QUADS * RING)
                for i in range(NMIX):
                    s = i % RING
                    n = WIDTH[PROJ[i][0]] if i < NPROJ else COLS
                    sync.wait_ge(slots_free, start + i + 1)
                    dst = ring[:, s, :].rearrange("p (k c) -> p k c", k=KD)
                    src = w_mix[l, i].rearrange("p (k c) -> p k c", k=KD)
                    if n == COLS:
                        dst, src = ring[:, s, :], w_mix[l, i]
                    else:
                        dst, src = dst[:, :, 0:n], src[:, :, 0:n]
                    sync.dma_start(dst, src).then_inc(arrived[s], 16)
                with sync.Fori(0, QUADS) as q:
                    load_quad(l, q, start + NMIX + q * RING)
                sync.sem_inc(layer_end, 1)
            sync.wait_ge(out_ready, 1)
            sync.dma_start(out, fin).then_inc(out_done, 16)
            sync.wait_ge(out_done, 16)

        @block.gpsimd
        def _(pool):
            pool.dma_start(par_next[:, :], params[0]).then_inc(par_in, 16)
            pool.dma_start(rw[:, :, :], router_w[0]).then_inc(rw_in, 16)
            pool.dma_start(lvl[:, :, :], level_masks).then_inc(lvl_in, 16)
            pool.memset(epsc[:, :], EPS).then_inc(init_done, 1)
            pool.memset(selin[:, :, :, :], 0.0).then_inc(init_done, 1)
            pool.memset(rows[:, :], 0.0).then_inc(init_done, 1)
            pool.memset(rt[:, :, :], -3e38).then_inc(init_done, 1)
            pool.memset(kqz[:, :, :, :], 0.0).then_inc(init_done, 1)
            pool.memset(sel[:, :, :, :], -1.0).then_inc(init_done, 1)
            with pool.Fori(0, LAYERS) as l:
                pool.wait_ge(par_ready, l + 1)
                pool.sem_inc(first, 1)
                pool.dma_start(par_next[:, :], params[l + 1]).then_inc(par_in, 16)
                pool.wait_ge(logits_read, l + 1)
                pool.sem_inc(first, 1)
                pool.dma_start(rw[:, :, :], router_w[l + 1]).then_inc(rw_in, 16)
                pool.wait_ge(layer_end, l * 4 + 4)
                pool.sem_inc(first, 1)
                pool.sem_clear(per_layer)
                pool.sem_inc(layer_go, 1)
            pool.dma_start(gfin, gain_final).then_inc(gfin_in, 16)
            pool.wait_ge(gfin_in, 16)

        @block.tensor
        def _(pe):
            rounds = pe.alloc_register("pe_rounds")
            pe.reg_mov(rounds, 0)
            nreg = pe.alloc_register("pe_nround")

            def begin(name):
                b, n = bank_of[name]
                if n:
                    pe.wait_ge(free[b], n)
                return ps[:, b, :]

            def done(ins, name):
                ins.then_inc(full[bank_of[name][0]], 1)

            def have_slot(start_lap, i):
                pe.wait_ge(arrived[i % RING], (start_lap + i // RING) * 16 + 16)

            def slot_w(i):
                return ring[:, i % RING, :].rearrange("p (k c) -> p k c", k=KD)

            held = []

            def release():
                if held:
                    b, n = bank_of[held.pop()]
                    pe.wait_ge(full[b], n + 1)
                    pe.sem_inc(slots_free, 1)

            def project_cm(name, start_lap):
                i = SLOT_OF[name]
                bank = begin(name)
                have_slot(start_lap, i)
                w = slot_w(i)
                for ct in range(WIDTH[name] // P):
                    for k in range(KD):
                        mm = pe.matmul(bank[:, ct * T:(ct + 1) * T], w[:, k, ct * P:(ct + 1) * P], hT3[:, k, :],
                                       start=(k == 0), stop=(k == KD - 1))
                done(mm, name)
                release()
                held.append(name)

            def project_tm(name, start_lap):
                i = SLOT_OF[name]
                n = WIDTH[name]
                bank = begin(name)
                have_slot(start_lap, i)
                w = slot_w(i)
                for j in range(TT):
                    for k in range(KD):
                        mm = pe.matmul(bank[:, j * n:(j + 1) * n], hT3[:, k, j * P:(j + 1) * P], w[:, k, 0:n],
                                       start=(k == 0), stop=(k == KD - 1))
                done(mm, name)
                release()
                held.append(name)

            def transpose_x(kind, xn_count):
                for i in range(4):
                    j, half = i // 2, i % 2
                    bank = begin((kind, i))
                    if half == 0:
                        pe.wait_ge(xn_ready, xn_count + j + 1)
                    for kk in range(4):
                        k = half * 4 + kk
                        mm = pe.transpose(bank[:, kk * P:(kk + 1) * P], xn3[:, j, k:D:KD], c("ident"))
                    done(mm, (kind, i))

            pe.sem_inc(slots_free, RING)
            pe.wait_ge(const_in, 16)
            pe.wait_ge(x_loaded, 16)
            with pe.Fori(0, LAYERS) as l:
                lap = l * (NMIX // RING + QUADS)
                transpose_x("hT", 0)
                pe.wait_ge(init_done, 6)
                pe.wait_ge(hT_ready, 4)
                project_tm("gates", lap)
                for s in range(5):
                    project_cm(("gdn", s), lap)

                pe.wait_ge(selin_ready, 1)
                bank = begin("rows")
                for j in range(TT):
                    o_ = bank[:, j * P:(j + 1) * P]
                    pe.matmul(o_, selin[:, 0, j, :], c("ncum"), start=True, stop=False)
                    pe.matmul(o_, selin[:, 1, j, :], c("ident"), start=False, stop=False)
                    pe.matmul(o_, selin[:, 2, j, :], c("cum"), start=False, stop=(j == 0))
                    if j:
                        pe.matmul(o_, selin[:, 2, 0, :], c("ones"), start=False, stop=True)
                for j in range(TT):
                    o_ = bank[64:64 + MH, T + j * P:T + (j + 1) * P]
                    mm = pe.matmul(o_, dpos[:, j, GH:GH + MH], c("ncum"), start=True, stop=(j == 0))
                    if j:
                        mm = pe.matmul(o_, dpos[:, 0, GH:GH + MH], c("nones"), start=False, stop=True)
                done(mm, "rows")
                release()
                bank = begin("cols")
                pe.matmul(bank[:, 0:12], c("cum"), dpos[:, 0, :], start=True, stop=True)
                pe.matmul(bank[:, 12:24], c("cum"), dpos[:, 1, :], start=True, stop=False)
                pe.matmul(bank[:, 18:24], c("ones"), dpos[:, 0, GH:GH + MH], start=False, stop=True)
                mm = pe.matmul(bank[:, 24:24 + GH], c("nsuffix"), dpos[:, 0, 0:GH], start=True, stop=True)
                done(mm, "cols")
                project_cm(("gate", 0), lap)
                project_cm(("gate", 1), lap)
                pe.wait_ge(rows_ready, 1)
                for p in range(GP):
                    if p % 2 == 0:
                        bank = begin(("beta", p // 2))
                    for a in range(2):
                        r = GH + 2 * p + a
                        mm = pe.matmul(bank[64 * a:64 * a + 64, (p % 2) * T:(p % 2) * T + T],
                                       cst[:, 0, r:r + 1].to_broadcast([P, 64]), rows[:, :], start=True, stop=True)
                    if p % 2 or p == GP - 1:
                        done(mm, ("beta", p // 2))
                for s in range(3):
                    bank = begin(("nrm", s))
                    pe.wait_ge(sq_ready, s + 1)
                    mm = pe.matmul(bank[:, :], c("headsum"), sqn[:, 2 * s:2 * s + 2, :], start=True, stop=True)
                    done(mm, ("nrm", s))
                def decay_rows(i):
                    bank = begin(("dec", i))
                    for a in range(2):
                        r = 2 * i + a
                        mm = pe.matmul(bank[:, a * T:(a + 1) * T], cst[:, 0, r:r + 1].to_broadcast([P, P]), rows[:, :],
                                       start=True, stop=True)
                    done(mm, ("dec", i))

                pe.wait_ge(raw_ready, 9)
                for p in range(GP):
                    bank = begin(("vt", p))
                    for j in range(TT):
                        mm = pe.transpose(bank[:, j * P:(j + 1) * P], raw3[:, 6 + p, j * P:(j + 1) * P], c("ident"))
                    done(mm, ("vt", p))
                decay_rows(0)
                for h in range(GH):
                    if h == 2:
                        project_cm(("gate", 2), lap)
                    if h % 2 == 0 and h // 2 + 1 < GP:
                        decay_rows(h // 2 + 1)
                    pe.wait_ge(kq_in_ready, h // 2 + 1)
                    bank = begin(("kq0", h))
                    done(pe.matmul(bank[:, :], kf[:, h // 2, 0:P], kqz[:, h, :, :], start=True, stop=True), ("kq0", h))
                    bank = begin(("kq1", h))
                    done(pe.matmul(bank[:, 0:T], kf[:, h // 2, P:T], kqz[:, h, :, P:T], start=True, stop=True), ("kq1", h))
                project_cm(("gate", 3), lap)
                for g in range(3):
                    bank = begin(("A", g))
                    pe.wait_ge(kq_ready, 2 * g + 2)
                    for m in range(4):
                        h, j = 2 * g + m // 2, m % 2
                        mm = pe.transpose(bank[:, m * P:(m + 1) * P], KQ[:, h, 0, 256 * j:256 * j + P], c("ident"))
                    done(mm, ("A", g))
                project_cm(("gate", 4), lap)
                for g in range(3):
                    bank = begin(("X", 0, g))
                    pe.wait_ge(xt_ready, g + 1)
                    for m in range(4):
                        mm = pe.transpose(bank[:, m * P:(m + 1) * P], XT[:, 4 * g + m, :], c("ident"))
                    done(mm, ("X", 0, g))
                for lev in range(1, 7):
                    for g in range(3):
                        bank = begin(("W", lev, g))
                        pe.wait_ge(a_ready, g + 1)
                        pe.wait_ge(xt_ready, 3 * lev + g - 2)
                        for m in range(4):
                            mm = pe.matmul(bank[:, m * P:(m + 1) * P], Amat[:, 4 * g + m, :], XT[:, 4 * g + m, :],
                                           start=True, stop=True)
                        done(mm, ("W", lev, g))
                    for g in range(3):
                        bank = begin(("Z", lev, g))
                        pe.wait_ge(w_ready, 3 * (lev - 1) + g + 1)
                        pe.wait_ge(x_ready, 3 * (lev - 1) + g + 1)
                        for m in range(4):
                            h, j = 2 * g + m // 2, m % 2
                            mm = pe.matmul(bank[:, m * P:(m + 1) * P], X[:, 4 * g + m, :], KQ[:, h, 0, 256 * j:256 * j + P],
                                           start=True, stop=True)
                        done(mm, ("Z", lev, g))
                    if lev < 6:
                        for g in range(3):
                            bank = begin(("X", lev, g))
                            pe.wait_ge(xt_ready, 3 * lev + g + 1)
                            for m in range(4):
                                mm = pe.transpose(bank[:, m * P:(m + 1) * P], XT[:, 4 * g + m, :], c("ident"))
                            done(mm, ("X", lev, g))
                bank = begin("u1")
                pe.wait_ge(xt_ready, 21)
                pe.wait_ge(vb_ready, 3)
                for h in range(GH):
                    mm = pe.matmul(bank[:, h * HD:(h + 1) * HD], XT[:, 2 * h, :], vb[:, 0, h * HD:(h + 1) * HD],
                                   start=True, stop=True)
                done(mm, "u1")
                project_cm(("rqk", 0), lap)
                bank = begin("t1")
                pe.wait_ge(u_ready, 1)
                for h in range(GH):
                    mm = pe.matmul(bank[:, h * HD:(h + 1) * HD], KQ[:, h, 0, P:2 * P], vb[:, 0, h * HD:(h + 1) * HD],
                                   start=True, stop=True)
                done(mm, "t1")
                bank = begin("u2")
                pe.wait_ge(t1_ready, 1)
                for h in range(GH):
                    mm = pe.matmul(bank[:, h * HD:(h + 1) * HD], XT[:, 2 * h + 1, :], vb[:, 1, h * HD:(h + 1) * HD],
                                   start=True, stop=True)
                done(mm, "u2")
                project_cm(("rqk", 1), lap)

                def head_out(dst, value, weights):
                    pe.matmul(dst, value[0], weights[:, 0:T], start=True, stop=False)
                    return pe.matmul(dst[:, P:T], value[1], weights[:, T:384], start=False, stop=True)

                pe.wait_ge(u_ready, 2)
                for p in range(GP):
                    bank = begin(("o", p))
                    for a in range(2):
                        h = 2 * p + a
                        v = [vb[:, j, h * HD:(h + 1) * HD] for j in range(TT)]
                        mm = head_out(bank[64 * a:64 * a + 64, 0:T], v, KQ[:, h, 1, :])
                    done(mm, ("o", p))

                def head_norm(cidx, src):
                    bank = begin(("on", cidx))
                    pe.wait_ge(o_sq_ready, cidx + 1)
                    done(pe.matmul(bank[:, 0:T], c("headsum"), src, start=True, stop=True), ("on", cidx))

                for p in range(GP):
                    head_norm(p, raw3[:, p, :])

                for a in range(2):
                    bank = begin(("rsw", a))
                    pe.wait_ge(rraw_ready, a + 1)
                    done(pe.matmul(bank[:, :], c("swap"), rraw[:, a, :, :], start=True, stop=True), ("rsw", a))
                for s in range(3):
                    project_cm(("mqk", s), lap)
                project_tm(("rv", 0), lap)
                project_tm(("mv", 0), lap)
                pe.wait_ge(rq_ready, 2)
                for h in range(RH):
                    bank = begin(("rs", h))
                    pe.matmul(bank[:, 0:T], rkf[:, h // 2, 0:P], kqz[:, h, 0, :], start=True, stop=True)
                    done(pe.matmul(bank[:, T:384], rkf[:, h // 2, P:T], kqz[:, h, 0, P:T], start=True, stop=True), ("rs", h))

                def m_decay(p):
                    bank = begin(("mdec", p))
                    for a in range(2):
                        r = 32 + 2 * p + a
                        mm = pe.matmul(bank[:, a * T:(a + 1) * T], cst[:, 0, r:r + 1].to_broadcast([P, P]), rows[:, :],
                                       start=True, stop=True)
                    done(mm, ("mdec", p))

                def m_scores(p):
                    for h in (2 * p, 2 * p + 1):
                        bank = begin(("ms", h))
                        pe.matmul(bank[:, 0:T], kf[:, p, 0:P], kqz[:, h, 1, :], start=True, stop=True)
                        done(pe.matmul(bank[:, T:384], kf[:, p, P:T], kqz[:, h, 1, P:T], start=True, stop=True), ("ms", h))
                    bank = begin(("em", p))
                    for a in range(2):
                        r = 64 + 2 * p + a
                        mm = pe.matmul(bank[64 * a:64 * a + 64, 0:T], cst[:, 0, r:r + 1].to_broadcast([P, 64]), rows[:, :],
                                       start=True, stop=True)
                    done(mm, ("em", p))

                def m_out(p):
                    bank = begin(("o", 5 + p))
                    one = [cst[:, CONST.index("ones"), 0:64]] * 2
                    for a in range(2):
                        h = 2 * p + a
                        pe.wait_ge(p_ready, RH + h + 1)
                        v = [vm[:, j, h * HD:(h + 1) * HD] for j in range(TT)]
                        head_out(bank[64 * a:64 * a + 64, 0:T], v, mprob[:, h, :])
                        mm = head_out(bank[64 * a:64 * a + 64, T:2 * T], one, mprob[:, h, :])
                    done(mm, ("o", 5 + p))

                m_decay(0)
                project_tm(("mv", 1), lap)
                for p in range(RP):
                    bank = begin(("o", 3 + p))
                    if p == 0:
                        pe.wait_ge(val_ready, 1)
                    for a in range(2):
                        h = 2 * p + a
                        pe.wait_ge(p_ready, h + 1)
                        v = [vr[:, j, h * HD:(h + 1) * HD] for j in range(TT)]
                        mm = head_out(bank[64 * a:64 * a + 64, 0:T], v, rprob[h])
                    done(mm, ("o", 3 + p))
                project_tm(("mv", 2), lap)
                release()
                for p in range(RP):
                    head_norm(3 + p, rsq[:, p, :])
                pe.wait_ge(mq_ready, 12)
                m_scores(0)
                m_decay(1)
                m_scores(1)
                pe.wait_ge(val_ready, 4)
                m_out(0)
                m_decay(2)
                m_scores(2)
                m_out(1)
                head_norm(5, msq[:, 0, :])
                m_out(2)
                head_norm(6, msq[:, 1, :])
                head_norm(7, msq[:, 2, :])
                pe.wait_ge(mix_ready, MIX)
                for n in range(D // COLS):
                    i = NPROJ + n
                    bank = begin(("wo", n))
                    have_slot(lap, i)
                    w = slot_w(i)
                    for j in range(TT):
                        for k in range(KD):
                            mm = pe.matmul(bank[:, j * COLS:(j + 1) * COLS], mixT[:, k, j * P:(j + 1) * P], w[:, k, :],
                                           start=(k == 0), stop=(k == KD - 1))
                    done(mm, ("wo", n))
                    release()
                    held.append(("wo", n))
                release()
                transpose_x("h2T", 2)
                pe.wait_ge(hT_ready, 8)
                bank = begin("logits")
                pe.wait_ge(rw_in, l * 16 + 16)
                pe.sem_inc(first, 1)
                for j in range(TT):
                    for k in range(KD):
                        mm = pe.matmul(bank[:, j * 36:(j + 1) * 36], hT3[:, k, j * P:(j + 1) * P], rw[:, k, :],
                                       start=(k == 0), stop=(k == KD - 1))
                done(mm, "logits")
                b_, n_ = bank_of["logits"]
                pe.wait_ge(full[b_], n_ + 1)
                pe.sem_inc(logits_read, 1)
                for b in range(4):
                    pe.wait_ge(free[b], uses[b])
                for j in range(TT):
                    for n in range(2):
                        mm = pe.matmul(ps[:, 2 * j + n, :], c("ident"), x[:, j, n * 512:(n + 1) * 512],
                                       start=True, stop=False, skip_group_check=True)
                mm.then_inc(acc_init, 1)
                bank = begin("rank")
                pe.wait_ge(mask_ready, 1)
                pe.matmul(bank[:, 0:32], c("before"), pick[:, 0, 0, :], start=True, stop=True)
                pe.matmul(bank[:, 32:64], c("before"), pick[:, 0, 1, :], start=True, stop=False)
                pe.matmul(bank[:, 32:64], c("ones"), pick[:, 0, 0, :], start=False, stop=True)
                pe.matmul(bank[:, 64:96], c("ones"), pick[:, 0, 0, :], start=True, stop=False)
                mm = pe.matmul(bank[:, 64:96], c("ones"), pick[:, 0, 1, :], start=False, stop=True)
                done(mm, "rank")
                for b in range(4, 8):
                    pe.wait_ge(free[b], uses[b])
                pe.wait_ge(routed, l + 1)
                pe.sem_inc(first, 1)

                def gather(n):
                    pe.wait_ge(psel_ready, n * 2 + 1)
                    for half in range(2):
                        for kk in range(4):
                            k = half * 4 + kk
                            for j in range(TT):
                                for i in range(3):
                                    mm = pe.matmul(ps[:, 4 + 3 * half, kk * P:(kk + 1) * P], part[i][:, j, k:D:KD], Psel[:, j, :],
                                                   start=(j == 0 and i == 0), stop=(j == TT - 1 and i == 2))
                        mm.then_inc(gath_full, 1)

                pe.wait_ge(part_ready, 3)
                pe.wait_ge(rest_ready, 2)
                gather(rounds_done(pe, rounds) + l)
                with pe.Fori(0, QUADS) as q:
                    pe.reg_load(nreg, nround[0:1, bass.ds(q, 1)])
                    nv = pe.snap(nreg, min_val=1, max_val=MAXROUND)
                    qlap = lap + NMIX // RING + q
                    with pe.Fori(0, nv) as r:
                        n = rounds_done(pe, rounds)
                        pe.wait_ge(hq_ready, (n + l) * 2 + 2)
                        for m in range(2):
                            for e in range(4):
                                pe.wait_ge(arrived[4 * m + e], qlap * 16 + 16)
                            for k in range(KD):
                                for e in range(4):
                                    mm = pe.matmul(ps[32 * e:32 * e + 32, 5 + m, 0:DE], hq[:, k, 32 * e:32 * e + 32],
                                                   ring[:, 4 * m + e, k * DE:(k + 1) * DE],
                                                   start=(k == 0), stop=(k == KD - 1), skip_group_check=True)
                            mm.then_inc((gate_full, up_full)[m], 1)
                            if m == 0:
                                pe.wait_ge(psel_ready, (n + l) * 2 + 2)
                                for j in range(TT):
                                    mm = pe.transpose(ps[:, 4, j * P:(j + 1) * P], Pwt[:, j, :], c("ident"))
                                mm.then_inc(pwt_full, 1)
                        pe.wait_ge(pwt_ready, n + 1)
                        gather(n + l + 1)
                        pe.wait_ge(up_full, n + 1)
                        with pe.If(r == nv - 1):
                            pe.sem_inc(slots_free, 8)
                        pe.wait_ge(hmid_ready, n + 1)
                        for f in range(2):
                            mm = pe.transpose(ps[:, 6, T + f * P:T + (f + 1) * P], hmid[:, f:DE:2], c("ident"))
                        mm.then_inc(hmt_full, 1)
                        pe.wait_ge(hmt_ready, n + 1)
                        for e in range(4):
                            pe.wait_ge(arrived[8 + e], qlap * 16 + 16)
                        for h in range(2):
                            for f in range(2):
                                for e in range(4):
                                    mm = pe.matmul(ps[32 * e:32 * e + 32, 5 + h, :], hmT[:, f, 32 * e:32 * e + 32],
                                                   ring[:, 8 + e, f * D + h * 512:f * D + (h + 1) * 512],
                                                   start=(f == 0), stop=(f == 1), skip_group_check=True)
                            mm.then_inc(y_full, 1)
                        pe.wait_ge(y_full, n * 2 + 2)
                        with pe.If(r == nv - 1):
                            pe.sem_inc(slots_free, 4)
                        for h in range(2):
                            pe.wait_ge((y0_ready, y1_ready)[h], n + 1)
                            for j in range(TT):
                                mm = pe.matmul(ps[:, 2 * j + h, :], PwT[:, j * P:(j + 1) * P], ysb[:, h, :],
                                               start=False, stop=False, skip_group_check=True)
                        pe.reg_add(rounds, rounds, 1)
                pe.drain().then_inc(acc_last, 1)
                end_of_layer(pe, l)

        @block.scalar
        def _(act):
            rounds = act.alloc_register("act_rounds")
            act.reg_mov(rounds, 0)
            nreg = act.alloc_register("act_nround")
            chain = [0]

            def link(ins):
                chain[0] += 1
                ins.then_inc(act_chain, 1)
                act.wait_ge(act_chain, chain[0])

            def get(name):
                b, n = bank_of[name]
                act.wait_ge(full[b], n + 1)
                return ps[:, b, :]

            def rstd(done_sem, count):
                for j in range(TT):
                    link(act.activation(junk, x[:, j, :], ACT.Square, accum_out=ss[:, j:j + 1]))
                link(act.activation(ss[:, 2:4], ss[:, 0:2], ACT.Ln, scale=1.0 / D, bias=epsc[:, :]))
                act.activation(ss[:, 4:6], ss[:, 2:4], ACT.Exp, scale=-0.5).then_inc(done_sem, 1)

            def conv_in(name, tiles, cin, i0):
                bank = get(name)
                for n_, _ in enumerate(tiles):
                    i = i0 + n_
                    if i >= 3:
                        act.wait_ge(cin_used, i - 2)
                    ins = act.activation(cin[:, i % 3, 3:3 + T], bank[:, n_ * T:(n_ + 1) * T], ACT.Copy)
                    link(ins)
                    act.sem_inc(cin_ready, 1)
                act.sem_inc(free[bank_of[name][0]], 1)

            def gates(s, f, scale=1.0):
                bank = get(("gate", s))
                tiles = GATE_TILES[s]
                link(act.activation(mixT[:, tiles[0]:tiles[-1] + 1, :],
                                    bank[:, 0:len(tiles) * T].rearrange("p (c t) -> p c t", t=T), f, scale=scale))
                act.sem_inc(gate_ready, 1)
                act.sem_inc(free[bank_of[("gate", s)][0]], 1)

            act.wait_ge(init_done, 1)
            act.wait_ge(x_loaded, 16)
            with act.Fori(0, LAYERS) as l:
                act.preload_act_table_set(LN_EXP)
                rstd(rstd_ready, 0)
                act.wait_ge(par_ready, l + 1)
                act.sem_inc(first, 1)
                act.activation(ea[:, :], pv("a_log", 0, GH), ACT.Exp).then_inc(gates_e, 1)
                act.wait_ge(gates_z, 1)
                link(act.activation(sp[:, 2, :, :], sp[:, 1, :, :], ACT.Exp, scale=-1.0))
                act.activation(sp[:, 3, :, :], sp[:, 2, :, :], ACT.Ln, bias=1.0).then_inc(gates_e, 1)
                act.wait_ge(gates_col, 1)
                act.activation(beta[:, :, :], sp[:, 0, :, 0:GH], ACT.Exp).then_inc(gates_e, 1)
                slots = [(0, 1), (2, 3), (4, 5), (6, 7), (8,)]
                for s, tiles in enumerate(slots):
                    conv_in(("gdn", s), tiles, cin_g, 2 * s)
                    if s:
                        for t in slots[s - 1]:
                            act.wait_ge(conv_ready, t + 1)
                            act.activation(raw3[:, t, :], acc_g[:, t % 4, :], ACT.Silu).then_inc(raw_ready, 1)
                act.wait_ge(conv_ready, 9)
                act.activation(raw3[:, 8, :], acc_g[:, 0, :], ACT.Silu).then_inc(raw_ready, 1)
                act.wait_ge(raw_ready, 9)
                for s in range(3):
                    act.activation(sqn[:, 2 * s:2 * s + 2, :], raw3[:, 2 * s:2 * s + 2, :], ACT.Square).then_inc(sq_ready, 1)
                act.wait_ge(const_in, 16)
                act.wait_ge(init_done, 6)
                gates(0, ACT.Silu)
                gates(1, ACT.Silu)
                act.preload_act_table_set(LN_EXP)
                for p in range(GP):
                    bank = get(("beta", p // 2))
                    ins = act.activation(betab[:, p, :], bank[:, (p % 2) * T:(p % 2) * T + T], ACT.Exp)
                    link(ins)
                    act.sem_inc(beta_ready, 1)
                    if p % 2 or p == GP - 1:
                        act.sem_inc(free[bank_of[("beta", p // 2)][0]], 1)
                for s in range(3):
                    bank = get(("nrm", s))
                    ins = act.activation(rn[:, 2 * s:2 * s + 2, :], bank[:, :], ACT.Ln, bias=epsc[:, :])
                    link(ins)
                    act.sem_inc(free[bank_of[("nrm", s)][0]], 1)
                    act.activation(rn[:, 2 * s:2 * s + 2, :], rn[:, 2 * s:2 * s + 2, :], ACT.Exp, scale=-0.5).then_inc(rn_ready, 1)
                for h in range(GH):
                    act.wait_ge(earg_ready, h + 1)
                    act.activation(ebuf[:, h % 2, :], ebuf[:, h % 2, :], ACT.Exp).then_inc(e_ready, 1)
                    if h == 3:
                        gates(2, ACT.Copy)
                act.wait_ge(kq_ready, GH)
                for g in range(3):
                    bank = get(("A", g))
                    link(act.activation(Amat[:, 4 * g:4 * g + 4, :], bank[:, :], ACT.Copy))
                    act.sem_inc(a_ready, 1)
                    act.sem_inc(free[bank_of[("A", g)][0]], 1)
                gates(3, ACT.Tanh, 0.5)
                gates(4, ACT.Tanh, 0.5)
                for lev in range(6):
                    for g in range(3):
                        bank = get(("X", lev, g))
                        link(act.activation(X[:, 4 * g:4 * g + 4, :], bank[:, :], ACT.Copy))
                        act.sem_inc(x_ready, 1)
                        act.sem_inc(free[bank_of[("X", lev, g)][0]], 1)
                    if lev == 0:
                        act.activation(mixT[:, 3:5, :], mixT[:, 3:5, :], ACT.Silu).then_inc(gate_ready, 1)
                act.preload_act_table_set(LN_EXP)
                for i, name in enumerate(("u1", "u2")):
                    bank = get(name)
                    link(act.activation(vb[:, i, :], bank[:, 0:GW], ACT.Copy))
                    act.sem_inc(u_ready, 1)
                    act.sem_inc(free[bank_of[name][0]], 1)

                def out_rr(cidx, dst):
                    bank = get(("on", cidx))
                    link(act.activation(dst, bank[:, 0:T], ACT.Ln, scale=1.0 / HD, bias=epsc[:, :]))
                    act.sem_inc(free[bank_of[("on", cidx)][0]], 1)
                    act.activation(dst, dst, ACT.Exp, scale=-0.5).then_inc(o_rr_ready, 1)

                for p in range(GP):
                    bank = get(("o", p))
                    act.activation(raw3[:, p, :], bank[:, 0:T], ACT.Square).then_inc(o_sq_ready, 1)
                for a in range(2):
                    bank = get(("rqk", a))
                    link(act.activation(rraw[:, a, :, :], bank[:, :], ACT.Copy))
                    act.sem_inc(rraw_ready, 1)
                    act.sem_inc(free[bank_of[("rqk", a)][0]], 1)
                for p in range(GP):
                    out_rr(p, raw3[:, 3 + p, :])
                for h in range(RH):
                    lgam = math.log(1.0 - 2.0 ** (-5.0 - h))
                    act.activation(rprob[h], dist[:, :], ACT.Exp, scale=lgam).then_inc(rdec_ready, 1)

                def mlstm_silu(t):
                    act.wait_ge(conv_ready, 9 + t + 1)
                    src = acc_m[:, t % 4, :]
                    if t < MP:
                        for a in range(2):
                            act.activation(kqz[64 * a:64 * a + 64, 2 * t + a, 1, :], src[64 * a:64 * a + 64, :],
                                           ACT.Silu).then_inc(mq_ready, 1)
                    else:
                        act.activation(kf[:, t - MP, :], src, ACT.Silu).then_inc(mq_ready, 2)

                act.wait_ge(conv_m_go, 1)
                for s in range(3):
                    conv_in(("mqk", s), (0, 1), cin_m, 9 + 2 * s)
                    if s:
                        mlstm_silu(2 * s - 2)
                        mlstm_silu(2 * s - 1)
                mlstm_silu(4)
                mlstm_silu(5)
                act.preload_act_table_set(LN_EXP)

                def values(name, dst):
                    bank = get(name)
                    n = WIDTH[name]
                    link(act.activation(dst, bank[:, 0:TT * n].rearrange("p (j c) -> p j c", j=TT), ACT.Copy))
                    act.sem_inc(val_ready, 1)
                    act.sem_inc(free[bank_of[name][0]], 1)

                def m_weights(p):
                    for h in (2 * p, 2 * p + 1):
                        act.wait_ge(earg_ready, GH + h + 1)
                        act.activation(mprob[:, h, :], mprob[:, h, :], ACT.Exp).then_inc(e_ready, 1)

                def m_floor(p):
                    bank = get(("em", p))
                    link(act.activation(mem[:, p, :], bank[:, 0:T], ACT.Exp, scale=-1.0))
                    act.sem_inc(free[bank_of[("em", p)][0]], 1)

                def m_abs(p):
                    bank = get(("o", 5 + p))
                    act.activation(mden[:, p, :], bank[:, T:2 * T], ACT.Abs).then_inc(em_ready, 1)

                def m_square(p):
                    act.wait_ge(o_sq_in, p + 1)
                    act.activation(msq[:, p, :], mh[:, p, :], ACT.Square).then_inc(o_sq_ready, 1)

                values(("rv", 0), vr[:, :, :])
                values(("mv", 0), vm[:, :, 0:P])
                values(("mv", 1), vm[:, :, P:2 * P])
                m_weights(0)
                act.wait_ge(rq_ready, 2)
                for p in range(RP):
                    bank = get(("o", 3 + p))
                    act.activation(rsq[:, p, :], bank[:, 0:T], ACT.Square).then_inc(o_sq_ready, 1)
                values(("mv", 2), vm[:, :, 2 * P:3 * P])
                for p in range(RP):
                    out_rr(3 + p, rrr[:, p, :])
                m_floor(0)
                m_weights(1)
                m_floor(1)
                m_abs(0)
                m_weights(2)
                m_floor(2)
                m_square(0)
                m_abs(1)
                out_rr(5, mrr[:, 0, :])
                m_square(1)
                m_abs(2)
                out_rr(6, mrr[:, 1, :])
                m_square(2)
                out_rr(7, mrr[:, 2, :])
                act.wait_ge(x_mixed, 4)
                rstd(rstd_ready, 1)
                for j in range(TT):
                    act.wait_ge(xn_ready, 3 + j)
                    act.activation(part[0][:, j, :], xn3[:, j, :], ACT.Copy).then_inc(part_ready, 1)
                act.wait_ge(rest_ready, 1)
                act.activation(part[1], rest, ACT.Copy).then_inc(part_ready, 1)
                act.wait_ge(route_in, 1)
                act.activation(rt[:, :, 24:28], rt[:, :, 20:24], ACT.Exp).then_inc(route_exp, 1)
                act.wait_ge(route_in, 2)
                act.activation(rt[:, :, 60:61], rt[:, :, 59:60], ACT.Exp).then_inc(route_exp, 1)
                act.wait_ge(routed, l + 1)
                act.sem_inc(first, 1)
                with act.Fori(0, QUADS) as q:
                    act.reg_load(nreg, nround[0:1, bass.ds(q, 1)])
                    nv = act.snap(nreg, min_val=1, max_val=MAXROUND)
                    with act.Fori(0, nv) as r:
                        n = rounds_done(act, rounds)
                        act.wait_ge(gate_full, n + 1)
                        act.activation(sg, ps[:, 5, 0:DE], ACT.Silu).then_inc(sg_ready, 1)
                        act.wait_ge(pwt_full, n + 1)
                        act.activation(PwT, ps[:, 4, 0:T], ACT.Copy).then_inc(pwt_ready, 1)
                        act.wait_ge(hmt_full, n + 1)
                        act.activation(hmT[:, :, :], ps[:, 6, T:2 * T], ACT.Copy).then_inc(hmt_ready, 1)
                        act.wait_ge(y_full, n * 2 + 1)
                        act.activation(ysb[:, 0, :], ps[:, 5, :], ACT.Copy).then_inc(y0_ready, 1)
                        act.reg_add(rounds, rounds, 1)
                act.wait_ge(acc_last, 1)
                for b in range(4):
                    act.activation(x[:, b // 2, (b % 2) * 512:(b % 2 + 1) * 512], ps[:, b, :], ACT.Copy).then_inc(x_out, 1)
                act.wait_ge(x_out, 4)
                end_of_layer(act, l)
            chain[0] = 0
            rstd(rstd_ready, 0)

        @block.vector
        def _(dve):
            rounds = dve.alloc_register("dve_rounds")
            dve.reg_mov(rounds, 0)
            nreg = dve.alloc_register("dve_nround")
            chain = [0]
            TTn = dve.tensor_tensor

            def link(ins):
                chain[0] += 1
                ins.then_inc(dve_chain, 1)
                dve.wait_ge(dve_chain, chain[0])

            def get(name):
                b, n = bank_of[name]
                dve.wait_ge(full[b], n + 1)
                return ps[:, b, :]

            def free_(name):
                dve.sem_inc(free[bank_of[name][0]], 1)

            def scale_x(count):
                dve.wait_ge(rstd_ready, count)
                for j in range(TT):
                    dve.tensor_scalar(xn3[:, j, :], x[:, j, :], ss[:, 4 + j:5 + j], None, ALU.mult).then_inc(xn_ready, 1)

            def evac_hT(kind, gain):
                for i in range(4):
                    j, half = i // 2, i % 2
                    bank = get((kind, i))
                    g = pv(gain, half * 4, 4).unsqueeze(2).to_broadcast([P, 4, P])
                    link(TTn(hT3[:, half * 4:half * 4 + 4, j * P:(j + 1) * P],
                             bank.rearrange("p (k t) -> p k t", k=4), g, ALU.mult))
                    dve.sem_inc(hT_ready, 1)
                    free_((kind, i))

            def conv(i, cin, acc, w):
                dve.wait_ge(cin_ready, i + 1)
                s, a = cin[:, i % 3, :], acc[:, (i if i < 9 else i - 9) % 4, :]
                j_ = i if i < 9 else i - 9
                if j_ >= 4:
                    if i < 9:
                        dve.wait_ge(raw_ready, j_ - 3)
                    else:
                        dve.wait_ge(mq_ready, 2 * (j_ - 3))
                link(dve.tensor_scalar(a, s[:, 0:T], w(0), None, ALU.mult))
                for t in range(1, CONV):
                    link(dve.scalar_tensor_tensor(out=a, in0=s[:, t:t + T], scalar=w(t), in1=a, op0=ALU.mult, op1=ALU.add))
                dve.sem_inc(conv_ready, 1)
                dve.sem_inc(cin_used, 1)

            dve.wait_ge(x_loaded, 16)
            with dve.Fori(0, LAYERS) as l:
                dve.wait_ge(par_in, l * 16 + 16)
                dve.sem_inc(first, 1)
                link(dve.tensor_copy(par[:, :], par_next[:, :]))
                dve.sem_inc(par_ready, 1)
                scale_x(1)
                evac_hT("hT", "gain_mix")
                dve.wait_ge(const_in, 16)
                dve.wait_ge(init_done, 6)
                link(dve.memset(cin_g[:, :, 0:3], 0.0))
                bank = get("gates")
                b3 = bank[:, 0:TT * NG].rearrange("p (j c) -> p j c", j=TT)
                bias = pv("bias3", 0, 24).unsqueeze(1).to_broadcast([P, TT, 24])
                link(TTn(gz[:, :, :], b3, bias, ALU.add))
                free_("gates")
                link(dve.tensor_scalar(sp[:, 0, :, 0:6], gz[:, :, 0:6], -1.0, None, ALU.mult))
                link(dve.tensor_copy(sp[:, 0, :, 6:12], gz[:, :, 6:12]))
                link(dve.tensor_scalar(sp[:, 0, :, 12:18], gz[:, :, 18:24], -1.0, None, ALU.mult))
                z2 = sp[:, 0, :, :].rearrange("p j c -> p (j c)")
                dve.scalar_tensor_tensor(out=sp[:, 1, :, :].rearrange("p j c -> p (j c)"), in0=z2, scalar=-1.0, in1=z2,
                                         op0=ALU.mult, op1=ALU.max).then_inc(gates_z, 1)
                dve.wait_ge(gates_e, 2)
                link(dve.scalar_tensor_tensor(out=sp[:, 1, :, :].rearrange("p j c -> p (j c)"), in0=z2, scalar=0.0,
                                              in1=sp[:, 3, :, :].rearrange("p j c -> p (j c)"), op0=ALU.max, op1=ALU.add))
                link(dve.tensor_scalar(sp[:, 0, :, 0:6], sp[:, 1, :, 0:6], -1.0, None, ALU.mult))
                dve.sem_inc(gates_col, 1)
                link(dve.tensor_copy(selin[:, 1, :, 6:12], sp[:, 0, :, 0:6]))
                eab = ea[:, :].unsqueeze(1).to_broadcast([P, TT, GH])
                link(TTn(dpos[:, :, 0:6], sp[:, 1, :, 6:12], eab, ALU.mult))
                link(dve.tensor_copy(dpos[:, :, 6:12], sp[:, 1, :, 12:18]))
                link(dve.tensor_copy(selin[:, 0, :, 0:6], dpos[:, :, 0:6]))
                for o_ in (32, 64):
                    link(dve.tensor_copy(selin[:, 1, :, o_:o_ + 6], gz[:, :, 12:18]))
                    link(dve.tensor_copy(selin[:, 2, :, o_:o_ + 6], dpos[:, :, 6:12]))
                dve.sem_inc(selin_ready, 1)

                def wg(t):
                    return lambda k: pv("conv_g", t * CONV + k)

                for t in range(9):
                    conv(t, cin_g, acc_g, wg(t))
                bank = get("rows")
                link(dve.tensor_copy(rowsraw[:, :], bank[:, 0:T]))
                link(dve.tensor_copy(rows[0:12, :], rowsraw[0:12, :]))
                for q0 in (32, 64):
                    s = rowsraw[q0:q0 + 6, :]
                    link(dve.tensor_tensor_scan(rows[q0:q0 + 6, :], s, s, 0.0, ALU.max, ALU.max))
                link(dve.tensor_scalar(rows[32:38, :], rows[32:38, :], -1.0, None, ALU.mult))
                link(TTn(rows[64:70, :], rows[64:70, :], bank[64:70, T:2 * T], ALU.add))
                dve.sem_inc(rows_ready, 1)
                free_("rows")
                bank = get("cols")
                link(dve.tensor_copy(colv[:, 0:30], bank[:, 0:30]))
                free_("cols")
                cv = colv[:, 0:24].rearrange("p (j c) -> p j c", j=TT)
                link(TTn(colA[:, :, :], cv[:, :, 6:12], gz[:, :, 12:18], ALU.add))
                dve.wait_ge(beta_ready, GP)
                for t in range(6):
                    dve.wait_ge(rn_ready, t // 2 + 1)
                    if t < 3:
                        for a in range(2):
                            r_ = slice(64 * a, 64 * a + 64)
                            link(dve.scalar_tensor_tensor(out=kqz[r_, 2 * t + a, 1, :], in0=raw3[r_, t, :], scalar=QK_SCALE,
                                                          in1=rn[r_, t, :], op0=ALU.mult, op1=ALU.mult))
                    else:
                        p = t - 3
                        link(TTn(kf[:, p, :], raw3[:, t, :], rn[:, t, :], ALU.mult))
                        for a in range(2):
                            r_ = slice(64 * a, 64 * a + 64)
                            link(TTn(kqz[r_, 2 * p + a, 0, :], kf[r_, p, :], betab[r_, p, :], ALU.mult))
                        dve.sem_inc(kq_in_ready, 1)
                dve.wait_ge(gates_e, 3)
                vb4 = vb[:, :, :].rearrange("p t (h d) -> p t h d", h=GH)

                def earg(i, p):
                    bank = get(("dec", p))
                    h = i
                    bc = bank[:, (h % 2) * T:(h % 2 + 1) * T]
                    e = ebuf[:, h % 2, :]
                    for dst, src, col, lim in ((slice(0, P), slice(0, P), colv[:, h:h + 1], maskc[:, 0:P]),
                                               (slice(P, T), slice(P, T), colv[:, 24 + h:25 + h], maskc[:, P:T]),
                                               (slice(T, 384), slice(P, T), colv[:, 12 + h:13 + h], maskc[:, 0:P])):
                        link(dve.scalar_tensor_tensor(out=e[:, dst], in0=bc[:, src], scalar=col, in1=lim,
                                                      op0=ALU.add, op1=ALU.min))
                    dve.sem_inc(earg_ready, 1)

                def kq_mul(h):
                    dve.wait_ge(e_ready, h + 1)
                    e = ebuf[:, h % 2, :]
                    bank = get(("kq0", h))
                    link(TTn(KQ[:, h, :, 0:T], bank.rearrange("p (a t) -> p a t", a=2),
                             e[:, 0:T].unsqueeze(1).to_broadcast([P, 2, T]), ALU.mult))
                    free_(("kq0", h))
                    bank = get(("kq1", h))
                    link(TTn(KQ[:, h, :, T:384], bank[:, 0:T].rearrange("p (a t) -> p a t", a=2),
                             e[:, T:384].unsqueeze(1).to_broadcast([P, 2, P]), ALU.mult))
                    free_(("kq1", h))
                    dve.sem_inc(kq_ready, 1)

                for p in range(GP):
                    bank = get(("vt", p))
                    b_ = beta[:, :, 2 * p:2 * p + 2].unsqueeze(3).to_broadcast([P, TT, 2, HD])
                    link(TTn(vb4[:, :, 2 * p:2 * p + 2, :],
                             bank[:, 0:T].rearrange("p (t h d) -> p t h d", t=TT, h=2), b_, ALU.mult))
                    free_(("vt", p))
                    dve.sem_inc(vb_ready, 1)
                for h in range(GH):
                    if h == 0:
                        earg(0, 0)
                    if h + 1 < GH:
                        earg(h + 1, (h + 1) // 2)
                    if h % 2 == 0:
                        free_(("dec", h // 2))
                    kq_mul(h)

                def diag(h):
                    return KQ[:, h, 0, :].rearrange("p (b t) -> p b t", b=3)[:, 0:3:2, :]

                dve.wait_ge(lvl_in, 16)
                idb = cst[:, 0, :].unsqueeze(1)
                for g in range(3):
                    for h in (2 * g, 2 * g + 1):
                        link(TTn(XT[:, 2 * h:2 * h + 2, :], diag(h), lvl[:, 0, :].unsqueeze(1).to_broadcast([P, 2, P]), ALU.mult))
                    link(TTn(XT[:, 4 * g:4 * g + 4, :], idb.to_broadcast([P, 4, P]), XT[:, 4 * g:4 * g + 4, :], ALU.subtract))
                    dve.sem_inc(xt_ready, 1)
                for lev in range(1, 7):
                    for g in range(3):
                        bank = get(("W", lev, g))
                        for a in range(2):
                            h = 2 * g + a
                            link(TTn(diag(h), bank[:, a * T:(a + 1) * T].rearrange("p (b t) -> p b t", b=2),
                                     lvl[:, lev, :].unsqueeze(1).to_broadcast([P, 2, P]), ALU.mult))
                        dve.sem_inc(w_ready, 1)
                        free_(("W", lev, g))
                    for g in range(3):
                        bank = get(("Z", lev, g))
                        link(TTn(XT[:, 4 * g:4 * g + 4, :], XT[:, 4 * g:4 * g + 4, :],
                                 bank.rearrange("p (m t) -> p m t", m=4), ALU.subtract))
                        dve.sem_inc(xt_ready, 1)
                        free_(("Z", lev, g))
                bank = get("t1")
                link(TTn(vb[:, 1, :], vb[:, 1, :], bank[:, 0:GW], ALU.subtract))
                dve.sem_inc(t1_ready, 1)
                free_("t1")

                def head_result(cidx, src, rr):
                    dve.wait_ge(o_rr_ready, cidx + 1)
                    link(dve.scalar_tensor_tensor(out=rr, in0=src, scalar=pv("head_gain", cidx), in1=rr,
                                                  op0=ALU.mult, op1=ALU.mult))
                    link(TTn(mixT[:, cidx, :], rr, mixT[:, cidx, :], ALU.mult))
                    dve.sem_inc(mix_ready, 1)

                dve.wait_ge(gate_ready, 6)
                link(dve.tensor_scalar(mixT[:, 5:8, :], mixT[:, 5:8, :], 0.5, 0.5, ALU.mult, ALU.add))
                for p in range(GP):
                    bank = get(("o", p))
                    head_result(p, bank[:, 0:T], raw3[:, 3 + p, :])
                    free_(("o", p))
                link(dve.memset(cin_m[:, :, 0:3], 0.0))
                dve.sem_inc(conv_m_go, 1)
                for a in range(2):
                    bank = get(("rsw", a))
                    sin_b = rot[:, 1, :].unsqueeze(1).to_broadcast([P, 2, T])
                    cos_b = rot[:, 0, :].unsqueeze(1).to_broadcast([P, 2, T])
                    link(TTn(rtmp[:, :, :], bank.rearrange("p (c t) -> p c t", c=2), sin_b, ALU.mult))
                    free_(("rsw", a))
                    link(TTn(rraw[:, a, :, :], rraw[:, a, :, :], cos_b, ALU.mult))
                    if a == 0:
                        for b in range(2):
                            r_ = slice(64 * b, 64 * b + 64)
                            link(TTn(kqz[r_, b:4:2, 0, :], rraw[r_, a, :, :], rtmp[r_, :, :], ALU.add))
                    else:
                        link(TTn(rkf[:, :, :], rraw[:, a, :, :], rtmp[:, :, :], ALU.add))
                    dve.sem_inc(rq_ready, 1)

                def wm(t):
                    return lambda k: pv("conv_m", t * CONV + k)

                for t in range(6):
                    conv(9 + t, cin_m, acc_m, wm(t))
                for h in range(RH):
                    bank = get(("rs", h))
                    dve.wait_ge(rdec_ready, h + 1)
                    link(dve.scalar_tensor_tensor(out=rprob[h], in0=bank[:, 0:384], scalar=QK_SCALE, in1=rprob[h],
                                                  op0=ALU.mult, op1=ALU.mult))
                    dve.sem_inc(p_ready, 1)
                    free_(("rs", h))

                def m_exponents(p):
                    bank = get(("mdec", p))
                    for a in range(2):
                        h = 2 * p + a
                        bc = bank[:, a * T:(a + 1) * T]
                        link(dve.scalar_tensor_tensor(out=mprob[:, h, 0:T], in0=bc, scalar=colA[:, 0, h:h + 1],
                                                      in1=maskc[:, :], op0=ALU.add, op1=ALU.min))
                        link(dve.scalar_tensor_tensor(out=mprob[:, h, T:384], in0=bc[:, P:T], scalar=colA[:, 1, h:h + 1],
                                                      in1=maskc[:, 0:P], op0=ALU.add, op1=ALU.min))
                        dve.sem_inc(earg_ready, 1)
                    free_(("mdec", p))

                def m_multiply(p):
                    for h in (2 * p, 2 * p + 1):
                        bank = get(("ms", h))
                        dve.wait_ge(e_ready, GH + h + 1)
                        link(dve.scalar_tensor_tensor(out=mprob[:, h, :], in0=bank[:, 0:384], scalar=QK_SCALE,
                                                      in1=mprob[:, h, :], op0=ALU.mult, op1=ALU.mult))
                        dve.sem_inc(p_ready, 1)
                        free_(("ms", h))

                def m_divide(p):
                    bank = get(("o", 5 + p))
                    dve.wait_ge(em_ready, p + 1)
                    link(TTn(mden[:, p, :], mem[:, p, :], mden[:, p, :], ALU.max))
                    link(dve.reciprocal(mden[:, p, :], mden[:, p, :]))
                    link(TTn(mh[:, p, :], bank[:, 0:T], mden[:, p, :], ALU.mult))
                    dve.sem_inc(o_sq_in, 1)
                    free_(("o", 5 + p))

                m_exponents(0)
                for p in range(RP):
                    bank = get(("o", 3 + p))
                    head_result(3 + p, bank[:, 0:T], rrr[:, p, :])
                    free_(("o", 3 + p))
                m_multiply(0)
                m_exponents(1)
                m_multiply(1)
                m_exponents(2)
                m_divide(0)
                m_multiply(2)
                m_divide(1)
                head_result(5, mh[:, 0, :], mrr[:, 0, :])
                m_divide(2)
                head_result(6, mh[:, 1, :], mrr[:, 1, :])
                head_result(7, mh[:, 2, :], mrr[:, 2, :])
                for n in range(D // COLS):
                    bank = get(("wo", n))
                    link(TTn(x[:, :, n * COLS:(n + 1) * COLS], x[:, :, n * COLS:(n + 1) * COLS],
                             bank.rearrange("p (j c) -> p j c", j=TT), ALU.add))
                    dve.sem_inc(x_mixed, 1)
                    free_(("wo", n))
                scale_x(2)
                evac_hT("h2T", "gain_ffn")
                dve.wait_ge(part_ready, 2)
                TTn(rest, xn3[:, :, :], part[0], ALU.subtract).then_inc(rest_ready, 1)
                bank = get("logits")
                link(TTn(lg[:, :, :], bank[:, 0:72].rearrange("p (j c) -> p j c", j=TT),
                         pv("router_bias", 0, 36).unsqueeze(1).to_broadcast([P, TT, 36]), ALU.add))
                free_("logits")
                link(dve.tensor_copy(rt[:, :, 0:4], lg[:, :, 0:4]))
                for j in range(TT):
                    link(dve.max(rt[:, j, 8:16], rt[:, j, 0:8]))
                    link(dve.max_index(rtx[:, 0, j, :], rt[:, j, 8:16], rt[:, j, 0:8]))
                link(dve.tensor_copy(rt[:, :, 30:31], rtx[:, 0, :, 0:1]))
                link(TTn(rt[:, :, 20:24], rt[:, :, 0:4], rt[:, :, 8:9].to_broadcast([P, TT, 4]), ALU.subtract))
                dve.sem_inc(route_in, 1)
                link(TTn(rt[:, :, 16:20], iota[:, 0:4].unsqueeze(1).to_broadcast([P, TT, 4]),
                         rt[:, :, 30:31].to_broadcast([P, TT, 4]), ALU.is_equal))
                el = lg[:, :, 4:36].rearrange("p j (g e) -> p j e g", g=GROUPS)
                prod = pick[:, 3, :, :].rearrange("p j (e g) -> p j e g", g=GROUPS)
                link(TTn(prod, el, rt[:, :, 16:20].unsqueeze(2).to_broadcast([P, TT, PER_GROUP, GROUPS]), ALU.mult))
                link(dve.tensor_reduce(rt[:, :, 32:40], prod, AX_X, ALU.add))
                for j in range(TT):
                    link(dve.max(rt[:, j, 40:48], rt[:, j, 32:40]))
                    link(dve.max_index(rtx[:, 1, j, :], rt[:, j, 40:48], rt[:, j, 32:40]))
                link(dve.tensor_copy(rt[:, :, 48:50], rtx[:, 1, :, 0:2]))
                link(TTn(rt[:, :, 59:60], rt[:, :, 41:42], rt[:, :, 40:41], ALU.subtract))
                dve.sem_inc(route_in, 1)
                link(dve.tensor_scalar(rt[:, :, 31:32], rt[:, :, 30:31], float(PER_GROUP), None, ALU.mult))
                link(TTn(rt[:, :, 48:50], rt[:, :, 48:50], rt[:, :, 31:32].to_broadcast([P, TT, 2]), ALU.add))
                dve.wait_ge(route_exp, 1)
                link(dve.tensor_reduce(rt[:, :, 28:29], rt[:, :, 24:28], AX_X, ALU.add))
                link(dve.reciprocal(rt[:, :, 29:30], rt[:, :, 28:29]))
                dve.wait_ge(route_exp, 2)
                link(dve.tensor_scalar(rt[:, :, 61:62], rt[:, :, 60:61], 1.0, None, ALU.add))
                link(dve.reciprocal(rt[:, :, 62:63], rt[:, :, 61:62]))
                link(TTn(rt[:, :, 52:53], rt[:, :, 62:63], rt[:, :, 29:30], ALU.mult))
                link(TTn(rt[:, :, 53:54], rt[:, :, 52:53], rt[:, :, 60:61], ALU.mult))
                io32 = iota[:, 0:32].unsqueeze(1).to_broadcast([P, TT, EXPERTS])

                def over(col):
                    return rt[:, :, col:col + 1].to_broadcast([P, TT, EXPERTS])

                link(TTn(pick[:, 2, :, :], io32, over(48), ALU.is_equal))
                link(TTn(pick[:, 3, :, :], io32, over(49), ALU.is_equal))
                link(TTn(pick[:, 0, :, :], pick[:, 2, :, :], pick[:, 3, :, :], ALU.add))
                dve.sem_inc(mask_ready, 1)
                link(TTn(pick[:, 1, :, :], pick[:, 2, :, :], over(52), ALU.mult))
                link(TTn(pick[:, 3, :, :], pick[:, 3, :, :], over(53), ALU.mult))
                link(TTn(sel[:, 1, :, 0:EXPERTS], pick[:, 1, :, :], pick[:, 3, :, :], ALU.add))
                dve.wait_ge(part_ready, 3)
                TTn(part[2], rest, part[1], ALU.subtract).then_inc(rest_ready, 1)
                bank = get("rank")
                rk = pick[:, 2, :, :].rearrange("p j e -> p (j e)")
                link(dve.scalar_tensor_tensor(out=rk, in0=bank[:, 0:64], scalar=1.0,
                                              in1=pick[:, 0, :, :].rearrange("p j e -> p (j e)"), op0=ALU.add, op1=ALU.mult))
                link(dve.tensor_scalar(sel[:, 0, :, 0:EXPERTS], pick[:, 2, :, :], -1.0, None, ALU.add))
                link(dve.tensor_reduce(nround_f[:, 0:QUADS], bank[:, 64:96].rearrange("p (q e) -> p q e", e=4), AX_X, ALU.max))
                free_("rank")
                over_q = pick[:, 3, :, :].rearrange("p j e -> p (j e)").rearrange("p (q k) -> p q k", q=QUADS)
                link(TTn(over_q, iota[:, COUNT:COUNT + 8].unsqueeze(1).to_broadcast([P, QUADS, 8]),
                         nround_f[:, 0:QUADS].unsqueeze(2).to_broadcast([P, QUADS, 8]), ALU.is_lt))
                link(dve.tensor_reduce(nround_f[:, QUADS:2 * QUADS], over_q, AX_X, ALU.add))
                link(dve.tensor_scalar(nround[:, :], nround_f[:, QUADS:2 * QUADS], 1.0, None, ALU.max))
                dve.sem_inc(routed, 1)
                gq = pv("gain_ffn", 0, KD)

                def select(q4, ids, n):
                    for j in range(TT):
                        rkq = sel[:, 0, j, q4].unsqueeze(2).to_broadcast([P, 4, CAP])
                        ins = TTn(Psel[:, j, :].rearrange("p (e s) -> p e s", e=4), ids.unsqueeze(1).to_broadcast([P, 4, CAP]),
                                  rkq, ALU.is_equal)
                    ins.then_inc(psel_ready, 1)
                    dve.wait_ge(psel_ready, n * 2 + 1)
                    for j in range(TT):
                        wq = sel[:, 1, j, q4].unsqueeze(2).to_broadcast([P, 4, CAP])
                        ins = TTn(Pwt[:, j, :].rearrange("p (e s) -> p e s", e=4),
                                  Psel[:, j, :].rearrange("p (e s) -> p e s", e=4), wq, ALU.mult)
                    ins.then_inc(psel_ready, 1)

                def selected(n):
                    for half in range(2):
                        dve.wait_ge(gath_full, n * 2 + half + 1)
                        TTn(hq[:, half * 4:half * 4 + 4, :], ps[:, 4 + 3 * half, :].rearrange("p (k s) -> p k s", k=4),
                            gq[:, half * 4:half * 4 + 4].unsqueeze(2).to_broadcast([P, 4, P]), ALU.mult).then_inc(hq_ready, 1)

                n0 = rounds_done(dve, rounds) + l
                select(slice(0, 4), iota[:, 0:CAP], n0)
                selected(n0)
                with dve.Fori(0, QUADS) as q:
                    dve.reg_load(nreg, nround[0:1, bass.ds(q, 1)])
                    nv = dve.snap(nreg, min_val=1, max_val=MAXROUND)
                    with dve.Fori(0, nv) as r:
                        n = rounds_done(dve, rounds)
                        dve.wait_ge(pwt_full, n + 1)
                        with dve.If(r < nv - 1):
                            select(bass.ds(q * 4, 4), iota[:, bass.ds(r * CAP + CAP, CAP)], n + l + 1)
                        with dve.Else():
                            select(bass.ds(q * 4 + 4, 4), iota[:, 0:CAP], n + l + 1)
                        dve.wait_ge(sg_ready, n + 1)
                        dve.wait_ge(up_full, n + 1)
                        TTn(hmid, sg, ps[:, 6, 0:DE], ALU.mult).then_inc(hmid_ready, 1)
                        selected(n + l + 1)
                        dve.wait_ge(y_full, n * 2 + 2)
                        dve.tensor_copy(ysb[:, 1, :], ps[:, 6, :]).then_inc(y1_ready, 1)
                        dve.reg_add(rounds, rounds, 1)
                end_of_layer(dve, l)
            chain[0] = 0
            dve.wait_ge(rstd_ready, 1)
            dve.wait_ge(gfin_in, 16)
            for j in range(TT):
                link(dve.scalar_tensor_tensor(out=fin[:, j, :], in0=x[:, j, :], scalar=ss[:, 4 + j:5 + j], in1=gfin,
                                              op0=ALU.mult, op1=ALU.mult))
            dve.sem_inc(out_ready, 1)



def kernel(**inputs):
    import numpy as np
    import concourse.bacc as bacc
    from concourse.bass_utils import run_bass_kernel_spmd

    g = {k: np.ascontiguousarray(v) for k, v in inputs.items()}

    i = np.arange(P)
    row, col = i[:, None], i[None, :]
    tiles = {
        "ident": row == col, "cum": row <= col, "ncum": -1.0 * (row <= col), "nsuffix": -1.0 * (row > col),
        "before": row < col, "ones": np.ones((P, P)), "nones": -np.ones((P, P)), "headsum": row // HD == col // HD,
        "swap": 1.0 * ((row == col - HD // 2) & (col % HD >= HD // 2)) - 1.0 * ((row == col + HD // 2) & (col % HD < HD // 2)),
    }
    maskc = np.concatenate([np.where(row <= col, 0.0, NEG), np.zeros((P, P))], 1)
    d0 = np.where(row <= col, col - row, -NEG)
    dist = np.concatenate([d0, col + P - row, d0], 1)
    inv_freq = (np.float32(10000.0) ** (-np.arange(0, HD, 2, dtype=np.float32) / np.float32(HD))).astype(np.float32)
    ang = np.arange(T, dtype=np.float32)[None, :] * inv_freq[i % (HD // 2)][:, None]
    count = np.concatenate([np.arange(COUNT), CAP * np.arange(8)])
    consts = np.concatenate([tiles[n].astype(np.float32) for n in CONST] + [maskc, dist, np.cos(ang), np.sin(ang),
                            np.broadcast_to(count, (P, COUNT + 8))], 1).astype(np.float32)
    level_masks = np.stack([((row // (2 * b) == col // (2 * b)) & (row // b % 2 == 0) & (col // b % 2 == 1))
                            for b in LEVELS], 1).astype(np.float32)

    w_in = g["w_in"].reshape(LAYERS, P, KD, D_IN)
    w_mix = np.zeros((LAYERS, NMIX, P, KD, COLS), np.float32)
    for s, (_, cols) in enumerate(PROJ):
        at = 0
        for a, n in cols:
            w_mix[:, s, :, :, at:at + n] = w_in[:, :, :, a:a + n]
            at += n
    w_out = g["w_out"].reshape(LAYERS, KD, P, D // COLS, COLS)
    w_mix[:, NPROJ:] = w_out.transpose(0, 3, 2, 1, 4)
    w_mix = w_mix.reshape(LAYERS, NMIX, P, SLOT)

    def rows_all(a):
        return np.broadcast_to(a[:, None, :], (LAYERS, P, a.shape[1]))

    def conv_cols(a):
        return a.reshape(LAYERS, CONV, -1, P).transpose(0, 3, 2, 1).reshape(LAYERS, P, -1)

    head_gain = np.concatenate([g["gdn_norm"], g["ret_norm"], g["mlstm_norm"]], 1).reshape(LAYERS, MIX, P).transpose(0, 2, 1)
    zeros = np.zeros((LAYERS, P, GH), np.float32)
    params = np.concatenate([
        g["norm_mix"].reshape(LAYERS, P, KD), g["norm_ffn"].reshape(LAYERS, P, KD), conv_cols(g["gdn_conv"]),
        conv_cols(g["mlstm_conv"]), head_gain, rows_all(g["gdn_a_log"]), zeros, rows_all(g["gdn_dt_bias"]),
        rows_all(g["mlstm_i_bias"]), rows_all(g["mlstm_f_bias"]), np.zeros((LAYERS, P, GROUPS), np.float32),
        rows_all(g["router_bias"])], 2)
    params = params[[*range(LAYERS), LAYERS - 1]]
    router_w = np.concatenate([g["router_group"], g["router_expert"]], 2).reshape(LAYERS, P, KD, GROUPS + EXPERTS)
    router_w = router_w[[*range(LAYERS), LAYERS - 1]]
    experts = [g[n].reshape(LAYERS, EXPERTS, P, SLOT) for n in ("expert_gate", "expert_up", "expert_down")]
    x_in = g["x"].reshape(TT, P, D).transpose(1, 0, 2)
    gain_final = np.broadcast_to(g["norm_final"][None, :], (P, D))

    nc = bacc.Bacc("TRN2", target_bir_lowering=False, num_devices=1)
    arrays, args = {}, []
    for name, a in [("x_in", x_in), ("consts", consts), ("level_masks", level_masks), ("params", params), ("w_mix", w_mix),
                    ("router_w", router_w), ("e_gate", experts[0]), ("e_up", experts[1]), ("e_down", experts[2]),
                    ("gain_final", gain_final)]:
        a = np.ascontiguousarray(a)
        arrays[name] = a
        args.append(nc.dram_tensor(name, a.shape, F32, kind="ExternalInput").ap())
    out = nc.dram_tensor("out", (T, D), F32, kind="ExternalOutput").ap()
    trunk(nc, *args, out.rearrange("(j p) d -> p j d", p=P))
    r = run_bass_kernel_spmd(nc, [arrays], core_ids=[0])
    return r.results[0]["out"].reshape(1, T, D)
```

```python
from contextlib import ExitStack
import math

import concourse.bass as bass
from concourse import mybir

F32 = mybir.dt.float32
BF16 = mybir.dt.bfloat16
U32 = mybir.dt.uint32
I32 = mybir.dt.int32
ALU = mybir.AluOpType
ACT = mybir.ActivationFunctionType
AX_X = mybir.AxisListType.X

P = 128
LAYERS = 2
D = 1024
T = 256
TT = T // P
KD = D // P
HD = 64
GH, RH, MH = 6, 4, 6
GP, RP, MP = GH // 2, RH // 2, MH // 2
MIX = GP + RP + MP
CONV = 4
GROUPS, PER_GROUP = 4, 8
EXPERTS = GROUPS * PER_GROUP
DE = D // 4
EPS = 1e-6
RING = 12
SPARE = 4
SLOT = 2048
COLS = SLOT // KD
QUADS = EXPERTS // 4
CAP = P // 4
MAXROUND = T // CAP
COUNT = T + CAP
NEG = -1e30
QK_SCALE = HD ** -0.5

GW, RW, MW = GH * HD, RH * HD, MH * HD
C_Z = 3 * GW
C_B = C_Z + GW
C_RQ = C_B + 2 * GH
C_RV = C_RQ + 2 * RW
C_RG = C_RV + RW
C_MQ = C_RG + RW
C_MV = C_MQ + 2 * MW
C_MO = C_MV + MW
C_I = C_MO + MW
D_IN = C_I + 2 * MH
NG = 2 * GH + 2 * MH
PROJ = [("gatesT", [(C_B, 2 * GH), (C_I, 2 * MH)])]
PROJ += [(("gdn", s), [(COLS * s, min(COLS, 3 * GW - COLS * s))]) for s in range(5)]
PROJ += [(("gate", 0), [(C_Z, COLS)]), (("gate", 1), [(C_Z + COLS, P)]), (("gate", 2), [(C_RG, RW)]),
         (("gate", 3), [(C_MO, COLS)]), (("gate", 4), [(C_MO + COLS, P)])]
PROJ += [(("rqk", 0), [(C_RQ, COLS)]), (("rqk", 1), [(C_RQ + RW, COLS)])]
PROJ += [(("mqk", s), [(C_MQ + COLS * s, COLS)]) for s in range(3)]
PROJ += [(("rv", 0), [(C_RV, RW)])]
PROJ += [(("mv", s), [(C_MV + P * s, P)]) for s in range(3)]
GATE_TILES = [(0, 1), (2,), (3, 4), (5, 6), (7,)]
SLOT_OF = {name: i for i, (name, _) in enumerate(PROJ)}
WIDTH = {name: sum(n for _, n in cols) for name, cols in PROJ}
NPROJ = len(PROJ)
NMIX = NPROJ + D // COLS
NMOE = 3 * EXPERTS
WIDE = RING + SPARE
LAP = 4
assert NMIX == 2 * RING and LAP * 12 % WIDE == 0 and QUADS % LAP == 0 and D_IN == 4120

CONST = ["ident", "cum", "ncum", "nsuffix", "before", "ones", "nones", "headsum", "swap"]
LEVELS = [2 ** i for i in range(7)]

PAR = {}
_at = 0
for _name, _n in [("gain_mix", KD), ("gain_ffn", KD), ("conv_g", 9 * CONV), ("conv_m", 6 * CONV),
                  ("head_gain", MIX), ("a_log", GH), ("bias3", 2 * GH + 2 * MH), ("router_bias", 36)]:
    PAR[_name] = (_at, _at + _n)
    _at += _n
NPAR = _at
NCONST = len(CONST) * P + T + 384 + 2 * T + COUNT + 8
LN_EXP = "natural_log_exp_and_others"


def psum_plan():
    order = [("hT", i) for i in range(4)] + ["gatesT", ("gdn", 0), "gates"] + [("gdn", s) for s in range(1, 5)]
    order += ["rows", "cols", ("gate", 0), ("beta", 0), ("beta", 1)] + [("nrm", s) for s in range(3)] + [("gate", 1)]
    order += [("vt", p) for p in range(GP)] + [("dec", 0)]
    for h in range(GH):
        if h in (2, 4):
            order += [("gate", h // 2 + 1)]
        if h % 2 == 0 and h // 2 + 1 < GP:
            order += [("dec", h // 2 + 1)]
        order += [("kq0", h), ("kq1", h)]
    order += [("A", g) for g in range(3)] + [("gate", 4)] + [("X", 0, g) for g in range(3)]
    for lev in range(1, 7):
        order += [("W", lev, g) for g in range(3)] + [("Z", lev, g) for g in range(3)]
        if lev < 6:
            order += [("X", lev, g) for g in range(3)]
    order += [("rqk", 0), "u1", "t1", ("rqk", 1), "u2"] + [("o", p) for p in range(GP)] + [("on", p) for p in range(GP)]
    order += [("rsw", 0), ("rsw", 1)] + [("mqk", s) for s in range(3)] + [("rv", 0), ("mv", 0)]
    order += [("rs", h) for h in range(RH)] + [("mdec", 0), ("mv", 1), ("o", 3), ("o", 4), ("mv", 2), ("on", 3), ("on", 4)]
    order += [("ms", 0), ("ms", 1), ("em", 0), ("mdec", 1), ("ms", 2), ("ms", 3), ("em", 1), ("em", 2)]
    banks = [i % 8 for i in range(len(order))]
    last = [("o", 5), ("mdec", 2), ("ms", 4), ("ms", 5), ("o", 6), ("on", 5), ("o", 7), ("on", 6), ("on", 7)]
    last += [("h2T", i) for i in range(4)] + ["logitsT", "logits", "rank"]
    banks += [n for n in range(D // COLS)] + [4 + i % 4 for i in range(len(last) - 1)] + [6]
    return list(zip(order + [("wo", n) for n in range(D // COLS)] + last, banks))


def trunk(nc, x_in, consts, level_masks, params, w_mix, router_w, e_gate, e_up, e_down, gain_final, out):
    bank_of, uses = {}, [0] * 8
    for name, b in psum_plan():
        bank_of[name] = (b, uses[b])
        uses[b] += 1

    with ExitStack() as ctx:
        def sb(name, shape, dt=F32):
            return ctx.enter_context(nc.sbuf_tensor(name, shape, dt))

        def sem(name):
            return ctx.enter_context(nc.semaphore(name))

        ring = sb("ring", [P, RING, SLOT])
        x = sb("x", [P, TT, D])
        xn = sb("xn", [P, TT * D])
        hT = sb("hT", [P, KD * T])
        shared = sb("shared", [P, 12 * T + 3 * T + 2 * GW + 9 * T + 12 * T])
        o = 0
        kqz = shared[:, o:o + 12 * T].rearrange("p (h a t) -> p h a t", h=GH, a=2)
        o += 12 * T
        kf = shared[:, o:o + 3 * T].rearrange("p (c t) -> p c t", c=GP)
        o += 3 * T
        vb = shared[:, o:o + 2 * GW].rearrange("p (t c) -> p t c", t=TT)
        o += 2 * GW
        raw = shared[:, o:o + 9 * T]
        o += 9 * T
        xxt = shared[:, o:o + 12 * T]
        slot = [ring[:, i, :] for i in range(RING)]
        slot[RING - SPARE:RING - SPARE] = [shared[:, i * SLOT:(i + 1) * SLOT] for i in range(SPARE)]
        kq = sb("kq", [P, GH * 2 * 384])
        shapes = sb("shapes", [P, NCONST])
        lvl = sb("lvl", [P, len(LEVELS), P], BF16)
        selin = sb("selin", [P, 3, TT, P])
        rows = sb("rows", [P, T])
        rowsraw = sb("rowsraw", [P, T])
        ebuf = sb("ebuf", [P, 2, 384])
        par = sb("par", [P, NPAR])
        par_next = sb("par_next", [P, NPAR])
        rw = sb("rw", [P, KD, 36])
        epsc = sb("epsc", [P, 1])
        ss = sb("ss", [P, 8])
        gz = sb("gz", [P, TT, 24])
        sp = sb("sp", [P, 4, TT, 18])
        ea = sb("ea", [P, GH])
        dpos = sb("dpos", [P, TT, 12])
        beta = sb("beta", [P, TT, GH])
        colv = sb("colv", [P, 32])
        colA = sb("colA", [P, TT, MH])
        lg = sb("lg", [P, TT, 36])
        lgT = sb("lgT", [P, T])
        rt = sb("rt", [P, TT, 64])
        rtx = sb("rtx", [P, 2, TT, 8], U32)
        rkw = sb("rkw", [P, TT, EXPERTS])
        pick = sb("pick", [P, 4, TT, EXPERTS])
        sel = sb("sel", [P, 2, TT, EXPERTS + 4])
        nround_f = sb("nround_f", [P, 32 + 2 * QUADS])
        nround = sb("nround", [P, QUADS], I32)

        o = len(CONST) * P
        cst = shapes[:, 0:o].rearrange("p (a b) -> p a b", b=P)
        maskc = shapes[:, o:o + T]
        dist = shapes[:, o + T:o + T + 384]
        o += T + 384
        rot = shapes[:, o:o + 2 * T].rearrange("p (a b) -> p a b", b=T)
        iota = shapes[:, o + 2 * T:NCONST]

        def c(name):
            return cst[:, CONST.index(name), :]

        def pv(name, i=0, n=1):
            a, _ = PAR[name]
            return par[:, a + i:a + i + n]

        xn3 = xn[:, :].rearrange("p (t d) -> p t d", t=TT)
        hT3 = hT[:, :].rearrange("p (k t) -> p k t", k=KD)
        mixT = xn[:, :].rearrange("p (c t) -> p c t", c=MIX)
        raw3 = raw[:, :].rearrange("p (c t) -> p c t", c=9)
        Amat = raw[:, 0:12 * P].rearrange("p (m t) -> p m t", m=12)
        XT = xxt[:, 0:12 * P].rearrange("p (m t) -> p m t", m=12)
        X = xxt[:, 12 * P:24 * P].rearrange("p (m t) -> p m t", m=12)
        sqn = xxt[:, 0:6 * T].rearrange("p (c t) -> p c t", c=6)
        rn = xxt[:, 6 * T:12 * T].rearrange("p (c t) -> p c t", c=6)
        KQ = kq[:, :].rearrange("p (h a t) -> p h a t", h=GH, a=2)
        betab = kq[:, 5 * 768:6 * 768].rearrange("p (c t) -> p c t", c=3)
        HAL = T + 4
        cin_g = xn[:, 0:3 * HAL].rearrange("p (b t) -> p b t", b=3)
        acc_g = xn[:, 3 * HAL:3 * HAL + 4 * T].rearrange("p (b t) -> p b t", b=4)
        cin_m = raw[:, 0:3 * HAL].rearrange("p (b t) -> p b t", b=3)
        acc_m = raw[:, 3 * HAL:3 * HAL + 4 * T].rearrange("p (b t) -> p b t", b=4)
        vm = kq[:, 0:768].rearrange("p (t c) -> p t c", t=TT)
        vr = kq[:, 768:1280].rearrange("p (t c) -> p t c", t=TT)
        rkf = kq[:, 1280:1792].rearrange("p (c t) -> p c t", c=RP)
        rprob = [kq[:, 1792 + 384 * h:2176 + 384 * h] for h in range(2)]
        rprob += [xxt[:, 2304 + 384 * h:2688 + 384 * h] for h in range(2)]
        mprob = raw[:, 0:MH * 384].rearrange("p (h t) -> p h t", h=MH)
        rraw = kq[:, 2560:3584].rearrange("p (a c t) -> p a c t", a=2, c=2)
        rtmp = kq[:, 3584:4096].rearrange("p (c t) -> p c t", c=2)
        rsq = kq[:, 4096:4608].rearrange("p (c t) -> p c t", c=2)
        rrr = rraw[:, 0, :, :]
        late = shared[:, SPARE * SLOT:SPARE * SLOT + 7 * T].rearrange("p (c t) -> p c t", c=7)
        mh, mden = late[:, 0:3, :], late[:, 3:6, :]
        mem = [late[:, 6, :], hT3[:, 6, :], hT3[:, 7, :]]
        msq, mrr = hT3[:, 0:3, :], hT3[:, 3:6, :]
        hq = hT[:, 0:1024].rearrange("p (k s) -> p k s", k=KD)
        ysb = hT[:, 1024:2048].rearrange("p (n s) -> p n s", n=2)
        Psel = kq[:, 0:128].bitcast(BF16).rearrange("p (t s) -> p t s", t=TT)
        Pwt = kq[:, 128:384].rearrange("p (t s) -> p t s", t=TT)
        PwT = kq[:, 384:640]
        sg = kq[:, 640:896]
        hmid = kq[:, 896:1152]
        hmT = kq[:, 1152:1408].rearrange("p (f s) -> p f s", f=2)
        part = [kq[:, 1408 + 1024 * i:1408 + 1024 * (i + 1)].bitcast(BF16).rearrange("p (t d) -> p t d", t=TT) for i in range(3)]
        rest = hT[:, :].rearrange("p (t d) -> p t d", t=TT)
        gfin = xn[:, D:2 * D]
        fin = shared[:, 0:TT * D].rearrange("p (t d) -> p t d", t=TT)
        junk = xn[:, 0:D]

        ps = ctx.enter_context(nc.psum_tensor("ps", [P, 8, 512], F32))

        first = sem("layer_first")
        full = [sem(f"bank_full{b}") for b in range(8)]
        free = [sem(f"bank_free{b}") for b in range(8)]
        dve_chain = sem("dve_chain")
        act_chain = sem("act_chain")
        rstd_ready = sem("rstd_ready")
        squared = sem("squared")
        xn_ready = sem("xn_ready")
        hT_ready = sem("hT_ready")
        gates_z = sem("gates_z")
        gates_e = sem("gates_e")
        gates_col = sem("gates_col")
        selin_ready = sem("selin_ready")
        rows_ready = sem("rows_ready")
        cin_ready = sem("cin_ready")
        cin_used = sem("cin_used")
        conv_ready = sem("conv_ready")
        conv_m_go = sem("conv_m_go")
        raw_ready = sem("raw_ready")
        sq_ready = sem("sq_ready")
        rn_ready = sem("rn_ready")
        beta_ready = sem("beta_ready")
        kq_in_ready = sem("kq_in_ready")
        earg_ready = sem("earg_ready")
        e_ready = sem("e_ready")
        kq_ready = sem("kq_ready")
        vb_ready = sem("vb_ready")
        a_ready = sem("a_ready")
        xt_ready = sem("xt_ready")
        x_ready = sem("x_ready")
        w_ready = sem("w_ready")
        u_ready = sem("u_ready")
        t1_ready = sem("t1_ready")
        o_sq_ready = sem("o_sq_ready")
        o_sq_in = sem("o_sq_in")
        o_rr_ready = sem("o_rr_ready")
        rraw_ready = sem("rraw_ready")
        rq_ready = sem("rq_ready")
        val_ready = sem("val_ready")
        mq_ready = sem("mq_ready")
        gate_ready = sem("gate_ready")
        rdec_ready = sem("rdec_ready")
        p_ready = sem("p_ready")
        em_ready = sem("em_ready")
        mix_ready = sem("mix_ready")
        x_mixed = sem("x_mixed")
        hT_ready_act = sem("hT_ready_act")
        rwg_ready = sem("rwg_ready")
        kqz_zero = sem("kqz_zero")
        lgT_ready = sem("lgT_ready")
        route_in = sem("route_in")
        route_exp = sem("route_exp")
        mask_ready = sem("mask_ready")
        part_ready = sem("part_ready")
        rest_ready = sem("rest_ready")
        acc_init = sem("acc_init")
        acc_last = sem("acc_last")
        x_out = sem("x_out")
        last = sem("layer_last")
        const_in = sem("const_in")
        sumsq = sem("sumsq")
        x_loaded = [sem(f"x_loaded{j}") for j in range(TT)]
        init_done = sem("init_done")
        par_in = sem("par_in")
        rw_in = sem("rw_in")
        lvl_in = sem("lvl_in")
        par_ready = sem("par_ready")
        routed = sem("routed")
        logits_read = sem("logits_read")
        layer_end = sem("layer_end")
        layer_go = sem("layer_go")
        arrived = [sem(f"slot_arrived{s}") for s in range(RING)]
        arrived[RING - SPARE:RING - SPARE] = [sem(f"spare_arrived{s}") for s in range(SPARE)]
        slots_free = sem("slots_free")
        psel_ready = sem("psel_ready")
        gath_full = sem("gath_full")
        hq_ready = sem("hq_ready")
        pwt_full = sem("pwt_full")
        pwt_ready = sem("pwt_ready")
        gate_full = sem("gate_full")
        sg_ready = sem("sg_ready")
        up_full = sem("up_full")
        hmid_ready = sem("hmid_ready")
        hmt_full = sem("hmt_full")
        hmt_ready = sem("hmt_ready")
        y_full = sem("y_full")
        y0_ready = sem("y0_ready")
        y1_ready = sem("y1_ready")
        gfin_in = sem("gfin_in")
        out_ready = sem("out_ready")
        out_done = sem("out_done")
        per_layer = range(first.num, last.num + 1)

        def rounds_done(eng, rounds):
            return eng.snap(rounds, min_val=0, max_val=MAXROUND * QUADS * LAYERS)

        def end_of_layer(eng, l):
            eng.sem_inc(layer_end, 1)
            eng.wait_ge(layer_go, l + 1)

        block = ctx.enter_context(nc.Block())

        @block.sync
        def _(sync):
            for j in range(TT):
                sync.dma_start(x[:, j, :], x_in[:, j, :]).then_inc(x_loaded[j], 16)
            sync.dma_start(shapes[:, :], consts).then_inc(const_in, 16)
            with sync.Fori(0, LAYERS) as l:
                start = l * (NMIX + SPARE + NMOE)
                for i in range(NMIX):
                    s = i % RING
                    at = s if s < RING - SPARE else s + SPARE
                    n = WIDTH[PROJ[i][0]] if i < NPROJ else COLS
                    sync.wait_ge(slots_free, start + i + 1)
                    dst = ring[:, s, :].rearrange("p (k c) -> p k c", k=KD)
                    src = w_mix[l, i].rearrange("p (k c) -> p k c", k=KD)
                    if n == COLS:
                        dst, src = ring[:, s, :], w_mix[l, i]
                    else:
                        dst, src = dst[:, :, 0:n], src[:, :, 0:n]
                    sync.dma_start(dst, src).then_inc(arrived[at], 16)
                with sync.Fori(0, QUADS // LAP) as lap:
                    for u in range(LAP):
                        for m, src in enumerate((e_gate, e_up, e_down)):
                            for e in range(4):
                                i = 12 * u + 4 * m + e
                                sync.wait_ge(slots_free, start + NMIX + lap * (12 * LAP) + i + 1)
                                sync.dma_start(slot[i % WIDE], src[l, lap * (4 * LAP) + (4 * u + e)]).then_inc(arrived[i % WIDE], 16)
                sync.sem_inc(layer_end, 1)
            for j in range(TT):
                sync.wait_ge(out_ready, j + 1)
                sync.dma_start(out[:, j, :], fin[:, j, :]).then_inc(out_done, 16)
            sync.wait_ge(out_done, 16 * TT)

        @block.gpsimd
        def _(pool):
            pool.dma_start(par_next[:, :], params[0]).then_inc(par_in, 16)
            pool.dma_start(rw[:, :, :], router_w[0]).then_inc(rw_in, 16)
            pool.dma_start(lvl[:, :, :], level_masks).then_inc(lvl_in, 16)
            pool.memset(epsc[:, :], EPS).then_inc(init_done, 1)
            pool.memset(lgT[:, :], 0.0).then_inc(init_done, 1)
            pool.memset(selin[:, :, :, :], 0.0).then_inc(init_done, 1)
            pool.memset(rows[:, :], 0.0).then_inc(init_done, 1)
            pool.memset(rt[:, :, :], -3e38).then_inc(init_done, 1)
            pool.memset(sel[:, :, :, :], -1.0).then_inc(init_done, 1)
            with pool.Fori(0, LAYERS) as l:
                pool.memset(kqz[:, :, :, :], 0.0).then_inc(kqz_zero, 1)
                pool.wait_ge(par_ready, l + 1)
                pool.sem_inc(first, 1)
                pool.dma_start(par_next[:, :], params[l + 1]).then_inc(par_in, 16)
                pool.wait_ge(lgT_ready, 2)
                for j in range(TT):
                    pool.wait_ge(part_ready, j + 1)
                    pool.tensor_tensor(rest[:, j, :], xn3[:, j, :], part[0][:, j, :], ALU.subtract).then_inc(rest_ready, 1)
                for j in range(TT):
                    pool.wait_ge(part_ready, TT + j + 1)
                    pool.tensor_tensor(part[2][:, j, :], rest[:, j, :], part[1][:, j, :], ALU.subtract).then_inc(rest_ready, 1)
                with pool.If(l == LAYERS - 1):
                    pool.dma_start(gfin, gain_final).then_inc(gfin_in, 16)
                pool.wait_ge(logits_read, l + 1)
                pool.sem_inc(first, 1)
                pool.dma_start(rw[:, :, :], router_w[l + 1]).then_inc(rw_in, 16)
                pool.wait_ge(layer_end, l * 4 + 4)
                pool.sem_inc(first, 1)
                pool.sem_clear(per_layer)
                pool.sem_inc(layer_go, 1)

        @block.tensor
        def _(pe):
            rounds = pe.alloc_register("pe_rounds")
            pe.reg_mov(rounds, 0)
            nreg = pe.alloc_register("pe_nround")

            def begin(name):
                b, n = bank_of[name]
                if n:
                    pe.wait_ge(free[b], n)
                return ps[:, b, :]

            def done(ins, name):
                ins.then_inc(full[bank_of[name][0]], 1)

            def have_slot(start_lap, i):
                s = i % RING
                pe.wait_ge(arrived[s if s < RING - SPARE else s + SPARE], (start_lap + i // RING) * 16 + 16)

            def slot_w(i):
                return ring[:, i % RING, :].rearrange("p (k c) -> p k c", k=KD)

            held = []

            def release():
                if held:
                    b, n = bank_of[held.pop()]
                    pe.wait_ge(full[b], n + 1)
                    pe.sem_inc(slots_free, 1)

            def project_cm(name, start_lap):
                i = SLOT_OF[name]
                bank = begin(name)
                have_slot(start_lap, i)
                w = slot_w(i)
                for ct in range(WIDTH[name] // P):
                    for k in range(KD):
                        mm = pe.matmul(bank[:, ct * T:(ct + 1) * T], w[:, k, ct * P:(ct + 1) * P], hT3[:, k, :],
                                       start=(k == 0), stop=(k == KD - 1))
                done(mm, name)
                release()
                held.append(name)

            def project_tm(name, start_lap):
                i = SLOT_OF[name]
                n = WIDTH[name]
                bank = begin(name)
                have_slot(start_lap, i)
                w = slot_w(i)
                for j in range(TT):
                    for k in range(KD):
                        mm = pe.matmul(bank[:, j * n:(j + 1) * n], hT3[:, k, j * P:(j + 1) * P], w[:, k, 0:n],
                                       start=(k == 0), stop=(k == KD - 1))
                done(mm, name)
                release()
                held.append(name)

            def transpose_x(kind, xn_count):
                for i in range(4):
                    j, half = i // 2, i % 2
                    bank = begin((kind, i))
                    if half == 0:
                        pe.wait_ge(xn_ready, xn_count + j + 1)
                    for kk in range(4):
                        k = half * 4 + kk
                        mm = pe.transpose(bank[:, kk * P:(kk + 1) * P], xn3[:, j, k:D:KD], c("ident"))
                    done(mm, (kind, i))

            pe.sem_inc(slots_free, RING)
            pe.wait_ge(const_in, 16)
            for j in range(TT):
                pe.wait_ge(x_loaded[j], 16)
            with pe.Fori(0, LAYERS) as l:
                lap = l * (NMIX // RING + NMOE // WIDE)
                transpose_x("hT", 0)
                pe.wait_ge(init_done, 6)
                pe.wait_ge(hT_ready, 4)
                bank = begin("gatesT")
                have_slot(lap, 0)
                for k in range(KD):
                    mm = pe.matmul(bank[0:NG, 0:T], slot_w(0)[:, k, 0:NG], hT3[:, k, :], start=(k == 0), stop=(k == KD - 1))
                done(mm, "gatesT")
                held.append("gatesT")
                project_cm(("gdn", 0), lap)
                bank = begin("gates")
                pe.wait_ge(lgT_ready, 1)
                for j in range(TT):
                    mm = pe.transpose(bank[:, j * P:(j + 1) * P], lgT[:, j * P:(j + 1) * P], c("ident"))
                done(mm, "gates")
                for s in range(1, 5):
                    project_cm(("gdn", s), lap)

                pe.wait_ge(selin_ready, 1)
                bank = begin("rows")
                for j in range(TT):
                    o_ = bank[:, j * P:(j + 1) * P]
                    pe.matmul(o_, selin[:, 0, j, :], c("ncum"), start=True, stop=False)
                    pe.matmul(o_, selin[:, 1, j, :], c("ident"), start=False, stop=False)
                    pe.matmul(o_, selin[:, 2, j, :], c("cum"), start=False, stop=(j == 0))
                    if j:
                        pe.matmul(o_, selin[:, 2, 0, :], c("ones"), start=False, stop=True)
                for j in range(TT):
                    o_ = bank[64:64 + MH, T + j * P:T + (j + 1) * P]
                    mm = pe.matmul(o_, dpos[:, j, GH:GH + MH], c("ncum"), start=True, stop=(j == 0))
                    if j:
                        mm = pe.matmul(o_, dpos[:, 0, GH:GH + MH], c("nones"), start=False, stop=True)
                done(mm, "rows")
                release()
                bank = begin("cols")
                pe.matmul(bank[:, 0:12], c("cum"), dpos[:, 0, :], start=True, stop=True)
                pe.matmul(bank[:, 12:24], c("cum"), dpos[:, 1, :], start=True, stop=False)
                pe.matmul(bank[:, 18:24], c("ones"), dpos[:, 0, GH:GH + MH], start=False, stop=True)
                mm = pe.matmul(bank[:, 24:24 + GH], c("nsuffix"), dpos[:, 0, 0:GH], start=True, stop=True)
                done(mm, "cols")
                project_cm(("gate", 0), lap)
                pe.wait_ge(rows_ready, 1)
                for p in range(GP):
                    if p % 2 == 0:
                        bank = begin(("beta", p // 2))
                    for a in range(2):
                        r = GH + 2 * p + a
                        mm = pe.matmul(bank[64 * a:64 * a + 64, (p % 2) * T:(p % 2) * T + T],
                                       cst[:, 0, r:r + 1].to_broadcast([P, 64]), rows[:, :], start=True, stop=True)
                    if p % 2 or p == GP - 1:
                        done(mm, ("beta", p // 2))
                for s in range(3):
                    bank = begin(("nrm", s))
                    pe.wait_ge(sq_ready, s + 1)
                    mm = pe.matmul(bank[:, :], c("headsum"), sqn[:, 2 * s:2 * s + 2, :], start=True, stop=True)
                    done(mm, ("nrm", s))
                project_cm(("gate", 1), lap)

                def decay_rows(i):
                    bank = begin(("dec", i))
                    for a in range(2):
                        r = 2 * i + a
                        mm = pe.matmul(bank[:, a * T:(a + 1) * T], cst[:, 0, r:r + 1].to_broadcast([P, P]), rows[:, :],
                                       start=True, stop=True)
                    done(mm, ("dec", i))

                pe.wait_ge(raw_ready, 9)
                for p in range(GP):
                    bank = begin(("vt", p))
                    for j in range(TT):
                        mm = pe.transpose(bank[:, j * P:(j + 1) * P], raw3[:, 6 + p, j * P:(j + 1) * P], c("ident"))
                    done(mm, ("vt", p))
                decay_rows(0)
                for h in range(GH):
                    if h in (2, 4):
                        project_cm(("gate", h // 2 + 1), lap)
                    if h % 2 == 0 and h // 2 + 1 < GP:
                        decay_rows(h // 2 + 1)
                    pe.wait_ge(kq_in_ready, h // 2 + 1)
                    bank = begin(("kq0", h))
                    done(pe.matmul(bank[:, :], kf[:, h // 2, 0:P], kqz[:, h, :, :], start=True, stop=True), ("kq0", h))
                    bank = begin(("kq1", h))
                    done(pe.matmul(bank[:, 0:T], kf[:, h // 2, P:T], kqz[:, h, :, P:T], start=True, stop=True), ("kq1", h))
                for g in range(3):
                    bank = begin(("A", g))
                    pe.wait_ge(kq_ready, 2 * g + 2)
                    for m in range(4):
                        h, j = 2 * g + m // 2, m % 2
                        mm = pe.transpose(bank[:, m * P:(m + 1) * P], KQ[:, h, 0, 256 * j:256 * j + P], c("ident"))
                    done(mm, ("A", g))
                project_cm(("gate", 4), lap)
                for g in range(3):
                    bank = begin(("X", 0, g))
                    pe.wait_ge(xt_ready, g + 1)
                    for m in range(4):
                        mm = pe.transpose(bank[:, m * P:(m + 1) * P], XT[:, 4 * g + m, :], c("ident"))
                    done(mm, ("X", 0, g))
                for lev in range(1, 7):
                    for g in range(3):
                        bank = begin(("W", lev, g))
                        pe.wait_ge(a_ready, g + 1)
                        pe.wait_ge(xt_ready, 3 * lev + g - 2)
                        rows_, c0 = (HD, HD) if lev == 6 else (P, 0)
                        for m in range(4):
                            mm = pe.matmul(bank[0:rows_, m * P + c0:(m + 1) * P], Amat[:, 4 * g + m, 0:rows_],
                                           XT[:, 4 * g + m, c0:P], start=True, stop=True)
                        done(mm, ("W", lev, g))
                    for g in range(3):
                        bank = begin(("Z", lev, g))
                        pe.wait_ge(w_ready, 3 * (lev - 1) + g + 1)
                        pe.wait_ge(x_ready, 3 * (lev - 1) + g + 1)
                        for m in range(4):
                            h, j = 2 * g + m // 2, m % 2
                            mm = pe.matmul(bank[0:rows_, m * P + c0:(m + 1) * P], X[:, 4 * g + m, 0:rows_],
                                           KQ[:, h, 0, 256 * j + c0:256 * j + P], start=True, stop=True)
                        done(mm, ("Z", lev, g))
                    if lev < 6:
                        for g in range(3):
                            bank = begin(("X", lev, g))
                            pe.wait_ge(xt_ready, 3 * lev + g + 1)
                            for m in range(4):
                                mm = pe.transpose(bank[:, m * P:(m + 1) * P], XT[:, 4 * g + m, :], c("ident"))
                            done(mm, ("X", lev, g))
                project_cm(("rqk", 0), lap)
                bank = begin("u1")
                pe.wait_ge(xt_ready, 21)
                pe.wait_ge(vb_ready, 3)
                for h in range(GH):
                    mm = pe.matmul(bank[:, h * HD:(h + 1) * HD], XT[:, 2 * h, :], vb[:, 0, h * HD:(h + 1) * HD],
                                   start=True, stop=True)
                done(mm, "u1")
                bank = begin("t1")
                pe.wait_ge(u_ready, 1)
                for h in range(GH):
                    mm = pe.matmul(bank[:, h * HD:(h + 1) * HD], KQ[:, h, 0, P:2 * P], vb[:, 0, h * HD:(h + 1) * HD],
                                   start=True, stop=True)
                done(mm, "t1")
                project_cm(("rqk", 1), lap)
                bank = begin("u2")
                pe.wait_ge(t1_ready, 1)
                for h in range(GH):
                    mm = pe.matmul(bank[:, h * HD:(h + 1) * HD], XT[:, 2 * h + 1, :], vb[:, 1, h * HD:(h + 1) * HD],
                                   start=True, stop=True)
                done(mm, "u2")

                def head_out(dst, value, weights):
                    pe.matmul(dst, value[0], weights[:, 0:T], start=True, stop=False)
                    return pe.matmul(dst[:, P:T], value[1], weights[:, T:384], start=False, stop=True)

                pe.wait_ge(u_ready, 2)
                for p in range(GP):
                    bank = begin(("o", p))
                    for a in range(2):
                        h = 2 * p + a
                        v = [vb[:, j, h * HD:(h + 1) * HD] for j in range(TT)]
                        mm = head_out(bank[64 * a:64 * a + 64, 0:T], v, KQ[:, h, 1, :])
                    done(mm, ("o", p))

                def head_norm(cidx, src):
                    bank = begin(("on", cidx))
                    pe.wait_ge(o_sq_ready, cidx + 1)
                    done(pe.matmul(bank[:, 0:T], c("headsum"), src, start=True, stop=True), ("on", cidx))

                for p in range(GP):
                    head_norm(p, raw3[:, p, :])

                for a in range(2):
                    bank = begin(("rsw", a))
                    pe.wait_ge(rraw_ready, a + 1)
                    done(pe.matmul(bank[:, :], c("swap"), rraw[:, a, :, :], start=True, stop=True), ("rsw", a))
                for s in range(3):
                    project_cm(("mqk", s), lap)
                project_tm(("rv", 0), lap)
                project_tm(("mv", 0), lap)
                pe.wait_ge(rq_ready, 2)
                for h in range(RH):
                    bank = begin(("rs", h))
                    pe.matmul(bank[:, 0:T], rkf[:, h // 2, 0:P], kqz[:, h, 0, :], start=True, stop=True)
                    done(pe.matmul(bank[:, T:384], rkf[:, h // 2, P:T], kqz[:, h, 0, P:T], start=True, stop=True), ("rs", h))

                def m_decay(p):
                    bank = begin(("mdec", p))
                    for a in range(2):
                        r = 32 + 2 * p + a
                        mm = pe.matmul(bank[:, a * T:(a + 1) * T], cst[:, 0, r:r + 1].to_broadcast([P, P]), rows[:, :],
                                       start=True, stop=True)
                    done(mm, ("mdec", p))

                def m_scores(p):
                    for h in (2 * p, 2 * p + 1):
                        bank = begin(("ms", h))
                        pe.matmul(bank[:, 0:T], kf[:, p, 0:P], kqz[:, h, 1, :], start=True, stop=True)
                        done(pe.matmul(bank[:, T:384], kf[:, p, P:T], kqz[:, h, 1, P:T], start=True, stop=True), ("ms", h))

                def m_floors(p):
                    bank = begin(("em", p))
                    for a in range(2):
                        r = 64 + 2 * p + a
                        mm = pe.matmul(bank[64 * a:64 * a + 64, 0:T], cst[:, 0, r:r + 1].to_broadcast([P, 64]), rows[:, :],
                                       start=True, stop=True)
                    done(mm, ("em", p))

                def m_out(p):
                    bank = begin(("o", 5 + p))
                    one = [cst[:, CONST.index("ones"), 0:64]] * 2
                    for a in range(2):
                        h = 2 * p + a
                        pe.wait_ge(p_ready, RH + h + 1)
                        v = [vm[:, j, h * HD:(h + 1) * HD] for j in range(TT)]
                        head_out(bank[64 * a:64 * a + 64, 0:T], v, mprob[:, h, :])
                        mm = head_out(bank[64 * a:64 * a + 64, T:2 * T], one, mprob[:, h, :])
                    done(mm, ("o", 5 + p))

                m_decay(0)
                project_tm(("mv", 1), lap)
                for p in range(RP):
                    bank = begin(("o", 3 + p))
                    if p == 0:
                        pe.wait_ge(val_ready, 1)
                    for a in range(2):
                        h = 2 * p + a
                        pe.wait_ge(p_ready, h + 1)
                        v = [vr[:, j, h * HD:(h + 1) * HD] for j in range(TT)]
                        mm = head_out(bank[64 * a:64 * a + 64, 0:T], v, rprob[h])
                    done(mm, ("o", 3 + p))
                project_tm(("mv", 2), lap)
                release()
                for p in range(RP):
                    head_norm(3 + p, rsq[:, p, :])
                pe.wait_ge(mq_ready, 12)
                m_scores(0)
                m_floors(0)
                m_decay(1)
                m_scores(1)
                m_floors(1)
                m_floors(2)
                def project_out(n, ks):
                    b = bank_of[("wo", n)][0]
                    w = slot_w(NPROJ + n)
                    for k in ks:
                        for j in range(TT):
                            mm = pe.matmul(ps[:, b, j * COLS:(j + 1) * COLS], mixT[:, k, j * P:(j + 1) * P], w[:, k, :],
                                           start=(k == 0 and j == 0), stop=(k == KD - 1 and j == TT - 1), skip_group_check=True)
                    return mm

                def buffers_read(name):
                    b, u = bank_of[name]
                    pe.wait_ge(full[b], u + 1)
                    pe.sem_inc(slots_free, SPARE // 2)

                def begin_out(n):
                    begin(("wo", n))
                    have_slot(lap, NPROJ + n)
                    project_out(n, range(GP + RP))

                pe.wait_ge(val_ready, 4)
                m_out(0)
                pe.wait_ge(mix_ready, GP + RP)
                begin_out(0)
                m_decay(2)
                m_scores(2)
                begin_out(1)
                buffers_read(("ms", 5))
                m_out(1)
                begin_out(2)
                head_norm(5, msq[:, 0, :])
                m_out(2)
                begin_out(3)
                buffers_read(("o", 7))
                head_norm(6, msq[:, 1, :])
                pe.wait_ge(mix_ready, 6)
                for n in range(D // COLS):
                    project_out(n, [5])
                head_norm(7, msq[:, 2, :])
                pe.wait_ge(mix_ready, 7)
                for n in range(D // COLS):
                    project_out(n, [6])
                pe.wait_ge(mix_ready, 8)
                for n in range(D // COLS):
                    done(project_out(n, [7]), ("wo", n))
                for n in range(D // COLS):
                    b, u = bank_of[("wo", n)]
                    pe.wait_ge(full[b], u + 1)
                    pe.sem_inc(slots_free, 1)
                for i in range(4):
                    j, half = i // 2, i % 2
                    bank = begin(("h2T", i))
                    pe.wait_ge(x_mixed, 4)
                    for kk in range(4):
                        mm = pe.transpose(bank[:, kk * P:(kk + 1) * P], x[:, j, half * 4 + kk:D:KD], c("ident"))
                    done(mm, ("h2T", i))
                bank = begin("logitsT")
                pe.wait_ge(rwg_ready, 1)
                pe.wait_ge(hT_ready, 6)
                pe.wait_ge(hT_ready_act, 2)
                for k in range(KD):
                    mm = pe.matmul(bank[0:36, 0:T], rw[:, k, :], hT3[:, k, :], start=(k == 0), stop=(k == KD - 1))
                done(mm, "logitsT")
                b_, n_ = bank_of["logitsT"]
                pe.wait_ge(full[b_], n_ + 1)
                pe.sem_inc(logits_read, 1)
                bank = begin("logits")
                pe.wait_ge(lgT_ready, 2)
                for j in range(TT):
                    mm = pe.transpose(bank[:, j * P:(j + 1) * P], lgT[:, j * P:(j + 1) * P], c("ident"))
                done(mm, "logits")
                for b in range(4):
                    pe.wait_ge(free[b], uses[b])
                for j in range(TT):
                    for n in range(2):
                        mm = pe.matmul(ps[:, 2 * j + n, :], c("ident"), x[:, j, n * 512:(n + 1) * 512],
                                       start=True, stop=False, skip_group_check=True)
                mm.then_inc(acc_init, 1)
                bank = begin("rank")
                pe.wait_ge(mask_ready, 1)
                pe.matmul(bank[:, 0:64], c("before"), pick[:, 0, :, :], start=True, stop=False, skip_group_check=True)
                pe.matmul(bank[:, 32:96], c("ones"), pick[:, 0, 0:1, :].to_broadcast([P, 2, EXPERTS]), start=False, stop=False,
                          skip_group_check=True)
                mm = pe.matmul(bank[:, 64:96], c("ones"), pick[:, 0, 1, :], start=False, stop=True, skip_group_check=True)
                done(mm, "rank")
                for b in range(4, 8):
                    if b != bank_of["rank"][0]:
                        pe.wait_ge(free[b], uses[b])

                def gather(n):
                    pe.wait_ge(psel_ready, n * 2 + 1)
                    for half in range(2):
                        for kk in range(4):
                            k = half * 4 + kk
                            for j in range(TT):
                                for i in range(3):
                                    mm = pe.matmul(ps[:, 4 + 3 * half, kk * P:(kk + 1) * P], part[i][:, j, k:D:KD], Psel[:, j, :],
                                                   start=(j == 0 and i == 0), stop=(j == TT - 1 and i == 2))
                        mm.then_inc(gath_full, 1)

                pe.wait_ge(part_ready, 2 * TT)
                pe.wait_ge(rest_ready, 2 * TT)
                gather(rounds_done(pe, rounds) + l)
                pe.wait_ge(free[bank_of["rank"][0]], uses[bank_of["rank"][0]])
                pe.wait_ge(routed, l + 1)
                pe.sem_inc(first, 1)
                with pe.Fori(0, QUADS // LAP) as mlap:
                    for u in range(LAP):
                        pe.reg_load(nreg, nround[0:1, bass.ds(mlap * LAP + u, 1)])
                        nv = pe.snap(nreg, min_val=1, max_val=MAXROUND)

                        def group(m):
                            g = 3 * u + m
                            before = l * (NMOE // WIDE) if g % 4 == 2 else lap + NMIX // RING
                            return [4 * (g % 4) + e for e in range(4)], (before + mlap * (12 * LAP // WIDE) + g // 4) * 16 + 16

                        with pe.Fori(0, nv) as r:
                            n = rounds_done(pe, rounds)
                            pe.wait_ge(hq_ready, (n + l) * 2 + 2)
                            for m in range(2):
                                at, count = group(m)
                                for e in range(4):
                                    pe.wait_ge(arrived[at[e]], count)
                                for k in range(KD):
                                    for e in range(4):
                                        mm = pe.matmul(ps[32 * e:32 * e + 32, 5 + m, 0:DE], hq[:, k, 32 * e:32 * e + 32],
                                                       slot[at[e]][:, k * DE:(k + 1) * DE],
                                                       start=(k == 0), stop=(k == KD - 1), skip_group_check=True)
                                mm.then_inc((gate_full, up_full)[m], 1)
                                if m == 0:
                                    pe.wait_ge(psel_ready, (n + l) * 2 + 2)
                                    for j in range(TT):
                                        mm = pe.transpose(ps[:, 4, j * P:(j + 1) * P], Pwt[:, j, :], c("ident"))
                                    mm.then_inc(pwt_full, 1)
                                    pe.wait_ge(gate_full, n + 1)
                                    with pe.If(r == nv - 1):
                                        pe.sem_inc(slots_free, 4)
                            pe.wait_ge(pwt_ready, n + 1)
                            gather(n + l + 1)
                            pe.wait_ge(up_full, n + 1)
                            with pe.If(r == nv - 1):
                                pe.sem_inc(slots_free, 4)
                            pe.wait_ge(hmid_ready, n + 1)
                            for f in range(2):
                                mm = pe.transpose(ps[:, 6, T + f * P:T + (f + 1) * P], hmid[:, f:DE:2], c("ident"))
                            mm.then_inc(hmt_full, 1)
                            pe.wait_ge(hmt_ready, n + 1)
                            at, count = group(2)
                            for e in range(4):
                                pe.wait_ge(arrived[at[e]], count)
                            for h in range(2):
                                for f in range(2):
                                    for e in range(4):
                                        mm = pe.matmul(ps[32 * e:32 * e + 32, 5 + h, :], hmT[:, f, 32 * e:32 * e + 32],
                                                       slot[at[e]][:, f * D + h * 512:f * D + (h + 1) * 512],
                                                       start=(f == 0), stop=(f == 1), skip_group_check=True)
                                mm.then_inc(y_full, 1)
                            pe.wait_ge(y_full, n * 2 + 2)
                            with pe.If(r == nv - 1):
                                pe.sem_inc(slots_free, 4)
                            for h in range(2):
                                pe.wait_ge((y0_ready, y1_ready)[h], n + 1)
                                for j in range(TT):
                                    mm = pe.matmul(ps[:, 2 * j + h, :], PwT[:, j * P:(j + 1) * P], ysb[:, h, :],
                                                   start=False, stop=False, skip_group_check=True)
                            pe.reg_add(rounds, rounds, 1)
                pe.drain().then_inc(acc_last, 1)
                end_of_layer(pe, l)

        @block.scalar
        def _(act):
            rounds = act.alloc_register("act_rounds")
            act.reg_mov(rounds, 0)
            nreg = act.alloc_register("act_nround")
            chain = [0]

            def link(ins):
                chain[0] += 1
                ins.then_inc(act_chain, 1)
                act.wait_ge(act_chain, chain[0])

            def get(name):
                b, n = bank_of[name]
                act.wait_ge(full[b], n + 1)
                return ps[:, b, :]

            def rstd(done_sem):
                link(act.activation(ss[:, 2:4], ss[:, 0:2], ACT.Ln, scale=1.0 / D, bias=epsc[:, :]))
                act.activation(ss[:, 4:6], ss[:, 2:4], ACT.Exp, scale=-0.5).then_inc(done_sem, 1)

            def conv_in(name, tiles, cin, i0):
                bank = get(name)
                for n_, _ in enumerate(tiles):
                    i = i0 + n_
                    if i >= 3:
                        act.wait_ge(cin_used, i - 2)
                    ins = act.activation(cin[:, i % 3, 3:3 + T], bank[:, n_ * T:(n_ + 1) * T], ACT.Copy)
                    link(ins)
                    act.sem_inc(cin_ready, 1)
                act.sem_inc(free[bank_of[name][0]], 1)

            def gates(s, f, scale=1.0):
                bank = get(("gate", s))
                tiles = GATE_TILES[s]
                link(act.activation(mixT[:, tiles[0]:tiles[-1] + 1, :],
                                    bank[:, 0:len(tiles) * T].rearrange("p (c t) -> p c t", t=T), f, scale=scale))
                act.sem_inc(gate_ready, 1)
                act.sem_inc(free[bank_of[("gate", s)][0]], 1)

            act.wait_ge(init_done, 1)
            act.preload_act_table_set(LN_EXP)
            for j in range(TT):
                act.wait_ge(x_loaded[j], 16)
                act.activation(junk, x[:, j, :], ACT.Square, accum_out=ss[:, j:j + 1]).then_inc(sumsq, 1)
                act.wait_ge(sumsq, j + 1)
            act.activation(ss[:, 2:4], ss[:, 0:2], ACT.Ln, scale=1.0 / D, bias=epsc[:, :]).then_inc(sumsq, 1)
            act.wait_ge(sumsq, 3)
            act.activation(ss[:, 4:6], ss[:, 2:4], ACT.Exp, scale=-0.5).then_inc(sumsq, 1)
            with act.Fori(0, LAYERS) as l:
                act.wait_ge(par_ready, l + 1)
                act.sem_inc(first, 1)
                act.activation(ea[:, :], pv("a_log", 0, GH), ACT.Exp).then_inc(gates_e, 1)
                act.wait_ge(gates_z, 1)
                link(act.activation(sp[:, 2, :, :], sp[:, 1, :, :], ACT.Exp, scale=-1.0))
                act.activation(sp[:, 3, :, :], sp[:, 2, :, :], ACT.Ln, bias=1.0).then_inc(gates_e, 1)
                act.wait_ge(gates_col, 1)
                act.activation(beta[:, :, :], sp[:, 0, :, 0:GH], ACT.Exp).then_inc(gates_e, 1)
                slots = [(0, 1), (2, 3), (4, 5), (6, 7), (8,)]
                for s, tiles in enumerate(slots):
                    conv_in(("gdn", s), tiles, cin_g, 2 * s)
                    if s:
                        for t in slots[s - 1]:
                            act.wait_ge(conv_ready, t + 1)
                            act.activation(raw3[:, t, :], acc_g[:, t % 4, :], ACT.Silu).then_inc(raw_ready, 1)
                act.wait_ge(conv_ready, 9)
                act.activation(raw3[:, 8, :], acc_g[:, 0, :], ACT.Silu).then_inc(raw_ready, 1)
                act.wait_ge(raw_ready, 9)
                for s in range(3):
                    act.activation(sqn[:, 2 * s:2 * s + 2, :], raw3[:, 2 * s:2 * s + 2, :], ACT.Square).then_inc(sq_ready, 1)
                act.wait_ge(const_in, 16)
                act.wait_ge(init_done, 6)
                gates(0, ACT.Silu)
                act.preload_act_table_set(LN_EXP)
                for p in range(GP):
                    bank = get(("beta", p // 2))
                    ins = act.activation(betab[:, p, :], bank[:, (p % 2) * T:(p % 2) * T + T], ACT.Exp)
                    link(ins)
                    act.sem_inc(beta_ready, 1)
                    if p % 2 or p == GP - 1:
                        act.sem_inc(free[bank_of[("beta", p // 2)][0]], 1)
                for s in range(3):
                    bank = get(("nrm", s))
                    ins = act.activation(rn[:, 2 * s:2 * s + 2, :], bank[:, :], ACT.Ln, bias=epsc[:, :])
                    link(ins)
                    act.sem_inc(free[bank_of[("nrm", s)][0]], 1)
                    act.activation(rn[:, 2 * s:2 * s + 2, :], rn[:, 2 * s:2 * s + 2, :], ACT.Exp, scale=-0.5).then_inc(rn_ready, 1)
                gates(1, ACT.Copy)
                for h in range(GH):
                    act.wait_ge(earg_ready, h + 1)
                    act.activation(ebuf[:, h % 2, :], ebuf[:, h % 2, :], ACT.Exp).then_inc(e_ready, 1)
                    if h == 3:
                        gates(2, ACT.Copy)
                gates(3, ACT.Copy)
                act.wait_ge(kq_ready, GH)
                for g in range(3):
                    bank = get(("A", g))
                    link(act.activation(Amat[:, 4 * g:4 * g + 4, :], bank[:, :], ACT.Copy))
                    act.sem_inc(a_ready, 1)
                    act.sem_inc(free[bank_of[("A", g)][0]], 1)
                link(act.activation(mixT[:, 5:7, :], mixT[:, 5:7, :], ACT.Tanh, scale=0.5))
                gates(4, ACT.Tanh, 0.5)
                for lev in range(6):
                    for g in range(3):
                        bank = get(("X", lev, g))
                        link(act.activation(X[:, 4 * g:4 * g + 4, :], bank[:, :], ACT.Copy))
                        act.sem_inc(x_ready, 1)
                        act.sem_inc(free[bank_of[("X", lev, g)][0]], 1)
                    if lev == 0:
                        act.activation(mixT[:, 2:5, :], mixT[:, 2:5, :], ACT.Silu).then_inc(gate_ready, 1)
                act.preload_act_table_set(LN_EXP)
                for i, name in enumerate(("u1", "u2")):
                    bank = get(name)
                    link(act.activation(vb[:, i, :], bank[:, 0:GW], ACT.Copy))
                    act.sem_inc(u_ready, 1)
                    act.sem_inc(free[bank_of[name][0]], 1)

                def out_rr(cidx, dst):
                    bank = get(("on", cidx))
                    link(act.activation(dst, bank[:, 0:T], ACT.Ln, scale=1.0 / HD, bias=epsc[:, :]))
                    act.sem_inc(free[bank_of[("on", cidx)][0]], 1)
                    act.activation(dst, dst, ACT.Exp, scale=-0.5).then_inc(o_rr_ready, 1)

                for p in range(GP):
                    bank = get(("o", p))
                    act.activation(raw3[:, p, :], bank[:, 0:T], ACT.Square).then_inc(o_sq_ready, 1)
                for a in range(2):
                    bank = get(("rqk", a))
                    link(act.activation(rraw[:, a, :, :], bank[:, :], ACT.Copy))
                    act.sem_inc(rraw_ready, 1)
                    act.sem_inc(free[bank_of[("rqk", a)][0]], 1)
                for p in range(GP):
                    out_rr(p, raw3[:, 3 + p, :])
                for h in range(RH):
                    lgam = math.log(1.0 - 2.0 ** (-5.0 - h))
                    act.activation(rprob[h], dist[:, :], ACT.Exp, scale=lgam).then_inc(rdec_ready, 1)

                def mlstm_silu(t):
                    act.wait_ge(conv_ready, 9 + t + 1)
                    src = acc_m[:, t % 4, :]
                    if t < MP:
                        for a in range(2):
                            act.activation(kqz[64 * a:64 * a + 64, 2 * t + a, 1, :], src[64 * a:64 * a + 64, :],
                                           ACT.Silu).then_inc(mq_ready, 1)
                    else:
                        act.activation(kf[:, t - MP, :], src, ACT.Silu).then_inc(mq_ready, 2)

                act.wait_ge(conv_m_go, 1)
                for s in range(3):
                    conv_in(("mqk", s), (0, 1), cin_m, 9 + 2 * s)
                    if s:
                        mlstm_silu(2 * s - 2)
                        mlstm_silu(2 * s - 1)
                mlstm_silu(4)
                mlstm_silu(5)
                act.preload_act_table_set(LN_EXP)

                def values(name, dst):
                    bank = get(name)
                    n = WIDTH[name]
                    link(act.activation(dst, bank[:, 0:TT * n].rearrange("p (j c) -> p j c", j=TT), ACT.Copy))
                    act.sem_inc(val_ready, 1)
                    act.sem_inc(free[bank_of[name][0]], 1)

                def m_weights(p):
                    for h in (2 * p, 2 * p + 1):
                        act.wait_ge(earg_ready, GH + h + 1)
                        act.activation(mprob[:, h, :], mprob[:, h, :], ACT.Exp).then_inc(e_ready, 1)

                def m_floor(p):
                    bank = get(("em", p))
                    link(act.activation(mem[p], bank[:, 0:T], ACT.Exp, scale=-1.0))
                    act.sem_inc(free[bank_of[("em", p)][0]], 1)

                def m_abs(p):
                    bank = get(("o", 5 + p))
                    act.activation(mden[:, p, :], bank[:, T:2 * T], ACT.Abs).then_inc(em_ready, 1)

                def m_square(p):
                    act.wait_ge(o_sq_in, p + 1)
                    act.activation(msq[:, p, :], mh[:, p, :], ACT.Square).then_inc(o_sq_ready, 1)

                values(("rv", 0), vr[:, :, :])
                values(("mv", 0), vm[:, :, 0:P])
                values(("mv", 1), vm[:, :, P:2 * P])
                m_weights(0)
                act.wait_ge(rq_ready, 2)
                for p in range(RP):
                    bank = get(("o", 3 + p))
                    act.activation(rsq[:, p, :], bank[:, 0:T], ACT.Square).then_inc(o_sq_ready, 1)
                values(("mv", 2), vm[:, :, 2 * P:3 * P])
                for p in range(RP):
                    out_rr(3 + p, rrr[:, p, :])
                m_floor(0)
                m_weights(1)
                m_floor(1)
                m_floor(2)
                m_abs(0)
                m_square(0)
                m_weights(2)
                m_abs(1)
                out_rr(5, mrr[:, 0, :])
                m_square(1)
                m_abs(2)
                out_rr(6, mrr[:, 1, :])
                m_square(2)
                out_rr(7, mrr[:, 2, :])
                act.wait_ge(x_mixed, 4)

                def x_square(j):
                    link(act.activation(junk, x[:, j, :], ACT.Square, accum_out=ss[:, j:j + 1]))

                x_square(0)
                for i in (1, 3):
                    j = i // 2
                    bank = get(("h2T", i))
                    act.activation(hT3[:, 4:8, j * P:(j + 1) * P], bank.rearrange("p (k t) -> p k t", k=4),
                                   ACT.Copy).then_inc(hT_ready_act, 1)
                x_square(1)
                act.wait_ge(hT_ready_act, 2)
                for i in (1, 3):
                    act.sem_inc(free[bank_of[("h2T", i)][0]], 1)
                rstd(rstd_ready)
                for j in range(TT):
                    act.wait_ge(xn_ready, 3 + j)
                    act.activation(part[0][:, j, :], xn3[:, j, :], ACT.Copy).then_inc(part_ready, 1)
                act.wait_ge(route_in, 1)
                act.activation(rt[:, :, 24:28], rt[:, :, 20:24], ACT.Exp).then_inc(route_exp, 1)
                for j in range(TT):
                    act.wait_ge(rest_ready, j + 1)
                    act.activation(part[1][:, j, :], rest[:, j, :], ACT.Copy).then_inc(part_ready, 1)
                act.wait_ge(route_in, 2)
                act.activation(rt[:, :, 60:61], rt[:, :, 59:60], ACT.Exp).then_inc(route_exp, 1)
                act.wait_ge(routed, l + 1)
                act.sem_inc(first, 1)
                with act.Fori(0, QUADS) as q:
                    act.reg_load(nreg, nround[0:1, bass.ds(q, 1)])
                    nv = act.snap(nreg, min_val=1, max_val=MAXROUND)
                    with act.Fori(0, nv) as r:
                        n = rounds_done(act, rounds)
                        act.wait_ge(gate_full, n + 1)
                        act.activation(sg, ps[:, 5, 0:DE], ACT.Silu).then_inc(sg_ready, 1)
                        act.wait_ge(pwt_full, n + 1)
                        act.activation(PwT, ps[:, 4, 0:T], ACT.Copy).then_inc(pwt_ready, 1)
                        act.wait_ge(hmt_full, n + 1)
                        act.activation(hmT[:, :, :], ps[:, 6, T:2 * T], ACT.Copy).then_inc(hmt_ready, 1)
                        act.wait_ge(y_full, n * 2 + 1)
                        act.activation(ysb[:, 0, :], ps[:, 5, :], ACT.Copy).then_inc(y0_ready, 1)
                        act.reg_add(rounds, rounds, 1)
                act.preload_act_table_set(LN_EXP)
                act.wait_ge(acc_last, 1)
                link(act.activation(junk, ps[:, 2:4, :], ACT.Square, accum_out=ss[:, 1:2]))
                act.sem_inc(squared, 1)
                act.wait_ge(x_out, 1)
                link(act.activation(junk, ps[:, 0:2, :], ACT.Square, accum_out=ss[:, 0:1]))
                rstd(rstd_ready)
                act.wait_ge(rstd_ready, 2)
                end_of_layer(act, l)
        @block.vector
        def _(dve):
            rounds = dve.alloc_register("dve_rounds")
            dve.reg_mov(rounds, 0)
            nreg = dve.alloc_register("dve_nround")
            chain = [0]
            TTn = dve.tensor_tensor

            def link(ins):
                chain[0] += 1
                ins.then_inc(dve_chain, 1)
                dve.wait_ge(dve_chain, chain[0])

            def get(name):
                b, n = bank_of[name]
                dve.wait_ge(full[b], n + 1)
                return ps[:, b, :]

            def free_(name):
                dve.sem_inc(free[bank_of[name][0]], 1)

            def scale_x():
                for j in range(TT):
                    dve.tensor_scalar(xn3[:, j, :], x[:, j, :], ss[:, 4 + j:5 + j], None, ALU.mult).then_inc(xn_ready, 1)

            def evac_hT(kind, gain):
                for i in range(4):
                    j, half = i // 2, i % 2
                    bank = get((kind, i))
                    g = pv(gain, half * 4, 4).unsqueeze(2).to_broadcast([P, 4, P])
                    link(TTn(hT3[:, half * 4:half * 4 + 4, j * P:(j + 1) * P],
                             bank.rearrange("p (k t) -> p k t", k=4), g, ALU.mult))
                    dve.sem_inc(hT_ready, 1)
                    free_((kind, i))

            def conv(i, cin, acc, w):
                dve.wait_ge(cin_ready, i + 1)
                s, a = cin[:, i % 3, :], acc[:, (i if i < 9 else i - 9) % 4, :]
                j_ = i if i < 9 else i - 9
                if j_ >= 4:
                    if i < 9:
                        dve.wait_ge(raw_ready, j_ - 3)
                    else:
                        dve.wait_ge(mq_ready, 2 * (j_ - 3))
                link(dve.tensor_scalar(a, s[:, 0:T], w(0), None, ALU.mult))
                for t in range(1, CONV):
                    link(dve.scalar_tensor_tensor(out=a, in0=s[:, t:t + T], scalar=w(t), in1=a, op0=ALU.mult, op1=ALU.add))
                dve.sem_inc(conv_ready, 1)
                dve.sem_inc(cin_used, 1)

            for j in range(TT):
                dve.wait_ge(x_loaded[j], 16)
            with dve.Fori(0, LAYERS) as l:
                dve.wait_ge(par_in, l * 16 + 16)
                dve.sem_inc(first, 1)
                dve.wait_ge(sumsq, 4)
                scale_x()
                link(dve.tensor_copy(par[:, :], par_next[:, :]))
                dve.sem_inc(par_ready, 1)
                evac_hT("hT", "gain_mix")
                dve.wait_ge(const_in, 16)
                dve.wait_ge(init_done, 6)
                link(dve.memset(cin_g[:, :, 0:3], 0.0))
                bank = get("gatesT")
                link(dve.tensor_copy(lgT[0:NG, :], bank[0:NG, 0:T]))
                dve.sem_inc(lgT_ready, 1)
                free_("gatesT")
                bank = get("gates")
                b3 = bank[:, 0:TT * P].rearrange("p (j c) -> p j c", j=TT)[:, :, 0:NG]
                bias = pv("bias3", 0, 24).unsqueeze(1).to_broadcast([P, TT, 24])
                link(TTn(gz[:, :, :], b3, bias, ALU.add))
                free_("gates")
                link(dve.tensor_scalar(sp[:, 0, :, 0:6], gz[:, :, 0:6], -1.0, None, ALU.mult))
                link(dve.tensor_copy(sp[:, 0, :, 6:12], gz[:, :, 6:12]))
                link(dve.tensor_scalar(sp[:, 0, :, 12:18], gz[:, :, 18:24], -1.0, None, ALU.mult))
                z2 = sp[:, 0, :, :].rearrange("p j c -> p (j c)")
                dve.scalar_tensor_tensor(out=sp[:, 1, :, :].rearrange("p j c -> p (j c)"), in0=z2, scalar=-1.0, in1=z2,
                                         op0=ALU.mult, op1=ALU.max).then_inc(gates_z, 1)
                dve.wait_ge(gates_e, 2)
                link(dve.scalar_tensor_tensor(out=sp[:, 1, :, :].rearrange("p j c -> p (j c)"), in0=z2, scalar=0.0,
                                              in1=sp[:, 3, :, :].rearrange("p j c -> p (j c)"), op0=ALU.max, op1=ALU.add))
                link(dve.tensor_scalar(sp[:, 0, :, 0:6], sp[:, 1, :, 0:6], -1.0, None, ALU.mult))
                dve.sem_inc(gates_col, 1)
                link(dve.tensor_copy(selin[:, 1, :, 6:12], sp[:, 0, :, 0:6]))
                eab = ea[:, :].unsqueeze(1).to_broadcast([P, TT, GH])
                link(TTn(dpos[:, :, 0:6], sp[:, 1, :, 6:12], eab, ALU.mult))
                link(dve.tensor_copy(dpos[:, :, 6:12], sp[:, 1, :, 12:18]))
                link(dve.tensor_copy(selin[:, 0, :, 0:6], dpos[:, :, 0:6]))
                for o_ in (32, 64):
                    link(dve.tensor_copy(selin[:, 1, :, o_:o_ + 6], gz[:, :, 12:18]))
                    link(dve.tensor_copy(selin[:, 2, :, o_:o_ + 6], dpos[:, :, 6:12]))
                dve.sem_inc(selin_ready, 1)

                def wg(t):
                    return lambda k: pv("conv_g", t * CONV + k)

                for t in range(9):
                    conv(t, cin_g, acc_g, wg(t))
                bank = get("rows")
                link(dve.tensor_copy(rowsraw[:, :], bank[:, 0:T]))
                link(dve.tensor_copy(rows[0:12, :], rowsraw[0:12, :]))
                for q0 in (32, 64):
                    s = rowsraw[q0:q0 + 6, :]
                    link(dve.tensor_tensor_scan(rows[q0:q0 + 6, :], s, s, 0.0, ALU.max, ALU.max))
                link(dve.tensor_scalar(rows[32:38, :], rows[32:38, :], -1.0, None, ALU.mult))
                link(TTn(rows[64:70, :], rows[64:70, :], bank[64:70, T:2 * T], ALU.add))
                dve.sem_inc(rows_ready, 1)
                free_("rows")
                bank = get("cols")
                link(dve.tensor_copy(colv[:, 0:30], bank[:, 0:30]))
                free_("cols")
                cv = colv[:, 0:24].rearrange("p (j c) -> p j c", j=TT)
                link(TTn(colA[:, :, :], cv[:, :, 6:12], gz[:, :, 12:18], ALU.add))
                dve.wait_ge(kqz_zero, 1)
                dve.wait_ge(beta_ready, GP)
                for t in range(6):
                    dve.wait_ge(rn_ready, t // 2 + 1)
                    if t < 3:
                        for a in range(2):
                            r_ = slice(64 * a, 64 * a + 64)
                            link(dve.scalar_tensor_tensor(out=kqz[r_, 2 * t + a, 1, :], in0=raw3[r_, t, :], scalar=QK_SCALE,
                                                          in1=rn[r_, t, :], op0=ALU.mult, op1=ALU.mult))
                    else:
                        p = t - 3
                        link(TTn(kf[:, p, :], raw3[:, t, :], rn[:, t, :], ALU.mult))
                        for a in range(2):
                            r_ = slice(64 * a, 64 * a + 64)
                            link(TTn(kqz[r_, 2 * p + a, 0, :], kf[r_, p, :], betab[r_, p, :], ALU.mult))
                        dve.sem_inc(kq_in_ready, 1)
                dve.wait_ge(gates_e, 3)
                vb4 = vb[:, :, :].rearrange("p t (h d) -> p t h d", h=GH)

                def earg(i, p):
                    bank = get(("dec", p))
                    h = i
                    bc = bank[:, (h % 2) * T:(h % 2 + 1) * T]
                    e = ebuf[:, h % 2, :]
                    for dst, src, col, lim in ((slice(0, P), slice(0, P), colv[:, h:h + 1], maskc[:, 0:P]),
                                               (slice(P, T), slice(P, T), colv[:, 24 + h:25 + h], maskc[:, P:T]),
                                               (slice(T, 384), slice(P, T), colv[:, 12 + h:13 + h], maskc[:, 0:P])):
                        link(dve.scalar_tensor_tensor(out=e[:, dst], in0=bc[:, src], scalar=col, in1=lim,
                                                      op0=ALU.add, op1=ALU.min))
                    dve.sem_inc(earg_ready, 1)

                def kq_mul(h):
                    dve.wait_ge(e_ready, h + 1)
                    e = ebuf[:, h % 2, :]
                    bank = get(("kq0", h))
                    link(TTn(KQ[:, h, :, 0:T], bank.rearrange("p (a t) -> p a t", a=2),
                             e[:, 0:T].unsqueeze(1).to_broadcast([P, 2, T]), ALU.mult))
                    free_(("kq0", h))
                    bank = get(("kq1", h))
                    link(TTn(KQ[:, h, :, T:384], bank[:, 0:T].rearrange("p (a t) -> p a t", a=2),
                             e[:, T:384].unsqueeze(1).to_broadcast([P, 2, P]), ALU.mult))
                    free_(("kq1", h))
                    dve.sem_inc(kq_ready, 1)

                for p in range(GP):
                    bank = get(("vt", p))
                    b_ = beta[:, :, 2 * p:2 * p + 2].unsqueeze(3).to_broadcast([P, TT, 2, HD])
                    link(TTn(vb4[:, :, 2 * p:2 * p + 2, :],
                             bank[:, 0:T].rearrange("p (t h d) -> p t h d", t=TT, h=2), b_, ALU.mult))
                    free_(("vt", p))
                    dve.sem_inc(vb_ready, 1)
                for h in range(GH):
                    if h == 0:
                        earg(0, 0)
                    if h + 1 < GH:
                        earg(h + 1, (h + 1) // 2)
                    if h % 2 == 0:
                        free_(("dec", h // 2))
                    kq_mul(h)

                def diag(h):
                    return KQ[:, h, 0, :].rearrange("p (b t) -> p b t", b=3)[:, 0:3:2, :]

                dve.wait_ge(lvl_in, 16)
                idb = cst[:, 0, :].unsqueeze(1)
                for g in range(3):
                    for h in (2 * g, 2 * g + 1):
                        link(TTn(XT[:, 2 * h:2 * h + 2, :], diag(h), lvl[:, 0, :].unsqueeze(1).to_broadcast([P, 2, P]), ALU.mult))
                    link(TTn(XT[:, 4 * g:4 * g + 4, :], idb.to_broadcast([P, 4, P]), XT[:, 4 * g:4 * g + 4, :], ALU.subtract))
                    dve.sem_inc(xt_ready, 1)
                for lev in range(1, 7):
                    r_, c0 = (slice(0, HD), HD) if lev == 6 else (slice(0, P), 0)
                    for g in range(3):
                        bank = get(("W", lev, g))
                        for a in range(2):
                            h = 2 * g + a
                            src = bank[r_, a * T:(a + 1) * T].rearrange("p (b t) -> p b t", b=2)[:, :, c0:P]
                            if lev == 6:
                                link(dve.tensor_copy(diag(h)[r_, :, c0:P], src))
                            else:
                                link(TTn(diag(h), src, lvl[:, lev, :].unsqueeze(1).to_broadcast([P, 2, P]), ALU.mult))
                        dve.sem_inc(w_ready, 1)
                        free_(("W", lev, g))
                    for g in range(3):
                        bank = get(("Z", lev, g))
                        link(TTn(XT[r_, 4 * g:4 * g + 4, c0:P], XT[r_, 4 * g:4 * g + 4, c0:P],
                                 bank.rearrange("p (m t) -> p m t", m=4)[r_, :, c0:P], ALU.subtract))
                        dve.sem_inc(xt_ready, 1)
                        free_(("Z", lev, g))
                bank = get("t1")
                link(TTn(vb[:, 1, :], vb[:, 1, :], bank[:, 0:GW], ALU.subtract))
                dve.sem_inc(t1_ready, 1)
                free_("t1")

                def head_result(cidx, src, rr):
                    dve.wait_ge(o_rr_ready, cidx + 1)
                    link(dve.scalar_tensor_tensor(out=rr, in0=src, scalar=pv("head_gain", cidx), in1=rr,
                                                  op0=ALU.mult, op1=ALU.mult))
                    link(TTn(mixT[:, cidx, :], rr, mixT[:, cidx, :], ALU.mult))
                    dve.sem_inc(mix_ready, 1)

                dve.wait_ge(rw_in, l * 16 + 16)
                dve.sem_inc(first, 1)
                link(TTn(rw[:, :, :], rw[:, :, :], pv("gain_ffn", 0, KD).unsqueeze(2).to_broadcast([P, KD, 36]), ALU.mult))
                dve.sem_inc(rwg_ready, 1)
                dve.wait_ge(gate_ready, 6)
                link(dve.tensor_scalar(mixT[:, 5:8, :], mixT[:, 5:8, :], 0.5, 0.5, ALU.mult, ALU.add))
                for p in range(GP):
                    bank = get(("o", p))
                    head_result(p, bank[:, 0:T], raw3[:, 3 + p, :])
                    free_(("o", p))
                link(dve.memset(cin_m[:, :, 0:3], 0.0))
                dve.sem_inc(conv_m_go, 1)
                for a in range(2):
                    bank = get(("rsw", a))
                    sin_b = rot[:, 1, :].unsqueeze(1).to_broadcast([P, 2, T])
                    cos_b = rot[:, 0, :].unsqueeze(1).to_broadcast([P, 2, T])
                    link(TTn(rtmp[:, :, :], bank.rearrange("p (c t) -> p c t", c=2), sin_b, ALU.mult))
                    free_(("rsw", a))
                    link(TTn(rraw[:, a, :, :], rraw[:, a, :, :], cos_b, ALU.mult))
                    if a == 0:
                        for b in range(2):
                            r_ = slice(64 * b, 64 * b + 64)
                            link(TTn(kqz[r_, b:4:2, 0, :], rraw[r_, a, :, :], rtmp[r_, :, :], ALU.add))
                    else:
                        link(TTn(rkf[:, :, :], rraw[:, a, :, :], rtmp[:, :, :], ALU.add))
                    dve.sem_inc(rq_ready, 1)

                def wm(t):
                    return lambda k: pv("conv_m", t * CONV + k)

                for t in range(6):
                    conv(9 + t, cin_m, acc_m, wm(t))
                for h in range(RH):
                    bank = get(("rs", h))
                    dve.wait_ge(rdec_ready, h + 1)
                    link(dve.scalar_tensor_tensor(out=rprob[h], in0=bank[:, 0:384], scalar=QK_SCALE, in1=rprob[h],
                                                  op0=ALU.mult, op1=ALU.mult))
                    dve.sem_inc(p_ready, 1)
                    free_(("rs", h))

                dve.wait_ge(mq_ready, 12)

                def m_exponents(p):
                    bank = get(("mdec", p))
                    for a in range(2):
                        h = 2 * p + a
                        bc = bank[:, a * T:(a + 1) * T]
                        link(dve.scalar_tensor_tensor(out=mprob[:, h, 0:T], in0=bc, scalar=colA[:, 0, h:h + 1],
                                                      in1=maskc[:, :], op0=ALU.add, op1=ALU.min))
                        link(dve.scalar_tensor_tensor(out=mprob[:, h, T:384], in0=bc[:, P:T], scalar=colA[:, 1, h:h + 1],
                                                      in1=maskc[:, 0:P], op0=ALU.add, op1=ALU.min))
                        dve.sem_inc(earg_ready, 1)
                    free_(("mdec", p))

                def m_multiply(p):
                    for h in (2 * p, 2 * p + 1):
                        bank = get(("ms", h))
                        dve.wait_ge(e_ready, GH + h + 1)
                        link(dve.scalar_tensor_tensor(out=mprob[:, h, :], in0=bank[:, 0:384], scalar=QK_SCALE,
                                                      in1=mprob[:, h, :], op0=ALU.mult, op1=ALU.mult))
                        dve.sem_inc(p_ready, 1)
                        free_(("ms", h))

                def m_divide(p):
                    bank = get(("o", 5 + p))
                    dve.wait_ge(em_ready, p + 1)
                    link(TTn(mden[:, p, :], mem[p], mden[:, p, :], ALU.max))
                    link(dve.reciprocal(mden[:, p, :], mden[:, p, :]))
                    link(TTn(mh[:, p, :], bank[:, 0:T], mden[:, p, :], ALU.mult))
                    dve.sem_inc(o_sq_in, 1)
                    free_(("o", 5 + p))

                m_exponents(0)
                m_multiply(0)
                for p in range(RP):
                    bank = get(("o", 3 + p))
                    head_result(3 + p, bank[:, 0:T], rrr[:, p, :])
                    free_(("o", 3 + p))
                m_exponents(1)
                m_multiply(1)
                m_exponents(2)
                m_divide(0)
                m_multiply(2)
                m_divide(1)
                head_result(5, mh[:, 0, :], mrr[:, 0, :])
                m_divide(2)
                head_result(6, mh[:, 1, :], mrr[:, 1, :])
                head_result(7, mh[:, 2, :], mrr[:, 2, :])
                for n in range(D // COLS):
                    bank = get(("wo", n))
                    link(TTn(x[:, :, n * COLS:(n + 1) * COLS], x[:, :, n * COLS:(n + 1) * COLS],
                             bank.rearrange("p (j c) -> p j c", j=TT), ALU.add))
                    dve.sem_inc(x_mixed, 1)
                    free_(("wo", n))
                for i in (0, 2):
                    j = i // 2
                    bank = get(("h2T", i))
                    link(dve.tensor_copy(hT3[:, 0:4, j * P:(j + 1) * P], bank.rearrange("p (k t) -> p k t", k=4)))
                    dve.sem_inc(hT_ready, 1)
                    free_(("h2T", i))
                dve.wait_ge(rstd_ready, 1)
                scale_x()
                bank = get("logitsT")
                link(dve.tensor_copy(lgT[0:36, :], bank[0:36, 0:T]))
                dve.sem_inc(lgT_ready, 1)
                free_("logitsT")
                bank = get("logits")
                for j in range(TT):
                    link(dve.scalar_tensor_tensor(out=lg[:, j, :], in0=bank[:, j * P:j * P + 36], scalar=ss[:, 4 + j:5 + j],
                                                  in1=pv("router_bias", 0, 36), op0=ALU.mult, op1=ALU.add))
                free_("logits")
                link(dve.tensor_copy(rt[:, :, 0:4], lg[:, :, 0:4]))
                for j in range(TT):
                    link(dve.max(rt[:, j, 8:16], rt[:, j, 0:8]))
                    link(dve.max_index(rtx[:, 0, j, :], rt[:, j, 8:16], rt[:, j, 0:8]))
                link(dve.tensor_copy(rt[:, :, 30:31], rtx[:, 0, :, 0:1]))
                link(TTn(rt[:, :, 20:24], rt[:, :, 0:4], rt[:, :, 8:9].to_broadcast([P, TT, 4]), ALU.subtract))
                dve.sem_inc(route_in, 1)
                link(TTn(rt[:, :, 16:20], iota[:, 0:4].unsqueeze(1).to_broadcast([P, TT, 4]),
                         rt[:, :, 30:31].to_broadcast([P, TT, 4]), ALU.is_equal))
                el = lg[:, :, 4:36].rearrange("p j (g e) -> p j e g", g=GROUPS)
                prod = pick[:, 3, :, :].rearrange("p j (e g) -> p j e g", g=GROUPS)
                link(TTn(prod, el, rt[:, :, 16:20].unsqueeze(2).to_broadcast([P, TT, PER_GROUP, GROUPS]), ALU.mult))
                link(dve.tensor_reduce(rt[:, :, 32:40], prod, AX_X, ALU.add))
                for j in range(TT):
                    link(dve.max(rt[:, j, 40:48], rt[:, j, 32:40]))
                    link(dve.max_index(rtx[:, 1, j, :], rt[:, j, 40:48], rt[:, j, 32:40]))
                link(dve.tensor_copy(rt[:, :, 48:50], rtx[:, 1, :, 0:2]))
                link(TTn(rt[:, :, 59:60], rt[:, :, 41:42], rt[:, :, 40:41], ALU.subtract))
                dve.sem_inc(route_in, 1)
                link(dve.tensor_scalar(rt[:, :, 31:32], rt[:, :, 30:31], float(PER_GROUP), None, ALU.mult))
                link(TTn(rt[:, :, 48:50], rt[:, :, 48:50], rt[:, :, 31:32].to_broadcast([P, TT, 2]), ALU.add))
                io32 = iota[:, 0:32].unsqueeze(1).to_broadcast([P, TT, EXPERTS])

                def over(col):
                    return rt[:, :, col:col + 1].to_broadcast([P, TT, EXPERTS])

                link(TTn(pick[:, 2, :, :], io32, over(48), ALU.is_equal))
                link(TTn(pick[:, 3, :, :], io32, over(49), ALU.is_equal))
                link(TTn(pick[:, 0, :, :], pick[:, 2, :, :], pick[:, 3, :, :], ALU.add))
                dve.sem_inc(mask_ready, 1)
                bank = get("rank")
                rk = rkw[:, :, :].rearrange("p j e -> p (j e)")
                link(dve.scalar_tensor_tensor(out=rk, in0=bank[:, 0:64], scalar=1.0,
                                              in1=pick[:, 0, :, :].rearrange("p j e -> p (j e)"), op0=ALU.add, op1=ALU.mult))
                link(dve.tensor_scalar(sel[:, 0, :, 0:EXPERTS], rkw[:, :, :], -1.0, None, ALU.add))
                gq = pv("gain_ffn", 0, KD)

                def select(q4, ids, n):
                    for j in range(TT):
                        rkq = sel[:, 0, j, q4].unsqueeze(2).to_broadcast([P, 4, CAP])
                        ins = TTn(Psel[:, j, :].rearrange("p (e s) -> p e s", e=4), ids.unsqueeze(1).to_broadcast([P, 4, CAP]),
                                  rkq, ALU.is_equal)
                    ins.then_inc(psel_ready, 1)

                def weigh(q4, n):
                    dve.wait_ge(psel_ready, n * 2 + 1)
                    for j in range(TT):
                        wq = sel[:, 1, j, q4].unsqueeze(2).to_broadcast([P, 4, CAP])
                        ins = TTn(Pwt[:, j, :].rearrange("p (e s) -> p e s", e=4),
                                  Psel[:, j, :].rearrange("p (e s) -> p e s", e=4), wq, ALU.mult)
                    ins.then_inc(psel_ready, 1)

                def selected(n):
                    for half in range(2):
                        dve.wait_ge(gath_full, n * 2 + half + 1)
                        TTn(hq[:, half * 4:half * 4 + 4, :], ps[:, 4 + 3 * half, :].rearrange("p (k s) -> p k s", k=4),
                            gq[:, half * 4:half * 4 + 4].unsqueeze(2).to_broadcast([P, 4, P]), ALU.mult).then_inc(hq_ready, 1)

                n0 = rounds_done(dve, rounds) + l
                select(slice(0, 4), iota[:, 0:CAP], n0)
                dve.wait_ge(route_exp, 1)
                link(dve.tensor_reduce(rt[:, :, 28:29], rt[:, :, 24:28], AX_X, ALU.add))
                link(dve.reciprocal(rt[:, :, 29:30], rt[:, :, 28:29]))
                dve.wait_ge(route_exp, 2)
                link(dve.tensor_scalar(rt[:, :, 61:62], rt[:, :, 60:61], 1.0, None, ALU.add))
                link(dve.reciprocal(rt[:, :, 62:63], rt[:, :, 61:62]))
                link(TTn(rt[:, :, 52:53], rt[:, :, 62:63], rt[:, :, 29:30], ALU.mult))
                link(TTn(rt[:, :, 53:54], rt[:, :, 52:53], rt[:, :, 60:61], ALU.mult))
                link(TTn(pick[:, 1, :, :], pick[:, 2, :, :], over(52), ALU.mult))
                link(TTn(pick[:, 3, :, :], pick[:, 3, :, :], over(53), ALU.mult))
                link(TTn(sel[:, 1, :, 0:EXPERTS], pick[:, 1, :, :], pick[:, 3, :, :], ALU.add))
                weigh(slice(0, 4), n0)
                link(dve.tensor_reduce(nround_f[:, 0:QUADS], bank[:, 64:96].rearrange("p (q e) -> p q e", e=4), AX_X, ALU.max))
                free_("rank")
                over_q = pick[:, 3, :, :].rearrange("p j e -> p (j e)").rearrange("p (q k) -> p q k", q=QUADS)
                link(TTn(over_q, iota[:, COUNT:COUNT + 8].unsqueeze(1).to_broadcast([P, QUADS, 8]),
                         nround_f[:, 0:QUADS].unsqueeze(2).to_broadcast([P, QUADS, 8]), ALU.is_lt))
                link(dve.tensor_reduce(nround_f[:, QUADS:2 * QUADS], over_q, AX_X, ALU.add))
                link(dve.tensor_scalar(nround[:, :], nround_f[:, QUADS:2 * QUADS], 1.0, None, ALU.max))
                dve.sem_inc(routed, 1)
                selected(n0)
                with dve.Fori(0, QUADS) as q:
                    dve.reg_load(nreg, nround[0:1, bass.ds(q, 1)])
                    nv = dve.snap(nreg, min_val=1, max_val=MAXROUND)
                    with dve.Fori(0, nv) as r:
                        n = rounds_done(dve, rounds)
                        dve.wait_ge(pwt_full, n + 1)
                        with dve.If(r < nv - 1):
                            select(bass.ds(q * 4, 4), iota[:, bass.ds(r * CAP + CAP, CAP)], n + l + 1)
                            weigh(bass.ds(q * 4, 4), n + l + 1)
                        with dve.Else():
                            select(bass.ds(q * 4 + 4, 4), iota[:, 0:CAP], n + l + 1)
                            weigh(bass.ds(q * 4 + 4, 4), n + l + 1)
                        dve.wait_ge(sg_ready, n + 1)
                        dve.wait_ge(up_full, n + 1)
                        TTn(hmid, sg, ps[:, 6, 0:DE], ALU.mult).then_inc(hmid_ready, 1)
                        selected(n + l + 1)
                        dve.wait_ge(y_full, n * 2 + 2)
                        dve.tensor_copy(ysb[:, 1, :], ps[:, 6, :]).then_inc(y1_ready, 1)
                        dve.reg_add(rounds, rounds, 1)
                dve.wait_ge(acc_last, 1)
                dve.tensor_copy(x[:, 0, :], ps[:, 0:2, :].rearrange("p b n -> p (b n)")).then_inc(x_out, 1)
                dve.wait_ge(squared, 1)
                dve.tensor_copy(x[:, 1, :], ps[:, 2:4, :].rearrange("p b n -> p (b n)")).then_inc(x_out, 1)
                dve.wait_ge(x_out, 2)
                end_of_layer(dve, l)
            dve.wait_ge(gfin_in, 16)
            for j in range(TT):
                dve.scalar_tensor_tensor(out=fin[:, j, :], in0=x[:, j, :], scalar=ss[:, 4 + j:5 + j], in1=gfin,
                                         op0=ALU.mult, op1=ALU.mult).then_inc(out_ready, 1)


def kernel(**inputs):
    import numpy as np
    import concourse.bacc as bacc
    from concourse.bass_utils import run_bass_kernel_spmd

    g = {k: np.ascontiguousarray(v) for k, v in inputs.items()}

    i = np.arange(P)
    row, col = i[:, None], i[None, :]
    tiles = {
        "ident": row == col, "cum": row <= col, "ncum": -1.0 * (row <= col), "nsuffix": -1.0 * (row > col),
        "before": row < col, "ones": np.ones((P, P)), "nones": -np.ones((P, P)), "headsum": row // HD == col // HD,
        "swap": 1.0 * ((row == col - HD // 2) & (col % HD >= HD // 2)) - 1.0 * ((row == col + HD // 2) & (col % HD < HD // 2)),
    }
    maskc = np.concatenate([np.where(row <= col, 0.0, NEG), np.zeros((P, P))], 1)
    d0 = np.where(row <= col, col - row, -NEG)
    dist = np.concatenate([d0, col + P - row, d0], 1)
    inv_freq = (np.float32(10000.0) ** (-np.arange(0, HD, 2, dtype=np.float32) / np.float32(HD))).astype(np.float32)
    ang = np.arange(T, dtype=np.float32)[None, :] * inv_freq[i % (HD // 2)][:, None]
    count = np.concatenate([np.arange(COUNT), CAP * np.arange(8)])
    consts = np.concatenate([tiles[n].astype(np.float32) for n in CONST] + [maskc, dist, np.cos(ang), np.sin(ang),
                            np.broadcast_to(count, (P, COUNT + 8))], 1).astype(np.float32)
    level_masks = np.stack([((row // (2 * b) == col // (2 * b)) & (row // b % 2 == 0) & (col // b % 2 == 1))
                            for b in LEVELS], 1).astype(np.float32)

    w_in = g["w_in"].reshape(LAYERS, P, KD, D_IN)
    w_mix = np.zeros((LAYERS, NMIX, P, KD, COLS), np.float32)
    for s, (_, cols) in enumerate(PROJ):
        at = 0
        for a, n in cols:
            w_mix[:, s, :, :, at:at + n] = w_in[:, :, :, a:a + n]
            at += n
    w_out = g["w_out"].reshape(LAYERS, KD, P, D // COLS, COLS)
    w_mix[:, NPROJ:] = w_out.transpose(0, 3, 2, 1, 4)
    w_mix = w_mix.reshape(LAYERS, NMIX, P, SLOT)

    def rows_all(a):
        return np.broadcast_to(a[:, None, :], (LAYERS, P, a.shape[1]))

    def conv_cols(a):
        return a.reshape(LAYERS, CONV, -1, P).transpose(0, 3, 2, 1).reshape(LAYERS, P, -1)

    head_gain = np.concatenate([g["gdn_norm"], g["ret_norm"], g["mlstm_norm"]], 1).reshape(LAYERS, MIX, P).transpose(0, 2, 1)
    zeros = np.zeros((LAYERS, P, GH), np.float32)
    params = np.concatenate([
        g["norm_mix"].reshape(LAYERS, P, KD), g["norm_ffn"].reshape(LAYERS, P, KD), conv_cols(g["gdn_conv"]),
        conv_cols(g["mlstm_conv"]), head_gain, rows_all(g["gdn_a_log"]), zeros, rows_all(g["gdn_dt_bias"]),
        rows_all(g["mlstm_i_bias"]), rows_all(g["mlstm_f_bias"]), np.zeros((LAYERS, P, GROUPS), np.float32),
        rows_all(g["router_bias"])], 2)
    params = params[[*range(LAYERS), LAYERS - 1]]
    router_w = np.concatenate([g["router_group"], g["router_expert"]], 2).reshape(LAYERS, P, KD, GROUPS + EXPERTS)
    router_w = router_w[[*range(LAYERS), LAYERS - 1]]
    experts = [g[n].reshape(LAYERS, EXPERTS, P, SLOT) for n in ("expert_gate", "expert_up", "expert_down")]
    x_in = g["x"].reshape(TT, P, D).transpose(1, 0, 2)
    gain_final = np.broadcast_to(g["norm_final"][None, :], (P, D))

    nc = bacc.Bacc("TRN2", target_bir_lowering=False, num_devices=1)
    arrays, args = {}, []
    for name, a in [("x_in", x_in), ("consts", consts), ("level_masks", level_masks), ("params", params), ("w_mix", w_mix),
                    ("router_w", router_w), ("e_gate", experts[0]), ("e_up", experts[1]), ("e_down", experts[2]),
                    ("gain_final", gain_final)]:
        a = np.ascontiguousarray(a)
        arrays[name] = a
        args.append(nc.dram_tensor(name, a.shape, F32, kind="ExternalInput").ap())
    out = nc.dram_tensor("out", (T, D), F32, kind="ExternalOutput").ap()
    trunk(nc, *args, out.rearrange("(j p) d -> p j d", p=P))
    r = run_bass_kernel_spmd(nc, [arrays], core_ids=[0])
    return r.results[0]["out"].reshape(1, T, D)
```
